# Optimizing a Trainium2 kernel written in Bass

```python
import jax, jax.numpy as jnp
from jax import lax
import numpy as np
import math
import jax
import jax.numpy as jnp

D_MODEL = 1024
BATCH = 1
SEQ = 256
DEPTH = 2

GRID_W = 64
CTX_LEN = 256
HEAD_DIM = 64
A_Q_HEADS = 6
A_KV_HEADS = 2
B_HEADS = 6
C_GROUPS = 4
C_WIDTH = C_GROUPS * HEAD_DIM
A_Q_W = A_Q_HEADS * HEAD_DIM
A_KV_W = A_KV_HEADS * HEAD_DIM
B_W = B_HEADS * HEAD_DIM
Q_W = A_Q_W + B_W
KV_W = 2 * A_KV_W + 2 * B_W
MIX_W = A_Q_W + B_W + C_WIDTH
PROJ_W = Q_W + KV_W + 3 * C_WIDTH
PROJ_SPLIT = (A_Q_W, Q_W, Q_W + KV_W, Q_W + KV_W + C_WIDTH, Q_W + KV_W + 2 * C_WIDTH)
KV_SPLIT = (A_KV_W, 2 * A_KV_W, 2 * A_KV_W + B_W)
Q_BLOCK = 128
WIN_R = 8
WIN_C = 16
ROPE_FREQS = HEAD_DIM // 4
ROPE_THETA = 10000.0
CONV_W = 3
FFN_DIM = 2816
N_MOD = 9
EPS = 1e-6


def rms_norm(x, g):
    xf = x.astype(jnp.float32)
    y = xf * lax.rsqrt(jnp.mean(xf * xf, axis=-1, keepdims=True) + EPS)
    return y.astype(x.dtype) * g

def heads(t, n):
    return t.reshape(t.shape[:-1] + (n, HEAD_DIM))

def axial_rope_tables(seq, dtype):
    pos = jnp.arange(seq, dtype=jnp.int32)
    row = (pos // GRID_W).astype(jnp.float32)
    col = (pos % GRID_W).astype(jnp.float32)
    freq = 1.0 / (ROPE_THETA ** (jnp.arange(ROPE_FREQS, dtype=jnp.float32) / ROPE_FREQS))
    ang = jnp.stack([row[:, None] * freq, col[:, None] * freq], axis=1)
    return jnp.cos(ang).astype(dtype), jnp.sin(ang).astype(dtype)

def apply_axial_rope(x, cos, sin):
    xr = x.reshape(x.shape[:-1] + (2, 2, ROPE_FREQS))
    x1, x2 = xr[..., 0, :], xr[..., 1, :]
    cs, sn = cos[None, :, None], sin[None, :, None]
    return jnp.stack([x1 * cs - x2 * sn, x2 * cs + x1 * sn], axis=-2).reshape(x.shape)

def gqa_attention(q, k, v):
    bsz, s_len, hq, dh = q.shape
    hkv = k.shape[2]
    grp = hq // hkv
    nb = s_len // Q_BLOCK
    qb = q.reshape(bsz, nb, Q_BLOCK, hkv, grp, dh).transpose(1, 0, 2, 3, 4, 5)
    scale = dh ** -0.5

    def block(qi):
        s = jnp.einsum('bqhgd,bkhd->bhgqk', qi, k).astype(jnp.float32) * scale
        p = jax.nn.softmax(s, axis=-1).astype(v.dtype)
        return jnp.einsum('bhgqk,bkhd->bqhgd', p, v)

    o = lax.map(block, qb)
    return o.transpose(1, 0, 2, 3, 4, 5).reshape(bsz, s_len, hq * dh)

def neighbourhood_attention(q, k, v, k_ctx, v_ctx, rpb, rows):
    bsz, s_len, nh, dh = q.shape
    wr = min(WIN_R, rows)
    n_win = wr * WIN_C
    scale = dh ** -0.5
    qg = q.reshape(bsz, rows, GRID_W, nh, dh)
    kg = k.reshape(bsz, rows, GRID_W, nh, dh)
    vg = v.reshape(bsz, rows, GRID_W, nh, dh)
    col = jnp.arange(GRID_W)
    cs = jnp.clip(col - WIN_C // 2, 0, GRID_W - WIN_C)
    col_idx = cs[:, None] + jnp.arange(WIN_C)[None, :]
    dc_idx = col_idx - col[:, None] + (WIN_C - 1)

    def row_block(r):
        rs = jnp.clip(r - wr // 2, 0, rows - wr)
        qr = lax.dynamic_index_in_dim(qg, r, axis=1, keepdims=False)
        kw = lax.dynamic_slice_in_dim(kg, rs, wr, axis=1)[:, :, col_idx]
        vw = lax.dynamic_slice_in_dim(vg, rs, wr, axis=1)[:, :, col_idx]
        dr_idx = rs + jnp.arange(wr) - r + (WIN_R - 1)
        bias = rpb[:, dr_idx][:, :, dc_idx].transpose(0, 2, 1, 3)
        s_win = jnp.einsum('bqhd,brqjhd->bhqrj', qr, kw).astype(jnp.float32) * scale + bias.astype(jnp.float32)[None]
        s_ctx = jnp.einsum('bqhd,bkhd->bhqk', qr, k_ctx).astype(jnp.float32) * scale
        s = jnp.concatenate([s_win.reshape(bsz, nh, GRID_W, n_win), s_ctx], axis=-1)
        p = jax.nn.softmax(s, axis=-1).astype(v.dtype)
        p_win = p[..., :n_win].reshape(bsz, nh, GRID_W, wr, WIN_C)
        return (jnp.einsum('bhqrj,brqjhd->bqhd', p_win, vw)
                + jnp.einsum('bhqk,bkhd->bqhd', p[..., n_win:], v_ctx))

    o = lax.map(row_block, jnp.arange(rows, dtype=jnp.int32))
    return o.transpose(1, 0, 2, 3, 4).reshape(bsz, s_len, nh * dh)

def short_conv_mixer(xi, gate_b, gate_c, w):
    z = gate_c * xi
    y = lax.conv_general_dilated(z, w[:, None, :], window_strides=(1,),
                                 padding=((CONV_W // 2, CONV_W // 2),),
                                 dimension_numbers=('NWC', 'WIO', 'NWC'),
                                 feature_group_count=z.shape[-1])
    return gate_b * y

def swiglu(u, wi, wo):
    g, up = jnp.split(u @ wi, 2, axis=-1)
    return (jax.nn.silu(g) * up) @ wo

def split_kv(pkv, k_gain):
    ka, va, kb, vb = jnp.split(pkv, KV_SPLIT, axis=-1)
    return (rms_norm(heads(ka, A_KV_HEADS), k_gain), heads(va, A_KV_HEADS),
            heads(kb, B_HEADS), heads(vb, B_HEADS))

def context_mix(p, qk_g, conv_w):
    qa, qb, pkv, cx, cb, cc = jnp.split(p, PROJ_SPLIT, axis=-1)
    ka, va, kb, vb = split_kv(pkv, qk_g[1])
    o_a = gqa_attention(rms_norm(heads(qa, A_Q_HEADS), qk_g[0]), ka, va)
    o_b = gqa_attention(heads(qb, B_HEADS), kb, vb)
    o_c = short_conv_mixer(cx, cb, cc, conv_w)
    return jnp.concatenate([o_a, o_b, o_c], axis=-1), (ka, va, kb, vb)

def latent_mix(p, kv_ctx, cos, sin, qk_g, rpb, conv_w, rows):
    qa, qb, pkv, cx, cb, cc = jnp.split(p, PROJ_SPLIT, axis=-1)
    ka, va, kb, vb = split_kv(pkv, qk_g[1])
    ka_c, va_c, kb_c, vb_c = kv_ctx
    qa = apply_axial_rope(rms_norm(heads(qa, A_Q_HEADS), qk_g[0]), cos, sin)
    ka = apply_axial_rope(ka, cos, sin)
    o_a = gqa_attention(qa, jnp.concatenate([ka, ka_c], axis=1), jnp.concatenate([va, va_c], axis=1))
    o_b = neighbourhood_attention(heads(qb, B_HEADS), kb, vb, kb_c, vb_c, rpb, rows)
    o_c = short_conv_mixer(cx, cb, cc, conv_w)
    return jnp.concatenate([o_a, o_b, o_c], axis=-1)

def hybrid_layer(h, hc, c, c_ctx, w_ada, b_ada, g, w_in, qk_g, rpb, conv_w, w_o, ffn_wi, ffn_wo,
                 cos, sin, rows, last):
    m = (jax.nn.silu(c) @ w_ada + b_ada).reshape(c.shape[0], 1, N_MOD, D_MODEL)
    mc = (jax.nn.silu(c_ctx) @ w_ada + b_ada).reshape(1, 1, N_MOD, D_MODEL)

    def pre(t, mm, i, gi):
        return rms_norm(t, g[gi]) * (1 + mm[:, :, i + 1]) + mm[:, :, i]

    def post(t, y, mm, i, gi, wres):
        return t + wres * mm[:, :, i + 2] * rms_norm(y, g[gi])

    h = post(h, swiglu(pre(h, m, 0, 0), ffn_wi[0], ffn_wo[0]), m, 0, 1, 0.5)
    hc = post(hc, swiglu(pre(hc, mc, 0, 0), ffn_wi[0], ffn_wo[0]), mc, 0, 1, 0.5)
    u = pre(h, m, 3, 2)
    uc = pre(hc, mc, 3, 2)
    if last:
        kv_c = split_kv(uc @ w_in[:, Q_W:Q_W + KV_W], qk_g[1])
    else:
        oc, kv_c = context_mix(uc @ w_in, qk_g, conv_w)
        hc = post(hc, oc @ w_o, mc, 3, 3, 1.0)
    o = latent_mix(u @ w_in, kv_c, cos, sin, qk_g, rpb, conv_w, rows)
    h = post(h, o @ w_o, m, 3, 3, 1.0)
    h = post(h, swiglu(pre(h, m, 6, 4), ffn_wi[1], ffn_wo[1]), m, 6, 5, 0.5)
    if not last:
        hc = post(hc, swiglu(pre(hc, mc, 6, 4), ffn_wi[1], ffn_wo[1]), mc, 6, 5, 0.5)
    return h, hc

def first_inputs(seed: int = 0) -> dict:
    key = jax.random.key(seed)
    ks = jax.random.split(key, 14)
    nrm = jax.random.normal
    f32 = jnp.float32
    return {
        'x': nrm(ks[0], (BATCH, SEQ, D_MODEL), f32),
        'c': nrm(ks[1], (BATCH, D_MODEL), f32),
        'ctx': nrm(ks[2], (BATCH, CTX_LEN, D_MODEL), f32),
        'c_ctx': nrm(ks[3], (D_MODEL,), f32),
        'w_ada': nrm(ks[4], (DEPTH, D_MODEL, N_MOD * D_MODEL), f32) * (0.5 * D_MODEL ** -0.5),
        'b_ada': 0.01 * nrm(ks[5], (DEPTH, N_MOD * D_MODEL), f32),
        'norm_g': 1.0 + 0.05 * nrm(ks[6], (DEPTH, 6, D_MODEL), f32),
        'w_in': nrm(ks[7], (DEPTH, D_MODEL, PROJ_W), f32) * D_MODEL ** -0.5,
        'qk_g': 1.0 + 0.05 * nrm(ks[8], (DEPTH, 2, HEAD_DIM), f32),
        'rpb': 0.1 * nrm(ks[9], (DEPTH, B_HEADS, 2 * WIN_R - 1, 2 * WIN_C - 1), f32),
        'conv_w': nrm(ks[10], (DEPTH, CONV_W, C_WIDTH), f32) * CONV_W ** -0.5,
        'w_o': nrm(ks[11], (DEPTH, MIX_W, D_MODEL), f32) * MIX_W ** -0.5,
        'ffn_wi': nrm(ks[12], (DEPTH, 2, D_MODEL, 2 * FFN_DIM), f32) * D_MODEL ** -0.5,
        'ffn_wo': nrm(ks[13], (DEPTH, 2, FFN_DIM, D_MODEL), f32) * FFN_DIM ** -0.5,
    }

def first_block(x, c, ctx, c_ctx, w_ada, b_ada, norm_g, w_in, qk_g, rpb, conv_w, w_o, ffn_wi, ffn_wo):
    seq = x.shape[1]
    rows = seq // GRID_W
    cos, sin = axial_rope_tables(seq, x.dtype)
    h, hc = x, ctx
    for i in range(DEPTH):
        h, hc = hybrid_layer(h, hc, c, c_ctx, w_ada[i], b_ada[i], norm_g[i], w_in[i], qk_g[i], rpb[i],
                             conv_w[i], w_o[i], ffn_wi[i], ffn_wo[i], cos, sin, rows, i == DEPTH - 1)
    return h


SSD_D_INNER = D_MODEL
SSD_HEADDIM = 64
SSD_HEADS = SSD_D_INNER // SSD_HEADDIM
SSD_GROUPS = 2
SSD_STATE = 128
SSD_CONV = 5
SSD_CHUNK = 128
MLSTM_D = D_MODEL
MLSTM_HEADS = 8
MLSTM_HEADDIM = MLSTM_D // MLSTM_HEADS
MLSTM_CHUNK = 128
GLA_HEADS = 4
GLA_DK = D_MODEL // 2
GLA_DV = D_MODEL
GLA_HEAD_DK = GLA_DK // GLA_HEADS
GLA_HEAD_DV = GLA_DV // GLA_HEADS
GLA_RANK = 16
GLA_TAU = 16.0
GLA_CHUNK = 64
FFN_DIM_2 = 11 * D_MODEL // 4
FFN_CONV = 3
NORM_EPS = 1e-6

SSD_XBC = SSD_D_INNER + 2 * SSD_GROUPS * SSD_STATE
L0_SPLITS = (SSD_D_INNER, SSD_XBC, 2 * SSD_HEADS, MLSTM_D, MLSTM_D, MLSTM_D, MLSTM_D, 4 * MLSTM_HEADS)
L0_IN = sum(L0_SPLITS)
L0_MIX = SSD_D_INNER + MLSTM_D
L1_SPLITS = (GLA_DK, GLA_DK, GLA_DV, GLA_DV, 2 * GLA_RANK)
L1_IN = sum(L1_SPLITS)
N_EVEN_LAYERS = (DEPTH + 1) // 2
N_ODD_LAYERS = DEPTH // 2


def _split(u, sizes):
    return jnp.split(u, np.cumsum(sizes)[:-1].tolist(), axis=-1)

def _rev(t):
    return jnp.flip(t, axis=1)

def _lower_tri(n):
    return jnp.tril(jnp.ones((n, n), dtype=bool))

def _rmsnorm(x, g):
    xf = x.astype(jnp.float32)
    y = xf * lax.rsqrt(jnp.mean(xf * xf, axis=-1, keepdims=True) + NORM_EPS)
    return (y * g.astype(jnp.float32)).astype(x.dtype)

def _head_rmsnorm(x, g, n_heads):
    shp = x.shape
    xh = x.reshape(shp[:-1] + (n_heads, shp[-1] // n_heads))
    return _rmsnorm(xh, g.reshape(n_heads, -1)).reshape(shp)

def _dwconv(x, w, b):
    k = w.shape[0]
    y = lax.conv_general_dilated(x, w[:, None, :], window_strides=(1,), padding=[(k // 2, k // 2)],
                                 dimension_numbers=('NWC', 'WIO', 'NWC'), feature_group_count=x.shape[-1])
    return y + b

def _bidirectional(scan_fn, seq_fwd, seq_bwd, par_fwd=(), par_bwd=()):
    y_f = scan_fn(*seq_fwd, *par_fwd)
    y_b = scan_fn(*[_rev(t) for t in seq_bwd], *par_bwd)
    return y_f + _rev(y_b)

def _ssd_scan(x, dt, bm, cm, a):
    bsz, s, nh, p = x.shape
    g, n = bm.shape[2], bm.shape[3]
    e = nh // g
    l = SSD_CHUNK
    c = s // l
    dt = dt.astype(jnp.float32)
    xdt = (x * dt[..., None]).reshape(bsz, c, l, g, e, p)
    cs = jnp.cumsum((dt * a.astype(jnp.float32)).reshape(bsz, c, l, g, e), axis=2)
    bm = bm.reshape(bsz, c, l, g, n)
    cm = cm.reshape(bsz, c, l, g, n)
    cs_t = jnp.transpose(cs, (0, 3, 4, 1, 2))
    decay = jnp.exp(jnp.where(_lower_tri(l), cs_t[..., :, None] - cs_t[..., None, :], -jnp.inf))
    cb = jnp.einsum('bclgn,bcsgn->bgcls', cm, bm)
    y = jnp.einsum('bgecls,bcsgep->bclgep', cb[:, :, None] * decay, xdt)
    x_end = xdt * jnp.exp(cs[:, :, -1:] - cs)[..., None]
    states = jnp.einsum('bclgn,bclgep->cbgepn', bm, x_end)
    chunk_decay = jnp.exp(jnp.transpose(cs[:, :, -1], (1, 0, 2, 3)))

    def step(hs, inp):
        st, dec = inp
        return dec[..., None, None] * hs + st, hs

    _, h_prev = lax.scan(step, jnp.zeros(states.shape[1:], states.dtype), (states, chunk_decay))
    y = y + jnp.einsum('bclgn,cbgepn->bclgep', cm, h_prev) * jnp.exp(cs)[..., None]
    return y.reshape(bsz, s, nh, p)

def _mlstm_scan(q, k, v, ig, lf):
    bsz, s, nh, dk = q.shape
    dv = v.shape[-1]
    l = MLSTM_CHUNK
    c = s // l
    q = q.reshape(bsz, c, l, nh, dk)
    k = k.reshape(bsz, c, l, nh, dk)
    v = v.reshape(bsz, c, l, nh, dv)
    ig = ig.astype(jnp.float32).reshape(bsz, c, l, nh)
    fc = jnp.cumsum(lf.astype(jnp.float32).reshape(bsz, c, l, nh), axis=2)
    f_end = fc[:, :, -1]
    a = f_end[:, :, None] - fc + ig
    m_loc = jnp.max(a, axis=2)
    kw = k * jnp.exp(a - m_loc[:, :, None])[..., None]
    c_loc = jnp.einsum('bclhk,bclhv->cbhkv', kw, v)
    n_loc = jnp.transpose(jnp.sum(kw, axis=2), (1, 0, 2, 3))

    def step(carry, inp):
        c_st, n_st, m_st = carry
        c_l, n_l, m_l, f_l = inp
        m_new = jnp.maximum(f_l + m_st, m_l)
        s_old = jnp.exp(f_l + m_st - m_new)
        s_loc = jnp.exp(m_l - m_new)
        c_new = s_old[..., None, None] * c_st + s_loc[..., None, None] * c_l
        n_new = s_old[..., None] * n_st + s_loc[..., None] * n_l
        return (c_new, n_new, m_new), (c_st, n_st, m_st)

    init = (jnp.zeros(c_loc.shape[1:], c_loc.dtype), jnp.zeros(n_loc.shape[1:], n_loc.dtype),
            jnp.zeros((bsz, nh), jnp.float32))
    _, (c_st, n_st, m_st) = lax.scan(step, init, (c_loc, n_loc, jnp.transpose(m_loc, (1, 0, 2)),
                                                  jnp.transpose(f_end, (1, 0, 2))))
    fc_t = jnp.transpose(fc, (0, 3, 1, 2))
    ig_t = jnp.transpose(ig, (0, 3, 1, 2))
    dmat = jnp.where(_lower_tri(l), fc_t[..., :, None] - fc_t[..., None, :] + ig_t[..., None, :], -jnp.inf)
    m_inter = fc_t + jnp.transpose(m_st, (1, 2, 0))[..., None]
    m_t = jnp.maximum(m_inter, jnp.max(dmat, axis=-1))
    wmat = jnp.einsum('bclhk,bcshk->bhcls', q, k) * jnp.exp(dmat - m_t[..., None])
    s_inter = jnp.transpose(jnp.exp(m_inter - m_t), (0, 2, 3, 1))
    num = (jnp.einsum('bhcls,bcshv->bclhv', wmat, v)
           + s_inter[..., None] * jnp.einsum('bclhk,cbhkv->bclhv', q, c_st))
    den = (jnp.transpose(jnp.sum(wmat, axis=-1), (0, 2, 3, 1))
           + s_inter * jnp.einsum('bclhk,cbhk->bclh', q, n_st))
    floor = jnp.exp(-jnp.transpose(m_t, (0, 2, 3, 1)))
    h = num / jnp.maximum(jnp.abs(den), floor)[..., None]
    return h.reshape(bsz, s, nh, dv)

def _gla_scan(q, k, v, la):
    bsz, s, nh, dk = q.shape
    dv = v.shape[-1]
    l = GLA_CHUNK
    c = s // l
    q = q.reshape(bsz, c, l, nh, dk)
    k = k.reshape(bsz, c, l, nh, dk)
    v = v.reshape(bsz, c, l, nh, dv)
    bc = jnp.cumsum(la.astype(jnp.float32).reshape(bsz, c, l, nh, dk), axis=2)
    b_end = bc[:, :, -1:]
    q_in = q * jnp.exp(bc)
    att = jnp.einsum('bclhk,bcshk->bhcls', q_in, k * jnp.exp(-bc))
    att = jnp.where(_lower_tri(l), att, 0.0)
    o = jnp.einsum('bhcls,bcshv->bclhv', att, v)
    u = jnp.einsum('bclhk,bclhv->cbhkv', k * jnp.exp(b_end - bc), v)
    dec = jnp.exp(jnp.transpose(b_end[:, :, 0], (1, 0, 2, 3)))

    def step(st, inp):
        u_c, d_c = inp
        return d_c[..., None] * st + u_c, st

    _, s_prev = lax.scan(step, jnp.zeros(u.shape[1:], u.dtype), (u, dec))
    o = o + jnp.einsum('bclhk,cbhkv->bclhv', q_in, s_prev)
    return o.reshape(bsz, s, nh, dv)

def _ssd_mlstm_mixer(h, w_in, conv_w, conv_b, dt_bias, a_log, d_skip, ssd_norm, ig_bias, fg_bias, mlstm_norm, w_out):
    bsz, s, _ = h.shape
    z, xbc, dt_raw, q, k, v, o_pre, gates = _split(h @ w_in, L0_SPLITS)
    xbc = jax.nn.silu(_dwconv(xbc, conv_w, conv_b))
    xs, bm, cm = _split(xbc, (SSD_D_INNER, SSD_GROUPS * SSD_STATE, SSD_GROUPS * SSD_STATE))
    xs = xs.reshape(bsz, s, SSD_HEADS, SSD_HEADDIM)
    bm = bm.reshape(bsz, s, SSD_GROUPS, SSD_STATE)
    cm = cm.reshape(bsz, s, SSD_GROUPS, SSD_STATE)
    dt = jax.nn.softplus(dt_raw.reshape(bsz, s, 2, SSD_HEADS).astype(jnp.float32) + dt_bias)
    a = -jnp.exp(a_log.astype(jnp.float32))
    y = _bidirectional(_ssd_scan, (xs, dt[:, :, 0], bm, cm), (xs, dt[:, :, 1], bm, cm), (a[0],), (a[1],))
    y = y + d_skip[:, None] * xs
    y = _head_rmsnorm(y.reshape(bsz, s, SSD_D_INNER) * jax.nn.silu(z), ssd_norm, SSD_GROUPS)
    q = q.reshape(bsz, s, MLSTM_HEADS, MLSTM_HEADDIM)
    k = k.reshape(bsz, s, MLSTM_HEADS, MLSTM_HEADDIM) * MLSTM_HEADDIM ** -0.5
    v = v.reshape(bsz, s, MLSTM_HEADS, MLSTM_HEADDIM)
    gates = gates.reshape(bsz, s, 2, 2, MLSTM_HEADS).astype(jnp.float32)
    ig = gates[:, :, 0] + ig_bias
    lf = jax.nn.log_sigmoid(gates[:, :, 1] + fg_bias)
    hm = _bidirectional(_mlstm_scan, (q, k, v, ig[:, :, 0], lf[:, :, 0]), (q, k, v, ig[:, :, 1], lf[:, :, 1]))
    hm = jax.nn.sigmoid(o_pre) * hm.reshape(bsz, s, MLSTM_D)
    hm = _head_rmsnorm(hm, mlstm_norm, MLSTM_HEADS)
    return jnp.concatenate([y, hm], axis=-1) @ w_out

def _gla_mixer(h, w_in, gate_w2, gate_b, gla_norm, w_out):
    bsz, s, _ = h.shape
    q, k, v, r, g_lr = _split(h @ w_in, L1_SPLITS)
    q = q.reshape(bsz, s, GLA_HEADS, GLA_HEAD_DK) * GLA_HEAD_DK ** -0.5
    k = k.reshape(bsz, s, GLA_HEADS, GLA_HEAD_DK)
    v = v.reshape(bsz, s, GLA_HEADS, GLA_HEAD_DV)
    g_lr = g_lr.reshape(bsz, s, 2, GLA_RANK)
    logits = jnp.einsum('bsdr,drk->bsdk', g_lr, gate_w2) + gate_b
    la = (jax.nn.log_sigmoid(logits.astype(jnp.float32)) / GLA_TAU).reshape(bsz, s, 2, GLA_HEADS, GLA_HEAD_DK)
    o = _bidirectional(_gla_scan, (q, k, v, la[:, :, 0]), (q, k, v, la[:, :, 1]))
    o = _head_rmsnorm(o.reshape(bsz, s, GLA_DV), gla_norm, GLA_HEADS) * jax.nn.silu(r)
    return o @ w_out

def _conv_ffn(h, w_up, conv_w, conv_b, w_down):
    u = _dwconv(h @ w_up, conv_w, conv_b)
    gate, val = jnp.split(u, 2, axis=-1)
    return (jax.nn.gelu(gate, approximate=True) * val) @ w_down

def second_inputs(seed: int = 0) -> dict:
    key = jax.random.key(seed)
    keys = jax.random.split(key, 24)

    def nrm(i, shape, scale):
        return scale * jax.random.normal(keys[i], shape, jnp.float32)

    ne, no = N_EVEN_LAYERS, N_ODD_LAYERS
    dt0 = jnp.exp(jax.random.uniform(keys[5], (ne, 2, SSD_HEADS), jnp.float32, math.log(1e-3), math.log(1e-1)))
    return {
        'x': nrm(0, (BATCH, SEQ, D_MODEL), 1.0),
        'norm_g': 1.0 + nrm(1, (DEPTH, 4, D_MODEL), 0.05),
        'ab_w_in': nrm(2, (ne, D_MODEL, L0_IN), D_MODEL ** -0.5),
        'ab_conv_w': nrm(3, (ne, SSD_CONV, SSD_XBC), SSD_CONV ** -0.5),
        'ab_conv_b': nrm(4, (ne, SSD_XBC), 0.02),
        'ab_dt_bias': dt0 + jnp.log(-jnp.expm1(-dt0)),
        'ab_a_log': jnp.log(jax.random.uniform(keys[6], (ne, 2, SSD_HEADS), jnp.float32, 1.0, 16.0)),
        'ab_d_skip': 1.0 + nrm(7, (ne, SSD_HEADS), 0.1),
        'ab_ssd_norm': 1.0 + nrm(8, (ne, SSD_D_INNER), 0.05),
        'ab_ig_bias': nrm(9, (ne, 2, MLSTM_HEADS), 0.1),
        'ab_fg_bias': jnp.linspace(3.0, 6.0, MLSTM_HEADS, dtype=jnp.float32) + nrm(10, (ne, 2, MLSTM_HEADS), 0.1),
        'ab_mlstm_norm': 1.0 + nrm(11, (ne, MLSTM_D), 0.05),
        'ab_w_out': nrm(12, (ne, L0_MIX, D_MODEL), L0_MIX ** -0.5),
        'c_w_in': nrm(13, (no, D_MODEL, L1_IN), D_MODEL ** -0.5),
        'c_gate_w2': nrm(14, (no, 2, GLA_RANK, GLA_DK), GLA_RANK ** -0.5),
        'c_gate_b': nrm(15, (no, 2, GLA_DK), 0.1),
        'c_norm': 1.0 + nrm(16, (no, GLA_DV), 0.05),
        'c_w_out': nrm(17, (no, GLA_DV, D_MODEL), GLA_DV ** -0.5),
        'ffn_w_up': nrm(18, (DEPTH, D_MODEL, 2 * FFN_DIM_2), D_MODEL ** -0.5),
        'ffn_conv_w': nrm(19, (DEPTH, FFN_CONV, 2 * FFN_DIM_2), FFN_CONV ** -0.5),
        'ffn_conv_b': nrm(20, (DEPTH, 2 * FFN_DIM_2), 0.02),
        'ffn_w_down': nrm(21, (DEPTH, FFN_DIM_2, D_MODEL), FFN_DIM_2 ** -0.5),
    }

def second_block(x, norm_g, ab_w_in, ab_conv_w, ab_conv_b, ab_dt_bias, ab_a_log, ab_d_skip, ab_ssd_norm,
              ab_ig_bias, ab_fg_bias, ab_mlstm_norm, ab_w_out, c_w_in, c_gate_w2, c_gate_b, c_norm, c_w_out,
              ffn_w_up, ffn_conv_w, ffn_conv_b, ffn_w_down):
    for i in range(DEPTH):
        j = i // 2
        h = _rmsnorm(x, norm_g[i, 0])
        if i % 2 == 0:
            h = _ssd_mlstm_mixer(h, ab_w_in[j], ab_conv_w[j], ab_conv_b[j], ab_dt_bias[j], ab_a_log[j],
                                 ab_d_skip[j], ab_ssd_norm[j], ab_ig_bias[j], ab_fg_bias[j], ab_mlstm_norm[j],
                                 ab_w_out[j])
        else:
            h = _gla_mixer(h, c_w_in[j], c_gate_w2[j], c_gate_b[j], c_norm[j], c_w_out[j])
        x = x + _rmsnorm(h, norm_g[i, 1])
        f = _conv_ffn(_rmsnorm(x, norm_g[i, 2]), ffn_w_up[i], ffn_conv_w[i], ffn_conv_b[i], ffn_w_down[i])
        x = x + _rmsnorm(f, norm_g[i, 3])
    return x


def setup_inputs(seed=0):
    out = dict(first_inputs(seed))
    for name, value in second_inputs(seed + 1).items():
        if name != "x":
            out[name + "_2"] = value
    return out


def reference(
    x, c, ctx, c_ctx, w_ada, b_ada, norm_g, w_in, qk_g, rpb, conv_w, w_o, ffn_wi, ffn_wo,
    norm_g_2, ab_w_in_2, ab_conv_w_2, ab_conv_b_2, ab_dt_bias_2, ab_a_log_2, ab_d_skip_2,
    ab_ssd_norm_2, ab_ig_bias_2, ab_fg_bias_2, ab_mlstm_norm_2, ab_w_out_2, c_w_in_2,
    c_gate_w2_2, c_gate_b_2, c_norm_2, c_w_out_2, ffn_w_up_2, ffn_conv_w_2, ffn_conv_b_2,
    ffn_w_down_2,
):
    x = first_block(
        x, c, ctx, c_ctx, w_ada, b_ada, norm_g, w_in, qk_g, rpb, conv_w, w_o, ffn_wi, ffn_wo,
    )
    return second_block(
        x, norm_g_2, ab_w_in_2, ab_conv_w_2, ab_conv_b_2, ab_dt_bias_2, ab_a_log_2, ab_d_skip_2,
        ab_ssd_norm_2, ab_ig_bias_2, ab_fg_bias_2, ab_mlstm_norm_2, ab_w_out_2, c_w_in_2,
        c_gate_w2_2, c_gate_b_2, c_norm_2, c_w_out_2, ffn_w_up_2, ffn_conv_w_2, ffn_conv_b_2,
        ffn_w_down_2,
    )


_drawn_inputs = setup_inputs


def setup_inputs(seed=0):
    import zlib

    import numpy as np

    out = dict(_drawn_inputs(seed))
    spreads = {}
    factors = {'qk_g': 7.938, 'rpb': 8.0, 'ab_ig_bias_2': 8.0}
    for name, (base, spread) in spreads.items():
        noise = np.random.default_rng([zlib.crc32(name.encode()), seed]).standard_normal(out[name].shape)
        drawn = base * np.exp(spread * noise) if base else spread * noise
        out[name] = jnp.asarray(drawn.astype(out[name].dtype))
    for name, factor in factors.items():
        out[name] = (out[name] * factor).astype(out[name].dtype)
    return out
```

```python
import math
from contextlib import ExitStack

import concourse.bass as bass
import numpy as np
from concourse import mybir

F32 = mybir.dt.float32
F32R = mybir.dt.float32r
ACT = mybir.ActivationFunctionType
ALU = mybir.AluOpType
AX_X = mybir.AxisListType.X
ds = bass.ds

P = 128
D = 1024
KD = D // P
S = 256
T2 = 2 * S
ST = S // P
DEPTH = 2
HD = 64
GRID_W, WIN_R, WIN_C = 64, 8, 16
ROWS = S // GRID_W
A_HEADS, A_KV, B_HEADS = 6, 2, 6
FFN = 2816
KF = FFN // P
N_MOD = 9
EPS = 1e-6
NEG = -1e30
RPB_H, RPB_W = 2 * WIN_R - 1, 2 * WIN_C - 1
RPB_PAD = 2 * GRID_W - 1
SSD_HEADS, SSD_GROUPS, SSD_CONV = 16, 2, 5
ML_HEADS = 8
GLA_HEADS, GLA_RANK, GLA_TAU, GLA_CHUNK = 4, 16, 16.0, 64
BANK = 512
RING = 2
ARENA = 20496
SLOT = 4096
HALF = SLOT // 2

CONSTS = ["ident", "ones", "half_ones", "upto", "from_", "mask_upto", "mask_from", "rot", "swap",
          "gla_upto", "gla_from"]


def constants():
    k = np.arange(P)[:, None]
    m = np.arange(P)[None, :]
    c = {
        "ident": k == m,
        "ones": k >= 0 * m,
        "half_ones": k // HD == m // HD,
        "upto": k <= m,
        "from_": k >= m,
        "mask_upto": np.where(k <= m, 0.0, NEG),
        "mask_from": np.where(k >= m, 0.0, NEG),
        "swap": k == (m + HD) % P,
        "gla_upto": (k <= m) & (k // GLA_CHUNK == m // GLA_CHUNK),
        "gla_from": (k >= m) & (k // GLA_CHUNK == m // GLA_CHUNK),
    }
    rot = np.zeros((P, P))
    half = (np.arange(P) // 16) % 2
    for j in range(P):
        if half[j] == 0:
            rot[j + 16, j] = -1.0
        else:
            rot[j - 16, j] = 1.0
    c["rot"] = rot
    freqs = HD // 4
    pos = np.arange(S)
    freq = (1.0 / (np.float32(10000.0) ** (np.arange(freqs, dtype=np.float32) / np.float32(freqs)))).astype(np.float32)
    axis = (np.arange(P) % HD) // 32
    f = np.arange(P) % 16
    where = np.where(axis[:, None] == 0, (pos // GRID_W)[None, :], (pos % GRID_W)[None, :]).astype(np.float32)
    ang = (where * freq[f][:, None]).astype(np.float32)
    q = np.arange(P) % GRID_W
    key = np.arange(S) % GRID_W
    start = np.clip(q - WIN_C // 2, 0, GRID_W - WIN_C)
    inside = (key[None, :] >= start[:, None]) & (key[None, :] < start[:, None] + WIN_C)
    parts = [np.asarray(c[n], np.float32) * np.ones((P, P), np.float32) for n in CONSTS]
    parts += [np.cos(ang), np.sin(ang), np.where(inside, 0.0, NEG)]
    parts += [(k // GRID_W == m // GRID_W) & (k % GRID_W + m % GRID_W == GRID_W - 1)]
    parts += [k % 32 == np.arange(2)[None, :]]
    return np.ascontiguousarray(np.concatenate([np.asarray(p, np.float32) for p in parts], axis=1))


CONST_W = len(CONSTS) * P + 3 * S


class Signal:

    def __init__(self, sem):
        self.sem = sem
        self.base = 0

    def at(self, n):
        return self.base + n

    def passed(self, n):
        self.base += n


class Chain:

    def __init__(self, sem):
        self.sem = sem
        self.n = 0

    def link(self, eng, ins):
        ins.then_inc(self.sem, 1)
        self.n += 1
        eng.wait_ge(self.sem, self.n)


def turns(eng, n, period, body):
    full = n // period
    if full >= 2:
        with eng.Fori(0, full) as turn:
            for k in range(period):
                body(turn, k)
    else:
        for turn in range(full):
            for k in range(period):
                body(turn, k)
    for k in range(n - full * period):
        body(full, k)


def two_blocks(nc, a, out, stop=None):
    ctx = ExitStack()
    with ctx:
        place = [(nc.sbuf_base + 31) // 32 * 32]

        def sb(name, shape, dt=F32, at=None):
            size = 4 * int(np.prod(shape[1:]))
            offset = place[0] if at is None else at
            if at is None:
                place[0] += (size + 31) // 32 * 32
            return nc.alloc_sbuf_tensor_at(name, shape, dt, offset=offset)

        def signal(name):
            return Signal(ctx.enter_context(nc.semaphore(name)))

        def chain(name):
            return Chain(ctx.enter_context(nc.semaphore(name)))

        ring = [sb(f"ring{i}", [P, SLOT]) for i in range(RING)]
        h = sb("h", [P, KD, T2])
        uh_at = place[0]
        uh = sb("uh", [P, KD, T2], F32R)
        ul_at = place[0]
        ul = sb("ul", [P, KD, T2], F32R)
        u32 = sb("u32", [P, 2 * KD, S], F32, at=uh_at)
        ul32 = sb("ul32", [P, KD * T2], F32, at=ul_at)
        wh = [sb(f"wh{i}", [P, HALF], F32R) for i in range(2)]
        wl = [sb(f"wl{i}", [P, HALF], F32R) for i in range(2)]
        arena = sb("arena", [P, ARENA])
        const = sb("const", [P, CONST_W])
        ps = ctx.enter_context(nc.psum_tensor("ps", [P, 8, BANK], F32))

        def mat(name):
            i = CONSTS.index(name)
            return const[:, i * P:(i + 1) * P]

        tables = len(CONSTS) * P
        cos_t = const[:, tables:tables + S]
        sin_t = const[:, tables + S:tables + 2 * S]
        window = const[:, tables + 2 * S:tables + 3 * S]
        ident, ones = mat("ident"), mat("ones")

        class Arena:

            def __init__(self, start=0):
                self.at = start

            def take(self, *shape):
                n = int(np.prod(shape))
                v = arena[:, self.at:self.at + n]
                self.at += n
                assert self.at <= ARENA, self.at
                if len(shape) == 2:
                    v = v.rearrange("p (a b) -> p a b", a=shape[0])
                if len(shape) == 3:
                    v = v.rearrange("p (a b c) -> p a b c", a=shape[0], b=shape[1])
                return v

        vectors = [("b_ada", a["b_ada"].rearrange("l (r p) -> (l r) p", p=P)),
                   ("c", a["c"].rearrange("l (r p) -> (l r) p", p=P)),
                   ("c_ctx", a["c_ctx"].rearrange("(r p) -> r p", p=P)),
                   ("norm_g", a["norm_g"].rearrange("l i (r p) -> (l i r) p", p=P)),
                   ("conv_w", a["conv_w"].rearrange("l i (r p) -> (l i r) p", p=P)),
                   ("norm_g_2", a["norm_g_2"].rearrange("l i (r p) -> (l i r) p", p=P)),
                   ("ab_conv_w", a["ab_conv_w_2"].rearrange("l i (r p) -> (l i r) p", p=P)),
                   ("ab_conv_b", a["ab_conv_b_2"].rearrange("l (r p) -> (l r) p", p=P)),
                   ("ssd_norm", a["ab_ssd_norm_2"].rearrange("l (r p) -> (l r) p", p=P)),
                   ("mlstm_norm", a["ab_mlstm_norm_2"].rearrange("l (r p) -> (l r) p", p=P)),
                   ("gate_b", a["c_gate_b_2"].rearrange("l i (r p) -> (l i r) p", p=P)),
                   ("gla_norm", a["c_norm_2"].rearrange("l (r p) -> (l r) p", p=P)),
                   ("ffn_conv_w", a["ffn_conv_w_2"].rearrange("l i (r p) -> (l i r) p", p=P)),
                   ("ffn_conv_b", a["ffn_conv_b_2"].rearrange("l (r p) -> (l r) p", p=P))]
        col_at, pieces, n_rows = {}, [], 0
        for name, v in vectors:
            col_at[name] = n_rows
            r = 0
            while r < v.shape[0]:
                m = min(v.shape[0] - r, P - n_rows % P)
                pieces.append((v[r:r + m, :], n_rows // P, n_rows % P, m))
                r += m
                n_rows += m
        row_tiles = [min(P, n_rows - P * t) for t in range((n_rows + P - 1) // P)]
        cols = sb("cols", [P, n_rows])
        head_gain = sb("head_gain", [P, DEPTH * 2])
        d_skip = sb("d_skip", [P, KD])
        gate_bias = sb("gate_bias", [P, 64])
        a_log = sb("a_log", [P, 2 * SSD_HEADS])
        mod = sb("mod", [P, DEPTH, N_MOD * KD, 2])
        pre_scale = sb("pre_scale", [P, KD, 2])
        post_scale = sb("post_scale", [P, KD, 2])
        rstd = sb("rstd", [P, T2])
        eps = sb("eps", [P, 1])
        CM = Arena(12288)
        act_c = CM.take(KD, 32)
        pick = CM.take(2)
        mod_rows = CM.take(2, 512)

        def col(name, i, n=1):
            return cols[:, col_at[name] + i:col_at[name] + i + n]

        ready = [signal(f"slot{i}_loaded") for i in range(RING)]
        high = signal("high_parts_done")
        split = signal("granules_split")
        prod = signal("products_done")
        band_load = signal("bands_loaded")
        flip_load = signal("flip_loaded")
        act_free = signal("act_evacuated")
        dve_free = signal("dve_evacuated")
        gate_done = signal("gate_done")
        loaded = signal("inputs_loaded")
        stored = signal("stored")
        pe_step, act_step, dve_step, pool_step = (signal(f"{e}_step") for e in ("pe", "act", "dve", "pool"))
        aux = signal("second_dve_step")
        act_chain, dve_chain, pool_chain = chain("act_chain"), chain("dve_chain"), chain("pool_chain")

        def stage():
            return nc.Block(no_gpsimd_drain=True)

        class Weights:

            def __init__(self, n, loads, parts=1, count=None, split=True, looped=True):
                self.n, self.loads, self.parts, self.split = n, loads, parts, split
                self.count = count or [2 if split else 1] * n
                self.looped = looped and count is None

        def column_tiles(w, k, width):
            v = w.rearrange("(k p) c -> p k c", p=P)

            def loads(i, slot):
                to = ring[slot][:, 0:k * width].rearrange("p (k c) -> p k c", k=k)
                return [(to, v[:, :, ds(i * width, width)])]
            return loads

        def pair_tiles(w, half, width):
            v = w.rearrange("(k p) c -> p k c", p=P)

            def loads(i, slot):
                to = ring[slot][:, 0:KD * 2 * width].rearrange("p (k c) -> p k c", k=KD)
                return [(to[:, :, 0:width], v[:, :, ds(i * width, width)]),
                        (to[:, :, width:2 * width], v[:, :, ds(i * width + half, width)])]
            return loads

        def listed_tiles(w, spans):
            v = w.rearrange("(k p) c -> p k c", p=P)

            def loads(i, slot):
                width = sum(n for _, n in spans[i])
                k = w.shape[0] // P
                to = ring[slot][:, 0:k * width].rearrange("p (k c) -> p k c", k=k)
                got, o = [], 0
                for c0, n in spans[i]:
                    got.append((to[:, :, o:o + n], v[:, :, c0:c0 + n]))
                    o += n
                return got
            return loads

        IN_SPANS = [[(0, 384)], [(384, 384)], [(768, 256)], [(1024, 384)], [(1408, 384)], [(1792, 512)], [(2304, 256)]]
        plan = {}
        order = []

        def planned(key, weights):
            plan[key] = weights
            order.append(key)

        def row_tiles_of(w, k):
            v = w.rearrange("(k p) c -> p k c", p=P)

            def loads(i, slot):
                n = min(4, k - 4 * i)
                return [(ring[slot][:, 0:n * D].rearrange("p (k c) -> p k c", k=n), v[:, 4 * i:4 * i + n, :])]
            return loads

        def granules(spans):
            return [(sum(n for _, n in span) + 255) // 256 for span in spans]

        for l in range(DEPTH):
            planned(("ada", l), Weights(N_MOD * KD // 4, column_tiles(a["w_ada"][l], KD, 512), split=False))
        for l in range(DEPTH):
            for f in range(2):
                if f == 1:
                    planned(("in", l), Weights(len(IN_SPANS), listed_tiles(a["w_in"][l], IN_SPANS), count=granules(IN_SPANS)))
                    planned(("o", l), Weights(2, column_tiles(a["w_o"][l], KD, 512)))
                planned(("up", l, f), Weights(KF // 2, pair_tiles(a["ffn_wi"][l, f], FFN, 256), parts=2))
                planned(("down", l, f), Weights((KF + 3) // 4, row_tiles_of(a["ffn_wo"][l, f], KF), count=[2] * 5 + [1]))
        AB_SPANS = [[(512 * i, 512)] for i in range(5)] + [[(2592 + 512 * i, 512)] for i in range(8)] + [[(2560, 32), (6688, 32)]]
        planned("ab_in", Weights(len(AB_SPANS), listed_tiles(a["ab_w_in_2"][0], AB_SPANS), count=granules(AB_SPANS)))
        planned("ab_out", Weights(4, column_tiles(a["ab_w_out_2"][0], 2 * KD, 256)))
        planned(("up2", 0), Weights(KF // 2, pair_tiles(a["ffn_w_up_2"][0], FFN, 256), parts=2))
        planned(("down2", 0), Weights((KF + 3) // 4, row_tiles_of(a["ffn_w_down_2"][0], KF), count=[2] * 5 + [1]))
        C_SPANS = [[(512 * i, 512)] for i in range(6)] + [[(3072, 32)]]
        planned("c_in", Weights(len(C_SPANS), listed_tiles(a["c_w_in_2"][0], C_SPANS), count=granules(C_SPANS)))
        planned("c_out", Weights(2, column_tiles(a["c_w_out_2"][0], KD, 512)))
        planned(("up2", 1), Weights(KF // 2, pair_tiles(a["ffn_w_up_2"][1], FFN, 256), parts=2))
        planned(("down2", 1), Weights((KF + 3) // 4, row_tiles_of(a["ffn_w_down_2"][1], KF), count=[2] * 5 + [1]))

        def parts_of(w, i):
            return len(w.loads(i, 0)) if not w.looped else w.parts

        def load_first(sp, key):
            w = plan[key]
            for k in range(min(RING, w.n)):
                yield k, lambda k=k: [sp.dma_start(to, fr).then_inc(ready[k].sem, 16) for to, fr in w.loads(k, k)]

        def stream(sp, key):
            w = plan[key]
            gone = split if w.split else prod
            done = np.cumsum([0] + w.count)
            if w.looped:
                def load(turn, k):
                    sp.wait_ge(gone.sem, gone.at((turn * RING + k + 1) * w.count[0]))
                    for to, fr in w.loads((turn + 1) * RING + k, k):
                        sp.dma_start(to, fr).then_inc(ready[k].sem, 16)
                turns(sp, max(w.n - RING, 0), RING, load)
            else:
                for i in range(RING, w.n):
                    sp.wait_ge(gone.sem, gone.at(int(done[i - RING + 1])))
                    for to, fr in w.loads(i, i % RING):
                        sp.dma_start(to, fr).then_inc(ready[i % RING].sem, 16)
            at = order.index(key) + 1
            if at < len(order):
                for k, load in load_first(sp, order[at]):
                    last = [i for i in range(w.n) if i % RING == k]
                    if last:
                        sp.wait_ge(gone.sem, gone.at(int(done[last[-1] + 1])))
                    load()

        def split_high(act, key, g, slot, tile_turn, raw, shape_of, b):
            tile_loaded(act, key, tile_turn, slot)
            act.wait_ge(prod.sem, prod.at(g - 1))
            act.activation(shape_of(wh[b]), raw, ACT.Copy).then_inc(high.sem, 1)

        def split_low(dve, g, raw, shape_of, b):
            dve.wait_ge(high.sem, high.at(g + 1))
            dve.tensor_tensor(shape_of(wl[b]), raw, shape_of(wh[b]), ALU.subtract).then_inc(split.sem, 1)

        def multiply(pe, to, terms, start=True, stop=True):
            passes = []
            for (sh, sl), (mh, ml) in terms:
                passes += [(sh, mh), (sh, ml), (sl, mh)]
            for n, (stat, mov) in enumerate(passes):
                mm = pe.matmul(to, stat, mov, start=start and n == 0, stop=stop and n == len(passes) - 1)
            return mm

        def with_lead(eng, n, lead, body):
            turns(eng, n - lead, 4, lambda turn, k: body(turn, k, True))
            for g in range(n - lead, n):
                body(g // 4, g % 4, False)

        def tile_loaded(pe, key, turn, k):
            w = plan[key]
            if w.looped:
                pe.wait_ge(ready[k].sem, ready[k].at((turn + 1) * 16 * w.parts))
            else:
                n = sum(parts_of(w, i) for i in range(k, turn * RING + k + 1, RING))
                pe.wait_ge(ready[k].sem, ready[k].at(16 * n))

        def stage_done(key):
            w = plan[key]
            prod.passed(sum(w.count))
            if w.split:
                high.passed(sum(w.count))
                split.passed(sum(w.count))
            for k in range(RING):
                ready[k].passed(16 * sum(parts_of(w, i) for i in range(k, w.n, RING)))

        def slot_view(k, n_k, width):
            return ring[k][:, 0:n_k * width].rearrange("p (k c) -> p k c", k=n_k)

        def setup():
            mem = Arena()
            rows = mem.take(len(row_tiles), P)
            tokens = mem.take(2 * ST, D)
            groups = len(row_tiles) + KD
            n_loads = 1 + 1 + len(pieces) + 2 * ST + 4 + 4
            with stage() as block:
                @block.sync
                def _(sp):
                    sp.dma_start(const[:, :], a["const"][:, 0:CONST_W]).then_inc(loaded.sem, 16)
                    sp.dma_start(pick, a["const"][:, CONST_W + P:CONST_W + P + 2]).then_inc(loaded.sem, 16)
                    for v, t, r, m in pieces:
                        sp.dma_start(rows[r:r + m, t, :], v).then_inc(loaded.sem, 16)
                    for t in range(ST):
                        sp.dma_start(tokens[:, t, :], a["x"][0, t * P:(t + 1) * P, :]).then_inc(loaded.sem, 16)
                        sp.dma_start(tokens[:, ST + t, :], a["ctx"][0, t * P:(t + 1) * P, :]).then_inc(loaded.sem, 16)
                    for half in range(2):
                        sp.dma_start(head_gain[half * HD:(half + 1) * HD, :],
                                     a["qk_g"].rearrange("l i d -> d (l i)"),
                                     allow_slow_non_contiguous=True).then_inc(loaded.sem, 16)
                        sp.dma_start(d_skip[half * HD:(half + 1) * HD, :],
                                     bass.AP(a["ab_d_skip_2"].tensor, half, [[0, HD], [2, KD]]),
                                     allow_slow_non_contiguous=True).then_inc(loaded.sem, 16)
                    for v, at, n in ((a["ab_dt_bias_2"], 0, 32), (a["ab_ig_bias_2"], 32, 16), (a["ab_fg_bias_2"], 48, 16)):
                        sp.dma_start(gate_bias[:, at:at + n], bass.AP(v.tensor, 0, [[0, P], [1, n]])).then_inc(loaded.sem, 16)
                    sp.dma_start(a_log[:, :], bass.AP(a["ab_a_log_2"].tensor, 0, [[0, P], [1, 32]])).then_inc(loaded.sem, 16)
                    for _, load in load_first(sp, order[0]):
                        load()

                @block.tensor
                def _(pe):
                    pe.wait_ge(loaded.sem, loaded.at(16 * n_loads))
                    for t, m in enumerate(row_tiles):
                        pe.transpose(ps[:, t % 8, 0:m], rows[0:m, t, :], ident[0:m, 0:m]).then_inc(prod.sem, 1)
                    for j in range(KD):
                        g = len(row_tiles) + j
                        if g >= 8:
                            pe.wait_ge(dve_free.sem, dve_free.at(g - 7))
                        for t in range(2 * ST):
                            last = pe.transpose(ps[:, g % 8, t * P:(t + 1) * P], tokens[:, t, j * P:(j + 1) * P], ident)
                        last.then_inc(prod.sem, 1)

                @block.gpsimd
                def _(pool):
                    pool.memset(act_c, 0.0).then_inc(pool_step.sem, 1)

                @block.vector
                def _(dve):
                    dve.memset(eps[:, :], EPS)
                    for t, m in enumerate(row_tiles):
                        dve.wait_ge(prod.sem, prod.at(t + 1))
                        dve.tensor_copy(cols[:, t * P:t * P + m], ps[:, t % 8, 0:m]).then_inc(dve_free.sem, 1)
                    for j in range(KD):
                        g = len(row_tiles) + j
                        dve.wait_ge(prod.sem, prod.at(g + 1))
                        dve.tensor_copy(h[:, j, :], ps[:, g % 8, :]).then_inc(dve_free.sem, 1)

                @block.scalar
                def _(act):
                    act.wait_ge(dve_free.sem, dve_free.at(len(row_tiles)))
                    act.wait_ge(pool_step.sem, pool_step.at(1))
                    act.activation(act_c[:, :, 0], col("c", 0, KD), ACT.Silu).then_inc(act_free.sem, 1)
                    act.activation(act_c[:, :, 1], col("c_ctx", 0, KD), ACT.Silu).then_inc(act_free.sem, 1)
                    for _ in range(6):
                        act.nop().then_inc(act_free.sem, 1)
            prod.passed(groups)
            dve_free.passed(groups)
            act_free.passed(8)
            pool_step.passed(1)
            loaded.passed(16 * n_loads)

        def modulation(l):
            key = ("ada", l)
            w = plan[key]
            with stage() as block:
                @block.sync
                def _(sp):
                    stream(sp, key)

                @block.tensor
                def _(pe):
                    def rows(turn, k):
                        tile_loaded(pe, key, turn, k)
                        pe.wait_ge(act_free.sem, act_free.at(turn * 2 + k - 1))
                        wt = slot_view(k, KD, 512)
                        for kk in range(KD):
                            q = 32 * (kk % 4)
                            last = pe.matmul(ps[q:q + 32, k, :], act_c[:, kk, :], wt[:, kk, :], start=(kk < 4), stop=(kk >= 4))
                        last.then_inc(prod.sem, 1)

                    def columns(turn, k):
                        pe.wait_ge(act_free.sem, act_free.at(turn * 2 + k + 1))
                        pe.wait_ge(dve_free.sem, dve_free.at(turn * 2 + k - 1))
                        for m in range(4):
                            last = pe.matmul(ps[:, 2 + k, 2 * m:2 * m + 2], mod_rows[:, k, m * P:(m + 1) * P], pick, start=True, stop=True)
                        last.then_inc(pe_step.sem, 1)

                    def step(turn, k):
                        rows(turn if k == 0 else turn + 1, 1 - k)
                        columns(turn, k)
                    rows(0, 0)
                    turns(pe, w.n - 1, 2, step)
                    columns((w.n - 1) // 2, (w.n - 1) % 2)

                @block.scalar
                def _(act):
                    def tile(turn, k):
                        act.wait_ge(prod.sem, prod.at(turn * 2 + k + 1))
                        act.wait_ge(dve_free.sem, dve_free.at(turn * 2 + k - 1))
                        act.activation(mod_rows[:, k, :], ps[:, k, :], ACT.Copy).then_inc(act_free.sem, 1)
                    turns(act, w.n, 2, tile)

                @block.vector
                def _(dve):
                    def tile(turn, k):
                        i = turn * 2 + k
                        dve.wait_ge(pe_step.sem, pe_step.at(i + 1))
                        bias = cols[:, ds(col_at["b_ada"] + l * N_MOD * KD + i * 4, 4)]
                        dve.tensor_tensor(mod[:, l, ds(i * 4, 4), :],
                                          ps[:, 2 + k, 0:8].rearrange("p (a b) -> p a b", a=4),
                                          bias.unsqueeze(2).broadcast_to([P, 4, 2]), ALU.add).then_inc(dve_free.sem, 1)
                    turns(dve, w.n, 2, tile)
            stage_done(key)
            act_free.passed(w.n)
            pe_step.passed(w.n)
            dve_free.passed(w.n)

        def pre(l, i, gi, T=T2):
            n_s = T // S
            sq = Arena().take(KD, T2)
            scaled = Arena(KD * T2).take(KD, T2)
            with stage() as block:
                @block.scalar
                def _(act):
                    for k in range(KD):
                        act.activation(sq[:, k, 0:T], h[:, k, 0:T], ACT.Square).then_inc(act_step.sem, 1)
                    act.wait_ge(pe_step.sem, pe_step.at(1))
                    act_chain.link(act, act.activation(rstd[:, 0:T], ps[:, 0, 0:T], ACT.Ln, scale=1.0 / D, bias=eps[:, 0:1]))
                    act.activation(rstd[:, 0:T], rstd[:, 0:T], ACT.Exp, scale=-0.5).then_inc(act_step.sem, 1)
                    for k in range(KD):
                        for s in range(n_s):
                            t = slice(s * S, (s + 1) * S)
                            act.wait_ge(dve_step.sem, dve_step.at(3 + n_s * k + s))
                            act.activation(uh[:, k, t], scaled[:, k, t], ACT.Identity,
                                           bias=mod[:, l, i * KD + k, s:s + 1]).then_inc(act_step.sem, 1)

                @block.tensor
                def _(pe):
                    for k in range(KD):
                        pe.wait_ge(act_step.sem, act_step.at(k + 1))
                        last = pe.matmul(ps[:, 0, 0:T], ones, sq[:, k, 0:T], start=(k == 0), stop=(k == KD - 1))
                    last.then_inc(pe_step.sem, 1)

                @block.vector
                def _(dve):
                    dve.tensor_scalar(pre_scale[:, :, :], mod[:, l, (i + 1) * KD:(i + 2) * KD, :], 1.0, None,
                                      ALU.add).then_inc(dve_step.sem, 1)
                    dve.wait_ge(dve_step.sem, dve_step.at(1))
                    g = col("norm_g", (l * 6 + gi) * KD, KD)
                    dve.tensor_tensor(pre_scale[:, :, :], pre_scale[:, :, :], g.unsqueeze(2).broadcast_to([P, KD, 2]),
                                      ALU.mult).then_inc(dve_step.sem, 1)
                    dve.wait_ge(dve_step.sem, dve_step.at(2))
                    dve.wait_ge(act_step.sem, act_step.at(KD + 1))
                    lag = 2
                    parts = [(k, s, slice(s * S, (s + 1) * S)) for k in range(KD) for s in range(n_s)]
                    for n in range(len(parts) + lag):
                        if n < len(parts):
                            k, s, t = parts[n]
                            dve.scalar_tensor_tensor(out=scaled[:, k, t], in0=h[:, k, t], scalar=pre_scale[:, k, s:s + 1],
                                                     in1=rstd[:, t], op0=ALU.mult, op1=ALU.mult).then_inc(dve_step.sem, 1)
                        if n >= lag:
                            k, s, t = parts[n - lag]
                            dve.wait_ge(act_step.sem, act_step.at(KD + 2 + n - lag))
                            dve.scalar_tensor_tensor(out=ul[:, k, t], in0=scaled[:, k, t], scalar=mod[:, l, i * KD + k, s:s + 1],
                                                     in1=uh[:, k, t], op0=ALU.add, op1=ALU.subtract)
            act_step.passed(KD + 1 + n_s * KD)
            pe_step.passed(1)
            dve_step.passed(2 + n_s * KD)

        def post(scales, T, prepare=None, n_prepared=0):
            n_s = T // S
            mem = Arena()
            sq = mem.take(KD, T)
            part = mem.take(KD, T)
            y0 = mem.take(T)
            with stage() as block:
                @block.scalar
                def _(act):
                    for k in [*range(1, KD), 0]:
                        if k == 0:
                            act.wait_ge(dve_step.sem, dve_step.at(1))
                        act.activation(sq[:, k, :], ps[:, k, 0:T] if k else y0, ACT.Square).then_inc(act_step.sem, 1)
                    act.wait_ge(pe_step.sem, pe_step.at(1))
                    act_chain.link(act, act.activation(rstd[:, 0:T], ps[:, 0, 0:T], ACT.Ln, scale=1.0 / D, bias=eps[:, 0:1]))
                    act.activation(rstd[:, 0:T], rstd[:, 0:T], ACT.Exp, scale=-0.5).then_inc(act_step.sem, 1)

                @block.tensor
                def _(pe):
                    pe.wait_ge(dve_step.sem, dve_step.at(1))
                    for n, k in enumerate([*range(1, KD), 0]):
                        pe.wait_ge(act_step.sem, act_step.at(n + 1))
                        last = pe.matmul(ps[:, 0, 0:T], ones, sq[:, k, :], start=(n == 0), stop=(n == KD - 1))
                    last.then_inc(pe_step.sem, 1)

                @block.vector
                def _(dve):
                    dve.tensor_copy(y0, ps[:, 0, 0:T]).then_inc(dve_step.sem, 1)
                    if prepare is not None:
                        prepare(dve)
                    dve.wait_ge(dve_step.sem, dve_step.at(1 + n_prepared))
                    dve.wait_ge(act_step.sem, act_step.at(KD + 1))
                    for k in range(KD):
                        for s in range(n_s):
                            t = slice(s * S, (s + 1) * S)
                            dve.scalar_tensor_tensor(out=part[:, k, t], in0=ps[:, k, t] if k else y0[:, t], scalar=scales(k, s),
                                                     in1=rstd[:, t], op0=ALU.mult, op1=ALU.mult).then_inc(dve_step.sem, 1)
                        if k % 2:
                            dve.wait_ge(dve_step.sem, dve_step.at(1 + n_prepared + n_s * (k + 1)))
                            dve.tensor_tensor(h[:, k, 0:T], h[:, k, 0:T], part[:, k, :], ALU.add)

                @block.gpsimd
                def _(pool):
                    for k in range(0, KD, 2):
                        pool.wait_ge(dve_step.sem, dve_step.at(1 + n_prepared + n_s * (k + 1)))
                        pool.tensor_tensor(h[:, k, 0:T], h[:, k, 0:T], part[:, k, :], ALU.add).then_inc(pool_step.sem, 1)
                    pool.wait_ge(pool_step.sem, pool_step.at(KD // 2))
            act_step.passed(KD + 1)
            pe_step.passed(1)
            dve_step.passed(1 + n_prepared + n_s * KD)
            pool_step.passed(KD // 2)

        def post1(l, i, gi, weight, T=T2):
            def prepare(dve):
                dve.tensor_scalar(post_scale[:, :, :], mod[:, l, (i + 2) * KD:(i + 3) * KD, :], weight, None,
                                  ALU.mult).then_inc(dve_step.sem, 1)
                dve.wait_ge(dve_step.sem, dve_step.at(2))
                g = col("norm_g", (l * 6 + gi) * KD, KD)
                dve.tensor_tensor(post_scale[:, :, :], post_scale[:, :, :], g.unsqueeze(2).broadcast_to([P, KD, 2]),
                                  ALU.mult).then_inc(dve_step.sem, 1)
            post(lambda k, s: post_scale[:, k, s:s + 1], T, prepare, 2)

        MID = Arena()
        mid = MID.take(KF, T2)
        gates = MID.take(4, T2)

        def pair_granule(k):
            raw = ring[k // 2][:, :].rearrange("p (k a f c) -> p k a f c", k=KD, a=2, f=2)[:, :, :, k % 2, :]
            return raw, lambda v: v[:, :].rearrange("p (k a c) -> p k a c", k=KD, a=2)

        def split_pairs(key, act=None, dve=None):
            def high_of(turn, k):
                raw, shaped = pair_granule(k)
                split_high(act, key, turn * 4 + k, k // 2, turn, raw, shaped, k % 2)

            def low_of(turn, k):
                raw, shaped = pair_granule(k)
                split_low(dve, turn * 4 + k, raw, shaped, k % 2)
            return high_of if act is not None else low_of

        def pair_products(pe, key, T, free):
            def granule(turn, k):
                g = turn * 4 + k
                pe.wait_ge(split.sem, split.at(g + 1))
                pe.wait_ge(free.sem, free.at(g - 3))
                vh, vl = (v[k % 2][:, :].rearrange("p (k a c) -> p k a c", k=KD, a=2) for v in (wh, wl))
                for part in range(2):
                    last = multiply(pe, ps[:, 2 * k + part, 0:T],
                                    [((vh[:, kk, part, :], vl[:, kk, part, :]), (uh[:, kk, 0:T], ul[:, kk, 0:T])) for kk in range(KD)])
                last.then_inc(prod.sem, 1)
            turns(pe, KF, 4, granule)

        def ahead(turn, k, lead=2):
            return (turn, k + lead) if k + lead < 4 else (turn + 1, k + lead - 4)

        def ffn_up(key, T, bands_of=None):
            with stage() as block:
                @block.sync
                def _(sp):
                    stream(sp, key)

                @block.tensor
                def _(pe):
                    pair_products(pe, key, T, dve_free)

                @block.scalar
                def _(act):
                    high_of = split_pairs(key, act=act)

                    def granule(turn, k, more):
                        g = turn * 4 + k
                        if more:
                            high_of(*ahead(turn, k))
                        act.wait_ge(prod.sem, prod.at(g + 1))
                        act.wait_ge(dve_free.sem, dve_free.at(g - 3))
                        act.activation(gates[:, k, 0:T], ps[:, 2 * k, 0:T], ACT.Silu).then_inc(gate_done.sem, 1)
                    high_of(0, 0)
                    high_of(0, 1)
                    with_lead(act, KF, 2, granule)

                @block.vector
                def _(dve):
                    low_of = split_pairs(key, dve=dve)

                    def granule(turn, k, more):
                        g = turn * 4 + k
                        if more:
                            low_of(*ahead(turn, k))
                        dve.wait_ge(gate_done.sem, gate_done.at(g + 1))
                        dve.tensor_tensor(mid[:, ds(g, 1), 0:T].squeeze(1), gates[:, k, 0:T], ps[:, 2 * k + 1, 0:T],
                                          ALU.mult).then_inc(dve_free.sem, 1)
                    low_of(0, 0)
                    low_of(0, 1)
                    with_lead(dve, KF, 2, granule)

                if bands_of is not None:
                    @block.gpsimd
                    def _(pool):
                        load_bands(pool, bands_of)
            stage_done(key)
            dve_free.passed(KF)
            gate_done.passed(KF)
            if bands_of is not None:
                pool_step.passed(1)
                flip_load.passed(16)
                band_load.passed(16 * (2 + B_HEADS * ROWS))

        def ffn_down(key, x, T):
            w = plan[key]
            n = KF // 2
            with stage() as block:
                @block.sync
                def _(sp):
                    stream(sp, key)

                def views(g):
                    raw = ring[(g // 2) % RING][:, (g % 2) * HALF:(g % 2 + 1) * HALF]
                    c = (2 * g) % KD
                    return raw, x[:, 2 * g:2 * g + 2, 0:T], uh[:, c:c + 2, 0:T], ul[:, c:c + 2, 0:T]

                @block.scalar
                def _(act):
                    for g in range(n):
                        raw, of, to_h, _ = views(g)
                        tile_loaded(act, key, g // 4, (g // 2) % RING)
                        if g >= 2:
                            act.wait_ge(prod.sem, prod.at(g - 1))
                        act.activation(wh[g % 2][:, :], raw, ACT.Copy)
                        act.activation(to_h, of, ACT.Copy).then_inc(high.sem, 1)

                @block.vector
                def _(dve):
                    for g in range(n):
                        raw, of, to_h, to_l = views(g)
                        dve.wait_ge(high.sem, high.at(g + 1))
                        dve.tensor_tensor(wl[g % 2][:, :], raw, wh[g % 2][:, :], ALU.subtract)
                        dve.tensor_tensor(to_l, of, to_h, ALU.subtract).then_inc(split.sem, 1)

                @block.tensor
                def _(pe):
                    for g in range(n):
                        pe.wait_ge(split.sem, split.at(g + 1))
                        _, _, xh, xl = views(g)
                        for kk in range(2):
                            for j in range(KD):
                                c = slice(kk * D + j * P, kk * D + (j + 1) * P)
                                last = multiply(pe, ps[:, j, 0:T], [((wh[g % 2][:, c], wl[g % 2][:, c]), (xh[:, kk, :], xl[:, kk, :]))],
                                                start=(g == 0 and kk == 0), stop=(g == n - 1 and kk == 1))
                        last.then_inc(prod.sem, 1)
            stage_done(key)

        def wide(key, xh, xl, n_k, T):
            w = plan[key]
            G = HALF // (n_k * P)
            n = 2 * w.n
            with stage() as block:
                @block.sync
                def _(sp):
                    stream(sp, key)

                def granule(g):
                    raw = slot_view((g // 2) % RING, n_k, 2 * G * P)[:, :, (g % 2) * G * P:(g % 2 + 1) * G * P]
                    return raw, lambda v: v[:, :].rearrange("p (k c) -> p k c", k=n_k)

                @block.scalar
                def _(act):
                    for g in range(n):
                        split_high(act, key, g, (g // 2) % RING, g // 2 // RING, *granule(g), g % 2)

                @block.vector
                def _(dve):
                    for g in range(n):
                        split_low(dve, g, *granule(g), g % 2)

                @block.tensor
                def _(pe):
                    for g in range(n):
                        pe.wait_ge(split.sem, split.at(g + 1))
                        _, shaped = granule(g)
                        vh, vl = shaped(wh[g % 2]), shaped(wl[g % 2])
                        for m in range(G):
                            c = slice(m * P, (m + 1) * P)
                            last = multiply(pe, ps[:, g * G + m, 0:T], [((vh[:, kk, c], vl[:, kk, c]), (xh[:, kk, 0:T], xl[:, kk, 0:T]))
                                                                         for kk in range(n_k)])
                        last.then_inc(prod.sem, 1)
            stage_done(key)

        def listed(key, spans, items):
            w = plan[key]
            widths = [sum(n for _, n in span) for span in spans]
            gran = [(i, q) for i in range(w.n) for q in range(w.count[i])]
            of_item = [gran.index((i, c0 // 256)) for i, c0, *_ in items]
            assert of_item == sorted(of_item)

            def granule(g):
                i, q = gran[g]
                n = min(256, widths[i] - 256 * q)
                raw = slot_view(i % RING, KD, widths[i])[:, :, 256 * q:256 * q + n]
                return raw, lambda v: v[:, 0:KD * n].rearrange("p (k c) -> p k c", k=KD)

            def steps(split_granule, take_items):
                for g in range(min(2, len(gran))):
                    split_granule(g)
                for g in range(len(gran)):
                    if g + 2 < len(gran):
                        split_granule(g + 2)
                    take_items(g)

            with stage() as block:
                @block.sync
                def _(sp):
                    stream(sp, key)

                @block.tensor
                def _(pe):
                    for g in range(len(gran)):
                        pe.wait_ge(split.sem, split.at(g + 1))
                        _, shaped = granule(g)
                        for n, (_, _, products, _) in enumerate(items):
                            if of_item[n] != g:
                                continue
                            free = (act_free, dve_free)[n % 2]
                            if n >= 8:
                                pe.wait_ge(free.sem, free.at(n // 2 - 3))
                            for to, terms in products(shaped(wh[g % 2]), shaped(wl[g % 2]), ps[:, n % 8, :]):
                                last = multiply(pe, to, terms)
                        last.then_inc(prod.sem, 1)

                def take(eng, odd, free, g):
                    for n, (_, _, _, taken) in enumerate(items):
                        if of_item[n] == g and n % 2 == odd:
                            eng.wait_ge(prod.sem, prod.at(g + 1))
                            to, of, scale = taken(ps[:, n % 8, :])
                            if odd:
                                eng.tensor_scalar(to, of, scale, None, ALU.mult).then_inc(free.sem, 1)
                            else:
                                eng.activation(to, of, ACT.Copy, scale=scale).then_inc(free.sem, 1)

                @block.scalar
                def _(act):
                    def split_one(g):
                        i = gran[g][0]
                        tile_loaded(act, key, i // RING, i % RING)
                        if g >= 2:
                            act.wait_ge(prod.sem, prod.at(g - 1))
                        raw, shaped = granule(g)
                        act.activation(shaped(wh[g % 2]), raw, ACT.Copy).then_inc(high.sem, 1)
                    steps(split_one, lambda g: take(act, 0, act_free, g))

                @block.vector
                def _(dve):
                    steps(lambda g: split_low(dve, g, *granule(g), g % 2), lambda g: take(dve, 1, dve_free, g))
            stage_done(key)
            act_free.passed((len(items) + 1) // 2)
            dve_free.passed(len(items) // 2)

        def chunk_item(tile, m, t0, t1, to, scale=1.0):
            def products(vh, vl, bank):
                c = slice((m % 2) * P, (m % 2 + 1) * P)
                return [(bank[:, 0:t1 - t0], [((vh[:, kk, c], vl[:, kk, c]), (uh[:, kk, t0:t1], ul[:, kk, t0:t1])) for kk in range(KD)])]
            return tile, m * P, products, lambda bank: (to, bank[:, 0:t1 - t0], scale)

        def token_item(tile, c0, n, tiles, to, scale=1.0):
            def products(vh, vl, bank):
                c = slice(c0 % 256, c0 % 256 + n)
                return [(bank[:, q * n:(q + 1) * n], [((uh[:, kk, t * P:(t + 1) * P], ul[:, kk, t * P:(t + 1) * P]),
                                                       (vh[:, kk, c], vl[:, kk, c])) for kk in range(KD)]) for q, t in enumerate(tiles)]
            return tile, c0, products, lambda bank: (to, bank[:, 0:n * len(tiles)].rearrange("p (t n) -> p t n", n=n)
                                                     if len(tiles) > 1 else bank[:, 0:n], scale)

        AM = Arena()
        qa = AM.take(3, T2)
        ka = AM.take(2, T2)
        qb = AM.take(3, T2)
        kb = AM.take(3, T2)
        va = AM.take(2 * ST, P)
        vb = AM.take(2 * ST, B_HEADS * HD)
        cx = AM.take(2, T2)
        cb = AM.take(2, T2)
        cc = AM.take(2, T2)
        SC = AM
        scores = SC.take(2, T2)
        probs = SC.take(2, T2)
        probs_t = SC.take(2, T2)
        conv_t = SC.take(2, T2)
        RB = Arena(MID.at)
        bands = RB.take(B_HEADS, ST * S)
        flip = RB.take(P)
        zero_rows = RB.take(B_HEADS * RPB_H * RPB_PAD // P + 1)
        assert RB.at <= ARENA - B_HEADS * ST * S and AM.at <= ARENA - B_HEADS * ST * S
        bias = Arena(ARENA - B_HEADS * ST * S).take(B_HEADS, ST, S)
        softs = sb("softs", [P, 8])

        def load_bands(pool, l):
            n = B_HEADS * RPB_H
            padded = a["padded"]
            pool.dma_start(flip, a["const"][:, CONST_W:CONST_W + P]).then_inc(flip_load.sem, 16)
            pool.memset(zero_rows, 0.0).then_inc(pool_step.sem, 1)
            pool.wait_ge(pool_step.sem, pool_step.at(1))
            pool.dma_start(padded, zero_rows).then_inc(band_load.sem, 16)
            pool.wait_ge(band_load.sem, band_load.at(16))
            middle = bass.AP(padded.tensor, GRID_W - WIN_C, [[RPB_PAD, n], [1, RPB_W]])
            pool.dma_start(middle, a["rpb"][l].rearrange("h r c -> (h r) c")).then_inc(band_load.sem, 16)
            pool.wait_ge(band_load.sem, band_load.at(32))
            for hh in range(B_HEADS):
                for r in range(ROWS):
                    at = (hh * RPB_H + WIN_R - 1 - r) * RPB_PAD
                    band = bass.AP(padded.tensor, at, [[1, GRID_W], [RPB_PAD, ROWS], [1, GRID_W]])
                    p0 = (r % 2) * GRID_W
                    to = bands[p0:p0 + GRID_W, hh, (r // 2) * S:(r // 2 + 1) * S].rearrange("p (r c) -> p r c", r=ROWS)
                    pool.dma_start(to, band).then_inc(band_load.sem, 16)
            pool.wait_ge(flip_load.sem, flip_load.at(16))
            pool.wait_ge(band_load.sem, band_load.at(16 * (2 + B_HEADS * ROWS)))

        def rel_bias():
            with stage() as block:
                @block.tensor
                def _(pe):
                    for hh in range(B_HEADS):
                        pe.matmul(ps[:, hh, :], flip, bands[:, hh, :], start=True, stop=True).then_inc(pe_step.sem, 1)

                @block.vector
                def _(dve):
                    for hh in range(B_HEADS):
                        dve.wait_ge(pe_step.sem, pe_step.at(hh + 1))
                        dve.tensor_tensor(bias[:, hh], ps[:, hh, :].rearrange("p (t k) -> p t k", t=ST),
                                          window.unsqueeze(1).broadcast_to([P, ST, S]), ALU.add)
            pe_step.passed(B_HEADS)

        def project(l):
            key = ("in", l)
            last = l == DEPTH - 1
            T = S if last else T2
            items = []
            for m in range(3):
                items.append(chunk_item(0, m, 0, T, qa[:, m, 0:T]))
            for m in range(3):
                items.append(chunk_item(1, m, 0, T, qb[:, m, 0:T]))
            items.append(chunk_item(2, 0, 0, T2, ka[:, 0, :]))
            items.append(token_item(2, P, P, range(2 * ST), va))
            for m in range(3):
                items.append(chunk_item(3, m, 0, T2, kb[:, m, :]))
            for c0, n in ((0, 256), (256, 128)):
                for t in range(0, 2 * ST, 512 // n):
                    k = 512 // n
                    items.append(token_item(4, c0, n, range(t, t + k), vb[:, t:t + k, c0:c0 + n]))
            for m, to in enumerate((cx[:, 0], cx[:, 1], cb[:, 0], cb[:, 1])):
                items.append(chunk_item(5, m, 0, T, to[:, 0:T]))
            for m in range(2):
                items.append(chunk_item(6, m, 0, T, cc[:, m, 0:T]))
            listed(key, IN_SPANS, items)

        def qk_norm(l):
            T = [S if l == DEPTH - 1 else T2] * 3 + [T2]
            xs = [qa[:, 0], qa[:, 1], qa[:, 2], ka[:, 0]]
            with stage() as block:
                @block.scalar
                def _(act):
                    for i in range(4):
                        act.activation(probs_t[:, i % 2, 0:T[i]] if i < 2 else scores[:, i % 2, 0:T[i]], xs[i][:, 0:T[i]],
                                       ACT.Square).then_inc(act_step.sem, 1)
                    for i in range(4):
                        act.wait_ge(pe_step.sem, pe_step.at(i + 1))
                        r = (probs if i < 2 else conv_t)[:, i % 2, 0:T[i]]
                        act_chain.link(act, act.activation(r, ps[:, i, 0:T[i]], ACT.Ln, scale=1.0 / HD, bias=eps[:, 0:1]))
                        act.activation(r, r, ACT.Exp, scale=-0.5).then_inc(act_step.sem, 1)
                    act.wait_ge(pe_step.sem, pe_step.at(9))
                    act.activation(ka[:, 1, :], ps[:, 0, :], ACT.Copy)

                @block.tensor
                def _(pe):
                    for i in range(4):
                        pe.wait_ge(act_step.sem, act_step.at(i + 1))
                        sq = (probs_t if i < 2 else scores)[:, i % 2, 0:T[i]]
                        pe.matmul(ps[:, i, 0:T[i]], mat("half_ones"), sq, start=True, stop=True).then_inc(pe_step.sem, 1)
                    for i in range(4):
                        pe.wait_ge(dve_step.sem, dve_step.at(i + 1))
                        pe.matmul(ps[:, 4 + i, 0:S], mat("rot"), xs[i][:, 0:S], start=True, stop=True).then_inc(pe_step.sem, 1)
                    pe.wait_ge(dve_step.sem, dve_step.at(16))
                    pe.matmul(ps[:, 0, :], mat("swap"), ka[:, 0, :], start=True, stop=True).then_inc(pe_step.sem, 1)

                @block.vector
                def _(dve):
                    for i in range(4):
                        dve.wait_ge(act_step.sem, act_step.at(5 + i))
                        r = (probs if i < 2 else conv_t)[:, i % 2, 0:T[i]]
                        gain = head_gain[:, 2 * l + (i == 3):2 * l + (i == 3) + 1]
                        dve.scalar_tensor_tensor(out=xs[i][:, 0:T[i]], in0=xs[i][:, 0:T[i]], scalar=gain, in1=r,
                                                 op0=ALU.mult, op1=ALU.mult).then_inc(dve_step.sem, 1)
                    for i in range(4):
                        dve.wait_ge(pe_step.sem, pe_step.at(5 + i))
                        turned = scores[:, i % 2, 0:S]
                        if i >= 1:
                            dve.wait_ge(dve_step.sem, dve_step.at(4 + 3 * i))
                        dve.tensor_tensor(turned, ps[:, 4 + i, 0:S], sin_t, ALU.mult).then_inc(dve_step.sem, 1)
                        dve.tensor_tensor(xs[i][:, 0:S], xs[i][:, 0:S], cos_t, ALU.mult).then_inc(dve_step.sem, 1)
                        dve.wait_ge(dve_step.sem, dve_step.at(4 + 3 * i + 2))
                        dve.tensor_tensor(xs[i][:, 0:S], xs[i][:, 0:S], turned, ALU.add).then_inc(dve_step.sem, 1)
            act_step.passed(8)
            pe_step.passed(9)
            dve_step.passed(16)

        def attention(l):
            last = l == DEPTH - 1
            units = []
            for hd in range(A_HEADS):
                b = HD * (hd % 2)
                kv = hd // (A_HEADS // A_KV)
                kt = ka[b:b + HD, 0 if kv == hd % 2 else 1, :]
                v = lambda t, kv=kv: va[:, t, kv * HD:(kv + 1) * HD]
                for t in range(ST):
                    units.append((qa[b:b + HD, hd // 2, t * P:(t + 1) * P], kt, 0, T2, None, v, hd // 2, b, t))
                    if not last:
                        tc = ST + t
                        units.append((qa[b:b + HD, hd // 2, tc * P:(tc + 1) * P], kt, S, T2, None, v, hd // 2, b, tc))
            for hd in range(B_HEADS):
                b = HD * (hd % 2)
                kt = kb[b:b + HD, hd // 2, :]
                v = lambda t, hd=hd: vb[:, t, hd * HD:(hd + 1) * HD]
                for t in range(ST):
                    units.append((qb[b:b + HD, hd // 2, t * P:(t + 1) * P], kt, 0, T2, bias[:, hd, t, :], v, 3 + hd // 2, b, t))
                    if not last:
                        tc = ST + t
                        units.append((qb[b:b + HD, hd // 2, tc * P:(tc + 1) * P], kt, S, T2, None, v, 3 + hd // 2, b, tc))
            n = len(units)
            scale = HD ** -0.5
            scored, softened, normed, turned_, moved, valued, taken, maxed = (
                pe_step, act_step, dve_step, prod, act_free, gate_done, dve_free, aux)
            with stage() as block:
                @block.tensor
                def _(pe):
                    for i in range(n + 2):
                        if i < n:
                            q, kt, k0, k1, bm, v, oc, b, t = units[i]
                            if i >= 2:
                                pe.wait_ge(softened.sem, softened.at(i - 1))
                            pe.matmul(ps[:, i % 2, 0:k1 - k0], q, kt[:, k0:k1], start=True, stop=True).then_inc(scored.sem, 1)
                        if 1 <= i <= n:
                            j = i - 1
                            _, _, k0, k1, *_ = units[j]
                            pe.wait_ge(normed.sem, normed.at(j + 1))
                            if j >= 2:
                                pe.wait_ge(moved.sem, moved.at(j - 1))
                            for m in range((k1 - k0) // P):
                                tr = pe.transpose(ps[:, 2 + j % 2, m * P:(m + 1) * P], probs[:, j % 2, m * P:(m + 1) * P], ident)
                            tr.then_inc(turned_.sem, 1)
                        if i >= 2:
                            j = i - 2
                            _, _, k0, k1, _, v, oc, b, t = units[j]
                            pe.wait_ge(moved.sem, moved.at(j + 1))
                            if j >= 2:
                                pe.wait_ge(taken.sem, taken.at(j - 1))
                            m_n = (k1 - k0) // P
                            for m in range(m_n):
                                mm = pe.matmul(ps[b:b + HD, 4 + j % 2, 0:P], v(k0 // P + m), probs_t[:, j % 2, m * P:(m + 1) * P],
                                               start=(m == 0), stop=(m == m_n - 1))
                            mm.then_inc(valued.sem, 1)

                @block.scalar
                def _(act):
                    for i in range(n + 1):
                        if i < n:
                            _, _, k0, k1, bm, *_ = units[i]
                            act.wait_ge(maxed.sem, maxed.at(i + 1))
                            if i >= 2:
                                act.wait_ge(turned_.sem, turned_.at(i - 1))
                            of = scores[:, i % 2, 0:k1 - k0] if bm is not None else ps[:, i % 2, 0:k1 - k0]
                            act.activation(probs[:, i % 2, 0:k1 - k0], of, ACT.Exp, bias=softs[:, i % 2:i % 2 + 1],
                                           scale=1.0 if bm is not None else scale,
                                           accum_out=softs[:, 2 + i % 2:3 + i % 2]).then_inc(softened.sem, 1)
                        if i >= 1:
                            j = i - 1
                            _, _, k0, k1, *_ = units[j]
                            act.wait_ge(turned_.sem, turned_.at(j + 1))
                            if j >= 2:
                                act.wait_ge(valued.sem, valued.at(j - 1))
                            act.activation(probs_t[:, j % 2, 0:k1 - k0], ps[:, 2 + j % 2, 0:k1 - k0], ACT.Copy).then_inc(moved.sem, 1)

                @block.vector
                def _(dve):
                    for i in range(n + 3):
                        if i < n:
                            _, _, k0, k1, bm, *_ = units[i]
                            N = k1 - k0
                            dve.wait_ge(scored.sem, scored.at(i + 1))
                            if i >= 2:
                                dve.wait_ge(softened.sem, softened.at(i - 1))
                            if bm is not None:
                                sc = scores[:, i % 2, 0:N]
                                dve.scalar_tensor_tensor(out=sc[:, 0:S], in0=ps[:, i % 2, 0:S], scalar=scale, in1=bm,
                                                         op0=ALU.mult, op1=ALU.add).then_inc(dve_chain.sem, 1)
                                dve.tensor_scalar(sc[:, S:N], ps[:, i % 2, S:N], scale, None, ALU.mult).then_inc(dve_chain.sem, 1)
                                dve_chain.n += 2
                                dve.wait_ge(dve_chain.sem, dve_chain.n)
                                dve_chain.link(dve, dve.tensor_reduce(softs[:, 4 + i % 2:5 + i % 2], sc, AX_X, ALU.max))
                                dve.tensor_scalar(softs[:, i % 2:i % 2 + 1], softs[:, 4 + i % 2:5 + i % 2], -1.0, None,
                                                  ALU.mult).then_inc(maxed.sem, 1)
                            else:
                                dve_chain.link(dve, dve.tensor_reduce(softs[:, 4 + i % 2:5 + i % 2], ps[:, i % 2, 0:N], AX_X, ALU.max))
                                dve.tensor_scalar(softs[:, i % 2:i % 2 + 1], softs[:, 4 + i % 2:5 + i % 2], -scale, None,
                                                  ALU.mult).then_inc(maxed.sem, 1)
                        if 1 <= i <= n:
                            j = i - 1
                            N = units[j][3] - units[j][2]
                            dve.wait_ge(softened.sem, softened.at(j + 1))
                            if j >= 2:
                                dve.wait_ge(normed.sem, normed.at(j - 1))
                            dve_chain.link(dve, dve.reciprocal(softs[:, 6 + j % 2:7 + j % 2], softs[:, 2 + j % 2:3 + j % 2]))
                            dve.tensor_scalar(probs[:, j % 2, 0:N], probs[:, j % 2, 0:N], softs[:, 6 + j % 2:7 + j % 2], None,
                                              ALU.mult).then_inc(normed.sem, 1)
                        if i >= 3:
                            j = i - 3
                            *_, oc, b, t = units[j]
                            dve.wait_ge(valued.sem, valued.at(j + 1))
                            of = ps[b:b + HD, 4 + j % 2, 0:P]
                            oh, ol = (v[b:b + HD, oc, t * P:(t + 1) * P] for v in (uh, ul))
                            dve_chain.link(dve, dve.tensor_copy(oh, of))
                            dve.tensor_tensor(ol, of, oh, ALU.subtract).then_inc(taken.sem, 1)

                @block.gpsimd
                def _(pool):
                    link = lambda ins: pool_chain.link(pool, ins)
                    T = S if last else T2
                    for j in range(2):
                        tap = lambda w_: col("conv_w", (l * 3 + w_) * 2 + j)
                        z, y, t_ = cx[:, j, 0:T], conv_t[:, 0, 0:T], conv_t[:, 1, 0:T]
                        link(pool.tensor_tensor(z, cc[:, j, 0:T], z, ALU.mult))
                        link(pool.tensor_scalar(y, z, tap(1), None, ALU.mult))
                        link(pool.tensor_scalar(t_, z, tap(0), None, ALU.mult))
                        for s in range(T // S):
                            link(pool.tensor_tensor(y[:, s * S + 1:(s + 1) * S], y[:, s * S + 1:(s + 1) * S],
                                                    t_[:, s * S:(s + 1) * S - 1], ALU.add))
                        link(pool.tensor_scalar(t_, z, tap(2), None, ALU.mult))
                        for s in range(T // S):
                            link(pool.tensor_tensor(y[:, s * S:(s + 1) * S - 1], y[:, s * S:(s + 1) * S - 1],
                                                    t_[:, s * S + 1:(s + 1) * S], ALU.add))
                        link(pool.tensor_tensor(y, y, cb[:, j, 0:T], ALU.mult))
                        link(pool.tensor_copy(uh[:, 6 + j, 0:T], y))
                        link(pool.tensor_tensor(ul[:, 6 + j, 0:T], y, uh[:, 6 + j, 0:T], ALU.subtract))
            for s_ in (scored, softened, normed, turned_, moved, valued, taken, maxed):
                s_.passed(n)

        def finish():
            tokens = Arena().take(ST, D)
            with stage() as block:
                @block.tensor
                def _(pe):
                    for t in range(ST):
                        for half in range(2):
                            g = 2 * t + half
                            for m in range(4):
                                tr = pe.transpose(ps[:, g, m * P:(m + 1) * P], h[:, 4 * half + m, t * P:(t + 1) * P], ident)
                            tr.then_inc(pe_step.sem, 1)

                @block.vector
                def _(dve):
                    for g in range(2 * ST):
                        dve.wait_ge(pe_step.sem, pe_step.at(g + 1))
                        dve.tensor_copy(tokens[:, g // 2, (g % 2) * 512:(g % 2 + 1) * 512], ps[:, g, :]).then_inc(dve_step.sem, 1)

                @block.sync
                def _(sp):
                    for t in range(ST):
                        sp.wait_ge(dve_step.sem, dve_step.at(2 * t + 2))
                        sp.dma_start(out[0, t * P:(t + 1) * P, :], tokens[:, t, :]).then_inc(stored.sem, 16)
                    sp.wait_ge(stored.sem, stored.at(16 * ST))

        def pre2(i, which):
            mem = Arena()
            sq = mem.take(KD, S)
            x = mem.take(KD, S)
            with stage() as block:
                @block.scalar
                def _(act):
                    for k in range(KD):
                        act.activation(sq[:, k, :], h[:, k, 0:S], ACT.Square).then_inc(act_step.sem, 1)
                    act.wait_ge(pe_step.sem, pe_step.at(1))
                    act_chain.link(act, act.activation(rstd[:, 0:S], ps[:, 0, 0:S], ACT.Ln, scale=1.0 / D, bias=eps[:, 0:1]))
                    act.activation(rstd[:, 0:S], rstd[:, 0:S], ACT.Exp, scale=-0.5).then_inc(act_step.sem, 1)
                    for k in range(0, KD, 2):
                        act.wait_ge(dve_step.sem, dve_step.at(k + 2))
                        act.activation(uh[:, k:k + 2, 0:S], x[:, k:k + 2, :], ACT.Copy).then_inc(act_step.sem, 1)

                @block.tensor
                def _(pe):
                    for k in range(KD):
                        pe.wait_ge(act_step.sem, act_step.at(k + 1))
                        last = pe.matmul(ps[:, 0, 0:S], ones, sq[:, k, :], start=(k == 0), stop=(k == KD - 1))
                    last.then_inc(pe_step.sem, 1)

                @block.vector
                def _(dve):
                    dve.wait_ge(act_step.sem, act_step.at(KD + 1))
                    for k in range(0, KD + 4, 2):
                        if k < KD:
                            for m in (k, k + 1):
                                dve.scalar_tensor_tensor(out=x[:, m, :], in0=h[:, m, 0:S], scalar=col("norm_g_2", (i * 4 + which) * KD + m),
                                                         in1=rstd[:, 0:S], op0=ALU.mult, op1=ALU.mult).then_inc(dve_step.sem, 1)
                        if k >= 4:
                            m = k - 4
                            dve.wait_ge(act_step.sem, act_step.at(KD + 2 + m // 2))
                            dve.tensor_tensor(ul[:, m:m + 2, 0:S], x[:, m:m + 2, :], uh[:, m:m + 2, 0:S], ALU.subtract)
            act_step.passed(KD + 1 + KD // 2)
            pe_step.passed(1)
            dve_step.passed(KD)

        def post2(i, which):
            post(lambda k, s: col("norm_g_2", (i * 4 + which) * KD + k), S)

        CF = Arena()
        mid2 = CF.take(KF, S)
        conv_buf = CF.take(4, 2, S)

        def ffn_up2(i):
            key = ("up2", i)
            n_ch = 2 * KF
            with stage() as block:
                @block.sync
                def _(sp):
                    stream(sp, key)

                @block.tensor
                def _(pe):
                    pair_products(pe, key, S, dve_step)

                def channel(name, tap, part, g):
                    at = col_at[name] + (i * (3 if name == "ffn_conv_w" else 1) + tap) * n_ch + part * KF
                    return cols[:, ds(g + at, 1)]

                @block.scalar
                def _(act):
                    high_of = split_pairs(key, act=act)

                    def granule(turn, q, more):
                        g = turn * 4 + q
                        if more:
                            high_of(*ahead(turn, q))
                        act.wait_ge(prod.sem, prod.at(g + 1))
                        act.wait_ge(dve_free.sem, dve_free.at(g - 3))
                        for part in range(2):
                            act.activation(conv_buf[:, q, part, :], ps[:, 2 * q + part, 0:S], ACT.Identity,
                                           bias=channel("ffn_conv_b", 0, part, g),
                                           scale=channel("ffn_conv_w", 1, part, g)).then_inc(gate_done.sem, 1)
                        act.wait_ge(dve_step.sem, dve_step.at(g + 1))
                        act.activation(conv_buf[:, q, 0, :], conv_buf[:, q, 0, :], ACT.Gelu_apprx_tanh).then_inc(gate_done.sem, 1)
                    high_of(0, 0)
                    high_of(0, 1)
                    with_lead(act, KF, 2, granule)

                @block.vector
                def _(dve):
                    low_of = split_pairs(key, dve=dve)

                    def granule(turn, q, more):
                        g = turn * 4 + q
                        if more:
                            low_of(*ahead(turn, q))
                        dve.wait_ge(gate_done.sem, gate_done.at(g * 3 + 2))
                        for tap, to, of in ((0, slice(1, S), slice(0, S - 1)), (2, slice(0, S - 1), slice(1, S))):
                            for part in range(2):
                                if tap == 2:
                                    dve.wait_ge(aux.sem, aux.at(g * 3 + 1 + part))
                                ins = dve.scalar_tensor_tensor(out=conv_buf[:, q, part, to], in0=ps[:, 2 * q + part, of],
                                                               scalar=channel("ffn_conv_w", tap, part, g),
                                                               in1=conv_buf[:, q, part, to], op0=ALU.mult, op1=ALU.add)
                                ins.then_inc(dve_step.sem if tap == 2 and part == 1 else aux.sem, 1)
                        dve.wait_ge(gate_done.sem, gate_done.at(g * 3 + 3))
                        dve.wait_ge(dve_step.sem, dve_step.at(g + 1))
                        dve.tensor_tensor(mid2[:, ds(g, 1), :].squeeze(1), conv_buf[:, q, 0, :], conv_buf[:, q, 1, :],
                                          ALU.mult).then_inc(dve_free.sem, 1)
                    low_of(0, 0)
                    low_of(0, 1)
                    with_lead(dve, KF, 2, granule)
            stage_done(key)
            n = KF
            dve_free.passed(n)
            dve_step.passed(n)
            gate_done.passed(3 * n)
            aux.passed(3 * n)

        def head_norm(base, n, per, gain, scratch, before=None, after=None):
            groups = n // per
            mem = Arena(scratch)
            sq = mem.take(n, S)
            rs = mem.take(groups, S)
            x = u32[:, base:base + n, :]
            xh, xl = (v[:, :, :].rearrange("p a b -> p (a b)").rearrange("p (a b) -> p a b", b=S)[:, base:base + n, :] for v in (uh, ul))
            with stage() as block:
                @block.scalar
                def _(act):
                    for of in (before, after):
                        if of is not None:
                            act.activation(of[1], of[1], of[0]).then_inc(gate_done.sem, 1)
                    for k in range(n):
                        if before is not None:
                            act.wait_ge(dve_step.sem, dve_step.at(k + 1))
                        act.activation(sq[:, k, :], x[:, k, :], ACT.Square).then_inc(act_step.sem, 1)
                    for g in range(groups):
                        act.wait_ge(pe_step.sem, pe_step.at(g + 1))
                        act_chain.link(act, act.activation(rs[:, g, :], ps[:, g, 0:S], ACT.Ln, scale=1.0 / (per * P), bias=eps[:, 0:1]))
                        act.activation(rs[:, g, :], rs[:, g, :], ACT.Exp, scale=-0.5).then_inc(act_step.sem, 1)
                    for k in range(n):
                        act.wait_ge(aux.sem, aux.at(k + 1))
                        act.activation(xh[:, k, :], sq[:, k, :], ACT.Copy).then_inc(act_step.sem, 1)

                @block.tensor
                def _(pe):
                    for k in range(n):
                        pe.wait_ge(act_step.sem, act_step.at(k + 1))
                        last = pe.matmul(ps[:, k // per, 0:S], ones, sq[:, k, :], start=(k % per == 0), stop=(k % per == per - 1))
                        if k % per == per - 1:
                            last.then_inc(pe_step.sem, 1)

                @block.vector
                def _(dve):
                    if before is not None:
                        dve.wait_ge(gate_done.sem, gate_done.at(1))
                        for k in range(n):
                            dve.tensor_tensor(x[:, k, :], x[:, k, :], before[1][:, k, :], ALU.mult).then_inc(dve_step.sem, 1)
                        dve.wait_ge(dve_step.sem, dve_step.at(n))
                    for k in range(n + 2):
                        if k < n:
                            dve.wait_ge(act_step.sem, act_step.at(n + k // per + 1))
                            ins = dve.scalar_tensor_tensor(out=sq[:, k, :], in0=x[:, k, :], scalar=col(gain, k), in1=rs[:, k // per, :],
                                                           op0=ALU.mult, op1=ALU.mult)
                            if after is not None:
                                dve_chain.link(dve, ins)
                                ins = dve.tensor_tensor(sq[:, k, :], sq[:, k, :], after[1][:, k, :], ALU.mult)
                            ins.then_inc(aux.sem, 1)
                        if k >= 2:
                            dve.wait_ge(act_step.sem, act_step.at(n + groups + k - 1))
                            dve.tensor_tensor(xl[:, k - 2, :], sq[:, k - 2, :], xh[:, k - 2, :], ALU.subtract)
            gate_done.passed((before is not None) + (after is not None))
            act_step.passed(2 * n + groups)
            pe_step.passed(groups)
            dve_step.passed(n * (before is not None))
            aux.passed(n)

        BM = Arena()
        z = h[:, :, S:T2]
        xbc = BM.take(12, S)
        mq = BM.take(ML_HEADS, S)
        mk = BM.take(ML_HEADS, S)
        mv = BM.take(ST, D)
        o_pre = BM.take(KD, S)
        gate_x = BM.take(ST, 64)
        soft = BM.take(ST, 64)
        dt = BM.take(ST, 32)
        dta = BM.take(ST, 32)
        ncs = BM.take(2, ST, SSD_HEADS)
        w_end = BM.take(2, SSD_HEADS)
        bcol = BM.take(6, ML_HEADS)
        HN_AT = BM.at
        SS = Arena(BM.at)
        xdt = ul32[:, :].rearrange("p (a b) -> p a b", b=D).rearrange("p (a b) c -> p a b c", a=2)
        xs_tok = SS.take(ST, D)
        b_tok = SS.take(ST, 2 * P)
        x_end = SS.take(2, D)
        state = SS.take(2, D)
        xbc_raw = Arena(BM.at).take(12, S)
        decays = x_end.rearrange("p a b -> p (a b)").rearrange("p (a b c) -> p a b c", a=2, b=8)
        cbt = xs_tok[:, 0, 0:512]
        carry = xs_tok[:, 1, :].rearrange("p (a b) -> p a b", a=2)
        FIRST = (0, ST - 1)
        tri = (mat("upto"), mat("from_"))
        tri_mask = (mat("mask_upto"), mat("mask_from"))
        mixed = u32

        def ab_project():
            items = []
            for m in range(20):
                to = z[:, m, :] if m < 8 else xbc_raw[:, m - 8, :]
                items.append(chunk_item(m // 4, m % 4, 0, S, to))
            for m in range(8):
                items.append(chunk_item(5 + m // 4, m % 4, 0, S, mq[:, m, :]))
            for m in range(8):
                items.append(chunk_item(7 + m // 4, m % 4, 0, S, mk[:, m, :], scale=(D // ML_HEADS) ** -0.5))
            for q in range(4):
                items.append(token_item(9 + q // 2, (q % 2) * 256, 256, range(ST), mv[:, :, q * 256:(q + 1) * 256]))
            for m in range(8):
                items.append(chunk_item(11 + m // 4, m % 4, 0, S, o_pre[:, m, :]))
            items.append(token_item(13, 0, 64, range(ST), gate_x))
            listed("ab_in", AB_SPANS, items)

        def ssd_conv():
            half = SSD_CONV // 2
            with stage() as block:
                @block.vector
                def _(dve):
                    link = lambda ins: dve_chain.link(dve, ins)
                    dve.tensor_tensor(gate_x, gate_x, gate_bias[:, :].unsqueeze(1).broadcast_to([P, ST, 64]), ALU.add).then_inc(dve_step.sem, 1)
                    taps = [2, 0, 1, 3, 4]
                    for j in range(12):
                        w_ = lambda tap: col("ab_conv_w", tap * 12 + j)
                        x_, y_ = xbc_raw[:, j, :], xbc[:, j, :]
                        for tap in taps:
                            s = tap - half
                            if s == 0:
                                ins = dve.tensor_scalar(y_, x_, w_(tap), col("ab_conv_b", j), ALU.mult, ALU.add)
                            else:
                                to = slice(max(0, -s), S - max(0, s))
                                of = slice(max(0, s), S - max(0, -s))
                                ins = dve.scalar_tensor_tensor(out=y_[:, to], in0=x_[:, of], scalar=w_(tap), in1=y_[:, to],
                                                               op0=ALU.mult, op1=ALU.add)
                            if tap != taps[-1]:
                                link(ins)
                        ins.then_inc(dve_step.sem, 1)
                    dve.wait_ge(act_step.sem, act_step.at(2))
                    link(dve.scalar_tensor_tensor(out=dt[:, :, :], in0=gate_x[:, :, 0:32], scalar=0.0, in1=soft[:, :, 0:32],
                                                  op0=ALU.max, op1=ALU.add))
                    link(dve.scalar_tensor_tensor(out=dta[:, :, :], in0=dt[:, :, :], scalar=-1.0,
                                                  in1=a_log[:, :].unsqueeze(1).broadcast_to([P, ST, 32]), op0=ALU.mult, op1=ALU.mult))
                    link(dve.scalar_tensor_tensor(out=gate_x[:, :, 48:64], in0=gate_x[:, :, 48:64], scalar=0.0,
                                                  in1=soft[:, :, 48:64], op0=ALU.min, op1=ALU.subtract))

                @block.scalar
                def _(act):
                    link = lambda ins: act_chain.link(act, ins)
                    act.activation(a_log[:, :], a_log[:, :], ACT.Exp).then_inc(act_step.sem, 1)
                    act.wait_ge(dve_step.sem, dve_step.at(1))
                    link(act.activation(soft, gate_x, ACT.Abs))
                    link(act.activation(soft, soft, ACT.Exp, scale=-1.0))
                    act.activation(soft, soft, ACT.Ln, bias=ones[:, 0:1]).then_inc(act_step.sem, 1)
                    for j in range(12):
                        act.wait_ge(dve_step.sem, dve_step.at(j + 2))
                        act.activation(xbc[:, j, :], xbc[:, j, :], ACT.Silu)
            act_step.passed(2)
            dve_step.passed(13)

        def ssd_prepare():
            with stage() as block:
                @block.tensor
                def _(pe):
                    for t in range(ST):
                        for q in range(2):
                            for m in range(4):
                                tr = pe.transpose(ps[:, 2 * t + q, m * P:(m + 1) * P], xbc[:, 4 * q + m, t * P:(t + 1) * P], ident)
                            tr.then_inc(pe_step.sem, 1)
                    for t in range(ST):
                        for g in range(2):
                            tr = pe.transpose(ps[:, 4, (2 * t + g) * P:(2 * t + g + 1) * P], xbc[:, 8 + g, t * P:(t + 1) * P], ident)
                    tr.then_inc(pe_step.sem, 1)
                    for d in range(2):
                        for t in range(ST):
                            o = (d * ST + t) * SSD_HEADS
                            pe.matmul(ps[:, 5, o:o + SSD_HEADS], tri[d], dta[:, t, d * SSD_HEADS:(d + 1) * SSD_HEADS], start=True, stop=True)
                    for t in range(ST):
                        mm = pe.matmul(ps[:, 5, 64 + t * 32:96 + t * 32], ones, dta[:, t, :], start=True, stop=True)
                    mm.then_inc(pe_step.sem, 1)
                    for t in range(ST):
                        for g in range(SSD_GROUPS):
                            o = (t * SSD_GROUPS + g) * P
                            mm = pe.matmul(ps[:, 6, o:o + P], xbc[:, 8 + g, t * P:(t + 1) * P], xbc[:, 10 + g, t * P:(t + 1) * P],
                                           start=True, stop=True)
                    mm.then_inc(pe_step.sem, 1)
                    pe.wait_ge(dve_step.sem, dve_step.at(10))
                    for d in range(2):
                        for g in range(SSD_GROUPS):
                            pe.matmul(ps[:, 2 * d + g, :], b_tok[:, FIRST[d], g * P:(g + 1) * P],
                                      x_end[:, d, g * 512:(g + 1) * 512], start=True, stop=True).then_inc(pe_step.sem, 1)

                @block.scalar
                def _(act):
                    for n in range(4):
                        act.wait_ge(pe_step.sem, pe_step.at(n + 1))
                        act.activation(xs_tok[:, n // 2, (n % 2) * 512:(n % 2 + 1) * 512], ps[:, n, :], ACT.Copy).then_inc(act_step.sem, 1)
                    act.wait_ge(pe_step.sem, pe_step.at(5))
                    act.activation(b_tok.rearrange("p a b -> p (a b)"), ps[:, 4, :], ACT.Copy).then_inc(act_step.sem, 1)
                    act.wait_ge(dve_step.sem, dve_step.at(3))
                    act.activation(w_end[:, :, :], w_end[:, :, :], ACT.Exp).then_inc(act_step.sem, 1)
                    for n in range(4):
                        act.wait_ge(pe_step.sem, pe_step.at(8 + n))
                        act.activation(state[:, n // 2, (n % 2) * 512:(n % 2 + 1) * 512], ps[:, n, :], ACT.Copy).then_inc(act_step.sem, 1)

                @block.vector
                def _(dve):
                    dve.wait_ge(pe_step.sem, pe_step.at(6))
                    dve.tensor_scalar(ncs.rearrange("p d t h -> p (d t h)"), ps[:, 5, 0:64], -1.0, None, ALU.mult).then_inc(dve_step.sem, 1)
                    dve.wait_ge(dve_step.sem, dve_step.at(1))
                    for d in range(2):
                        t = FIRST[d]
                        o = 64 + t * 32 + d * SSD_HEADS
                        dve.tensor_tensor(w_end[:, d, :], ps[:, 5, o:o + SSD_HEADS], ncs[:, d, t, :], ALU.add).then_inc(dve_step.sem, 1)
                    dve.wait_ge(act_step.sem, act_step.at(4))
                    for d in range(2):
                        for t in range(ST):
                            dve.tensor_tensor(xdt[:, d, t, :].rearrange("p (h e) -> p h e", e=HD),
                                              xs_tok[:, t, :].rearrange("p (h e) -> p h e", e=HD),
                                              dt[:, t, d * SSD_HEADS:(d + 1) * SSD_HEADS].unsqueeze(2).broadcast_to([P, SSD_HEADS, HD]),
                                              ALU.mult).then_inc(dve_step.sem, 1)
                    dve.wait_ge(act_step.sem, act_step.at(6))
                    dve.wait_ge(dve_step.sem, dve_step.at(7))
                    for d in range(2):
                        dve.tensor_tensor(x_end[:, d, :].rearrange("p (h e) -> p h e", e=HD),
                                          xdt[:, d, FIRST[d], :].rearrange("p (h e) -> p h e", e=HD),
                                          w_end[:, d, :].unsqueeze(2).broadcast_to([P, SSD_HEADS, HD]), ALU.mult).then_inc(dve_step.sem, 1)
                    dve.wait_ge(pe_step.sem, pe_step.at(7))
                    dve.tensor_copy(cbt, ps[:, 6, :]).then_inc(dve_step.sem, 1)
            pe_step.passed(11)
            act_step.passed(10)
            dve_step.passed(10)

        def ssd_scan():
            units = [(t, q) for t in range(ST) for q in range(4)]
            n = len(units)
            with stage() as block:
                @block.tensor
                def _(pe):
                    for i in range(n + 1):
                        if i < n:
                            t, q = units[i]
                            into = 1 - t
                            if i >= 2:
                                pe.wait_ge(act_step.sem, act_step.at(i - 1))
                            b0 = 3 * (i % 2)
                            for d in range(2):
                                for m in range(4):
                                    hh = d * SSD_HEADS + 4 * q + m
                                    o = m * P
                                    pe.matmul(ps[:, b0 + d, o:o + P], dta[:, t, hh:hh + 1].broadcast_to([P, P]), tri[d], start=True, stop=False)
                                    pe.matmul(ps[:, b0 + d, o:o + P], ident, tri_mask[d], start=False, stop=True)
                            d = 0 if t == 1 else 1
                            for m in range(4):
                                hh = d * SSD_HEADS + 4 * q + m
                                mm = pe.matmul(ps[:, b0 + 2, m * P:(m + 1) * P], dta[:, t, hh:hh + 1].broadcast_to([P, P]), tri[d],
                                               start=True, stop=True)
                            mm.then_inc(pe_step.sem, 1)
                        if i >= 1:
                            j = i - 1
                            t, q = units[j]
                            d_in = 0 if t == 1 else 1
                            pe.wait_ge(dve_step.sem, dve_step.at(j + 1))
                            if j >= 2:
                                pe.wait_ge(dve_free.sem, dve_free.at(j - 1))
                            for m in range(4):
                                c0 = (4 * q + m) * HD
                                b = HD * (m % 2)
                                to = ps[b:b + HD, 6 + j % 2, (m // 2) * P:(m // 2 + 1) * P]
                                for d in range(2):
                                    pe.matmul(to, xdt[:, d, t, c0:c0 + HD], decays[:, j % 2, 4 * d + m, :], start=(d == 0), stop=False)
                                mm = pe.matmul(to, state[:, d_in, c0:c0 + HD], carry[:, j % 2, m * P:(m + 1) * P], start=False, stop=True)
                            mm.then_inc(gate_done.sem, 1)

                @block.scalar
                def _(act):
                    for i in range(n):
                        t, q = units[i]
                        b0 = 3 * (i % 2)
                        act.wait_ge(pe_step.sem, pe_step.at(i + 1))
                        if i >= 2:
                            act.wait_ge(gate_done.sem, gate_done.at(i - 1))
                        for d in range(2):
                            for m in range(4):
                                hh = 4 * q + m
                                act.activation(decays[:, i % 2, 4 * d + m, :], ps[:, b0 + d, m * P:(m + 1) * P], ACT.Exp,
                                               bias=ncs[:, d, t, hh:hh + 1])
                        act.activation(carry[:, i % 2, :], ps[:, b0 + 2, :], ACT.Exp).then_inc(act_step.sem, 1)

                @block.vector
                def _(dve):
                    for i in range(n + 1):
                        if i < n:
                            t, q = units[i]
                            g = q // 2
                            dve.wait_ge(act_step.sem, act_step.at(i + 1))
                            o = (t * SSD_GROUPS + g) * P
                            dve.tensor_tensor(decays[:, i % 2, :, :], decays[:, i % 2, :, :],
                                              cbt[:, o:o + P].unsqueeze(1).broadcast_to([P, 8, P]), ALU.mult).then_inc(aux.sem, 1)
                            c4 = carry[:, i % 2, :].rearrange("p (m l) -> p m l", m=4)
                            dve.wait_ge(aux.sem, aux.at(i + 1))
                            dve.tensor_tensor(c4, c4, xbc[:, 10 + g, t * P:(t + 1) * P].unsqueeze(1).broadcast_to([P, 4, P]),
                                              ALU.mult).then_inc(dve_step.sem, 1)
                        if i >= 1:
                            j = i - 1
                            t, q = units[j]
                            dve.wait_ge(gate_done.sem, gate_done.at(j + 1))
                            for m in range(2):
                                c = 2 * q + m
                                ins = dve.scalar_tensor_tensor(out=mixed[:, c, t * P:(t + 1) * P], in0=xbc[:, c, t * P:(t + 1) * P],
                                                               scalar=d_skip[:, c:c + 1], in1=ps[:, 6 + j % 2, m * P:(m + 1) * P],
                                                               op0=ALU.mult, op1=ALU.add)
                            ins.then_inc(dve_free.sem, 1)
            pe_step.passed(n)
            act_step.passed(n)
            dve_step.passed(n)
            gate_done.passed(n)
            dve_free.passed(n)
            aux.passed(n)

        MM = Arena(HN_AT)
        k_tok = ul32[:, 0:ST * D].rearrange("p (a b) -> p a b", a=ST)
        IG, LF, FC, BB, MX, NM, FL, SI = [MM.take(2, S) for _ in range(8)]
        kwr = MM.take(2, P)
        wts = MM.take(2, 2, S)
        floors = MM.take(2, S)
        dens = MM.take(2, S)
        nums = MM.take(2, S)
        kws = MM.take(2, P)
        cst = MM.take(2, P)
        qst = MM.take(2, P)
        ml = sb("ml", [P, 8])
        nst = sb("nst", [P, 2])

        def mlstm_prepare():
            H8 = ML_HEADS
            with stage() as block:
                @block.tensor
                def _(pe):
                    for kind, at in ((0, 32), (1, 48)):
                        for d in range(2):
                            for t in range(ST):
                                tr = pe.transpose(ps[0:H8, kind, (d * ST + t) * P:(d * ST + t + 1) * P],
                                                  gate_x[:, t, at + d * H8:at + (d + 1) * H8], ident)
                        tr.then_inc(pe_step.sem, 1)
                    for t in range(ST):
                        for q in range(2):
                            for m in range(4):
                                tr = pe.transpose(ps[:, 2 + 2 * t + q, m * P:(m + 1) * P], mk[:, 4 * q + m, t * P:(t + 1) * P], ident)
                            tr.then_inc(pe_step.sem, 1)
                    pe.wait_ge(dve_step.sem, dve_step.at(1))
                    for d in range(2):
                        for t in range(ST):
                            o = (d * ST + t) * H8
                            pe.transpose(ps[:, 6, o:o + H8], BB[0:H8, d, t * P:(t + 1) * P], ident[0:H8, 0:H8])
                    pe.wait_ge(act_step.sem, act_step.at(7))
                    for d in range(2):
                        tr = pe.transpose(ps[:, 6, (4 + d) * H8:(5 + d) * H8], kwr[0:H8, d, :], ident[0:H8, 0:H8])
                    tr.then_inc(pe_step.sem, 1)

                @block.scalar
                def _(act):
                    act.wait_ge(pe_step.sem, pe_step.at(1))
                    act.activation(IG[0:H8].rearrange("p a b -> p (a b)"), ps[0:H8, 0, :], ACT.Copy).then_inc(act_step.sem, 1)
                    for n in range(4):
                        act.wait_ge(pe_step.sem, pe_step.at(3 + n))
                        act.activation(k_tok[:, n // 2, (n % 2) * 512:(n % 2 + 1) * 512], ps[:, 2 + n, :], ACT.Copy).then_inc(act_step.sem, 1)
                    act.wait_ge(dve_step.sem, dve_step.at(2))
                    for d in range(2):
                        t = FIRST[d]
                        act.activation(kwr[0:H8, d, :], BB[0:H8, d, t * P:(t + 1) * P], ACT.Exp, bias=ml[0:H8, 2 + d:3 + d]).then_inc(act_step.sem, 1)
                    for d in range(2):
                        t = 1 - FIRST[d]
                        act.activation(SI[0:H8, d, t * P:(t + 1) * P], MX[0:H8, d, t * P:(t + 1) * P], ACT.Exp, scale=-1.0,
                                       bias=ml[0:H8, d:d + 1])
                    act.activation(FL[0:H8], FL[0:H8], ACT.Exp, scale=-1.0)

                @block.vector
                def _(dve):
                    link = lambda ins: dve_chain.link(dve, ins)
                    dve.wait_ge(pe_step.sem, pe_step.at(2))
                    link(dve.tensor_copy(LF[0:H8].rearrange("p a b -> p (a b)"), ps[0:H8, 1, :]))

                    def part(v, d, t):
                        s = v[0:H8, d, t * P:(t + 1) * P]
                        return s if d == 0 else s[:, ::-1]
                    one = ones[0:H8, :]
                    for d in range(2):
                        for t in range(ST):
                            link(dve.tensor_tensor_scan(part(FC, d, t), one, part(LF, d, t), 0.0, ALU.mult, ALU.add))
                    dve.wait_ge(act_step.sem, act_step.at(1))
                    link(dve.tensor_tensor(BB[0:H8], IG[0:H8], FC[0:H8], ALU.subtract))
                    for d in range(2):
                        t = FIRST[d]
                        b = part(BB, d, t)
                        link(dve.tensor_tensor_scan(part(MX, d, t), b, b, 0.0, ALU.max, ALU.max))
                        end = t * P + (P - 1 if d == 0 else 0)
                        link(dve.tensor_tensor(ml[0:H8, d:d + 1], FC[0:H8, d, end:end + 1], MX[0:H8, d, end:end + 1], ALU.add))
                        link(dve.tensor_scalar(ml[0:H8, 2 + d:3 + d], MX[0:H8, d, end:end + 1], -1.0, None, ALU.mult))
                        b = part(BB, d, 1 - t)
                        link(dve.tensor_tensor_scan(part(MX, d, 1 - t), b, b, ml[0:H8, d:d + 1], ALU.max, ALU.max))
                    dve.tensor_scalar(NM[0:H8], MX[0:H8], -1.0, None, ALU.mult).then_inc(dve_step.sem, 1)
                    dve.tensor_tensor(FL[0:H8], FC[0:H8], MX[0:H8], ALU.add).then_inc(dve_step.sem, 1)
                    dve.wait_ge(pe_step.sem, pe_step.at(7))
                    dve.tensor_copy(bcol.rearrange("p a b -> p (a b)"), ps[:, 6, 0:6 * H8])
            pe_step.passed(7)
            act_step.passed(7)
            dve_step.passed(2)

        def mlstm():
            H8 = ML_HEADS
            with stage() as block:
                @block.tensor
                def _(pe):
                    for hh in range(H8):
                        sel = ident[0:H8, hh:hh + 1].broadcast_to([H8, P])
                        if hh >= 1:
                            pe.wait_ge(dve_free.sem, dve_free.at(hh))
                        for t in range(ST):
                            pe.matmul(ps[:, 0, t * P:(t + 1) * P], mk[:, hh, t * P:(t + 1) * P], mq[:, hh, t * P:(t + 1) * P], start=True, stop=True)
                        for d in range(2):
                            t = 1 - FIRST[d]
                            pe.matmul(ps[:, 0, (2 + d) * P:(3 + d) * P], sel, SI[0:H8, d, t * P:(t + 1) * P], start=True, stop=True)
                        for d in range(2):
                            pe.matmul(ps[:, 1, d * S:(d + 1) * S], sel, NM[0:H8, d, :], start=True, stop=False)
                            mm = pe.matmul(ps[:, 1, d * S:(d + 1) * S], ident, tri_mask[d].unsqueeze(1).broadcast_to([P, ST, P]), start=False, stop=True)
                        mm.then_inc(pe_step.sem, 1)
                        for d in range(2):
                            mm = pe.matmul(ps[:, 2, d * S:(d + 1) * S], sel, FL[0:H8, d, :], start=True, stop=True)
                        mm.then_inc(pe_step.sem, 1)
                        pe.wait_ge(dve_step.sem, dve_step.at(2 * hh + 1))
                        for d in range(2):
                            pe.matmul(ps[:, 3, d * P:(d + 1) * P], kws[:, d, :], mv[:, FIRST[d], hh * P:(hh + 1) * P], start=True, stop=True)
                            mm = pe.matmul(ps[:, 3, S + d:S + d + 1], kws[:, d, :], ones[:, 0:1], start=True, stop=True)
                        mm.then_inc(pe_step.sem, 1)
                        pe.wait_ge(dve_step.sem, dve_step.at(2 * hh + 2))
                        pe.wait_ge(act_step.sem, act_step.at(4 * hh + 3))
                        for d in range(2):
                            for t in range(ST):
                                o = (d * ST + t) * P
                                wt = wts[:, hh % 2, d, t * P:(t + 1) * P]
                                second = t != FIRST[d]
                                pe.matmul(ps[:, 4, o:o + P], mv[:, t, hh * P:(hh + 1) * P], wt, start=True, stop=not second)
                                if second:
                                    pe.matmul(ps[:, 4, o:o + P], cst[:, d, :], qst[:, d, :], start=False, stop=True)
                                mm = pe.matmul(ps[:, 5, o:o + P], ones, wt, start=True, stop=not second)
                                if second:
                                    mm = pe.matmul(ps[:, 5, o:o + P], nst[:, d:d + 1].broadcast_to([P, P]), qst[:, d, :], start=False, stop=True)
                        mm.then_inc(pe_step.sem, 1)

                @block.scalar
                def _(act):
                    for hh in range(H8):
                        act.wait_ge(pe_step.sem, pe_step.at(4 * hh + 1))
                        if hh >= 2:
                            act.wait_ge(pe_step.sem, pe_step.at(4 * (hh - 1)))
                        for d in range(2):
                            for t in range(ST):
                                ins = act.activation(wts[:, hh % 2, d, t * P:(t + 1) * P], ps[:, 1, (d * ST + t) * P:(d * ST + t + 1) * P],
                                                     ACT.Exp, bias=bcol[:, d * ST + t, hh:hh + 1])
                        ins.then_inc(act_step.sem, 1)
                        act.wait_ge(pe_step.sem, pe_step.at(4 * hh + 2))
                        if hh >= 1:
                            act.wait_ge(dve_free.sem, dve_free.at(hh))
                        act.activation(floors.rearrange("p a b -> p (a b)"), ps[:, 2, :], ACT.Copy).then_inc(act_step.sem, 1)
                        act.wait_ge(pe_step.sem, pe_step.at(4 * hh + 3))
                        act.activation(cst.rearrange("p a b -> p (a b)"), ps[:, 3, 0:S], ACT.Copy)
                        act.activation(nst[:, :], ps[:, 3, S:S + 2], ACT.Copy).then_inc(act_step.sem, 1)
                        act.wait_ge(pe_step.sem, pe_step.at(4 * hh + 4))
                        act.activation(dens.rearrange("p a b -> p (a b)"), ps[:, 5, :], ACT.Abs).then_inc(act_step.sem, 1)

                @block.vector
                def _(dve):
                    link = lambda ins: dve_chain.link(dve, ins)
                    for hh in range(H8):
                        for d in range(2):
                            if hh >= 1:
                                dve.wait_ge(pe_step.sem, pe_step.at(4 * hh))
                            ins = dve.tensor_scalar(kws[:, d, :], k_tok[:, FIRST[d], hh * P:(hh + 1) * P], bcol[:, 4 + d, hh:hh + 1], None, ALU.mult)
                        ins.then_inc(dve_step.sem, 1)
                        dve.wait_ge(act_step.sem, act_step.at(4 * hh + 1))
                        dve.tensor_tensor(wts[:, hh % 2, :, :], wts[:, hh % 2, :, :],
                                          ps[:, 0, 0:S].unsqueeze(1).broadcast_to([P, 2, S]), ALU.mult)
                        for d in range(2):
                            t = 1 - FIRST[d]
                            ins = dve.tensor_tensor(qst[:, d, :], mq[:, hh, t * P:(t + 1) * P], ps[:, 0, (2 + d) * P:(3 + d) * P], ALU.mult)
                        ins.then_inc(dve_step.sem, 1)
                        dve.wait_ge(pe_step.sem, pe_step.at(4 * hh + 4))
                        dve.wait_ge(act_step.sem, act_step.at(4 * hh + 4))
                        flat = lambda v: v.rearrange("p a b -> p (a b)")
                        link(dve.tensor_tensor(flat(dens), flat(dens), flat(floors), ALU.max))
                        link(dve.reciprocal(flat(dens), flat(dens)))
                        link(dve.tensor_tensor(flat(nums), ps[:, 4, :], flat(dens), ALU.mult))
                        dve.tensor_tensor(mixed[:, KD + hh, :], nums[:, 0, :], nums[:, 1, :], ALU.add).then_inc(dve_free.sem, 1)
                        dve.wait_ge(dve_free.sem, dve_free.at(hh + 1))
            pe_step.passed(4 * H8)
            act_step.passed(4 * H8)
            dve_step.passed(2 * H8)
            dve_free.passed(H8)

        GM = Arena()
        gq = GM.take(GLA_HEADS, S)
        gk = GM.take(GLA_HEADS, S)
        gv = GM.take(ST, D)
        gr = h[:, :, S:T2]
        low = GM.take(ST, 32)
        low_t = GM.take(2, S)
        w2 = GM.take(2, 512)
        la = GM.take(2, GLA_HEADS, S)
        eb = GM.take(2, GLA_HEADS, S)
        qin = GM.take(2, GLA_HEADS, S)
        kout = GM.take(2, GLA_HEADS, S)
        kend_t = ul32[:, 0:2 * GLA_HEADS * ST * P].rearrange("p (a b) -> p a b", b=P)
        gst = GM.take(2, 3, 2 * P)
        restart = GM.take(2, S)
        N_CH = S // GLA_CHUNK
        dec = GM.take(2, GLA_HEADS, N_CH)
        GLA_SQ = GM.at

        def c_project():
            items = []
            for m in range(4):
                items.append(chunk_item(0, m, 0, S, gq[:, m, :], scale=P ** -0.5))
            for m in range(4):
                items.append(chunk_item(1, m, 0, S, gk[:, m, :]))
            for q in range(4):
                items.append(token_item(2 + q // 2, (q % 2) * 256, 256, range(ST), gv[:, :, q * 256:(q + 1) * 256]))
            for m in range(8):
                items.append(chunk_item(4 + m // 4, m % 4, 0, S, gr[:, m, :]))
            items.append(token_item(6, 0, 32, range(ST), low))
            listed("c_in", C_SPANS, items)

        def gla_prepare():
            flat = lambda v: v.rearrange("p a b c -> p (a b c)")
            with stage() as block:
                @block.sync
                def _(sp):
                    sp.dma_start(w2[0:GLA_RANK], a["c_gate_w2_2"][0].rearrange("i r c -> r i c")).then_inc(loaded.sem, 16)

                @block.gpsimd
                def _(pool):
                    pool_chain.link(pool, pool.memset(restart, 1.0))
                    pool.memset(restart[:, 0, 0::GLA_CHUNK], 0.0).then_inc(pool_step.sem, 1)
                    pool.memset(restart[:, 1, GLA_CHUNK - 1::GLA_CHUNK], 0.0).then_inc(pool_step.sem, 1)
                    pool.wait_ge(pool_step.sem, pool_step.at(2))

                @block.tensor
                def _(pe):
                    for d in range(2):
                        for t in range(ST):
                            tr = pe.transpose(ps[0:GLA_RANK, 0, (d * ST + t) * P:(d * ST + t + 1) * P],
                                              low[:, t, d * GLA_RANK:(d + 1) * GLA_RANK], ident)
                    tr.then_inc(pe_step.sem, 1)
                    pe.wait_ge(loaded.sem, loaded.at(16))
                    pe.wait_ge(act_step.sem, act_step.at(1))
                    for d in range(2):
                        for hh in range(GLA_HEADS):
                            mm = pe.matmul(ps[:, 1 + 2 * d + hh // 2, (hh % 2) * S:(hh % 2 + 1) * S],
                                           w2[0:GLA_RANK, d, hh * P:(hh + 1) * P], low_t[0:GLA_RANK, d, :], start=True, stop=True)
                            if hh % 2:
                                mm.then_inc(pe_step.sem, 1)
                    for n in range(4):
                        pe.wait_ge(dve_step.sem, dve_step.at(3 + n))
                        for m in range(4):
                            b = 4 * n + m
                            d, hh, t = b // 8, (b // 2) % 4, b % 2
                            tr = pe.transpose(ps[:, 4 + n if n < 4 else 0, m * P:(m + 1) * P], eb[:, d, hh, t * P:(t + 1) * P], ident)
                        tr.then_inc(pe_step.sem, 1)

                @block.scalar
                def _(act):
                    link = lambda ins: act_chain.link(act, ins)
                    act.wait_ge(pe_step.sem, pe_step.at(1))
                    act.activation(low_t[0:GLA_RANK].rearrange("p a b -> p (a b)"), ps[0:GLA_RANK, 0, :], ACT.Copy).then_inc(act_step.sem, 1)
                    act.wait_ge(dve_step.sem, dve_step.at(1))
                    link(act.activation(flat(eb), flat(la), ACT.Abs))
                    link(act.activation(flat(eb), flat(eb), ACT.Exp, scale=-1.0))
                    act.activation(flat(eb), flat(eb), ACT.Ln, bias=ones[:, 0:1]).then_inc(act_step.sem, 1)
                    act.wait_ge(dve_step.sem, dve_step.at(2))
                    act.activation(flat(qin), flat(la), ACT.Exp).then_inc(act_step.sem, 1)
                    act.activation(flat(kout), flat(la), ACT.Exp, scale=-1.0).then_inc(act_step.sem, 1)
                    for d in range(2):
                        end = la[:, d, :, (GLA_CHUNK - 1 if d == 0 else 0)::GLA_CHUNK]
                        act.activation(dec[:, d, :, :], end, ACT.Exp).then_inc(act_step.sem, 1)
                    for n in range(4):
                        act.wait_ge(pe_step.sem, pe_step.at(6 + n))
                        act.activation(kend_t[:, 4 * n:4 * n + 4, :].rearrange("p a b -> p (a b)"), ps[:, 4 + n, :], ACT.Copy)

                @block.vector
                def _(dve):
                    link = lambda ins: dve_chain.link(dve, ins)
                    for d in range(2):
                        for hh in range(GLA_HEADS):
                            dve.wait_ge(pe_step.sem, pe_step.at(2 + 2 * d + hh // 2))
                            ins = dve.tensor_scalar(la[:, d, hh, :], ps[:, 1 + 2 * d + hh // 2, (hh % 2) * S:(hh % 2 + 1) * S],
                                                    col("gate_b", d * GLA_HEADS + hh), None, ALU.add)
                            if d == 1 and hh == GLA_HEADS - 1:
                                ins.then_inc(dve_step.sem, 1)
                            else:
                                link(ins)
                    dve.wait_ge(act_step.sem, act_step.at(2))
                    dve.wait_ge(dve_step.sem, dve_step.at(1))
                    link(dve.scalar_tensor_tensor(out=flat(la), in0=flat(la), scalar=0.0, in1=flat(eb), op0=ALU.min, op1=ALU.subtract))
                    link(dve.tensor_scalar(flat(la), flat(la), 1.0 / GLA_TAU, None, ALU.mult))
                    dve.wait_ge(pool_step.sem, pool_step.at(2))
                    for d in range(2):
                        for hh in range(GLA_HEADS):
                            x_, r_ = la[:, d, hh, :], restart[:, d, :]
                            if d == 1:
                                x_, r_ = x_[:, ::-1], r_[:, ::-1]
                            ins = dve.tensor_tensor_scan(x_, r_, x_, 0.0, ALU.mult, ALU.add)
                            if d == 1 and hh == GLA_HEADS - 1:
                                ins.then_inc(dve_step.sem, 1)
                            else:
                                link(ins)
                    dve.wait_ge(act_step.sem, act_step.at(6))
                    for d in range(2):
                        link(dve.tensor_tensor(kout[:, d], kout[:, d], gk, ALU.mult))
                        for half in range(2):
                            v = kout[:, d, 2 * half:2 * half + 2, :].rearrange("p h (c l) -> p (h c) l", c=N_CH)
                            to = eb[:, d, 2 * half:2 * half + 2, :].rearrange("p h (c l) -> p (h c) l", c=N_CH)
                            by = dec[:, d, 2 * half:2 * half + 2, :].rearrange("p h c -> p (h c)")
                            dve.tensor_tensor(to, v, by.unsqueeze(2).broadcast_to([P, 2 * N_CH, GLA_CHUNK]), ALU.mult).then_inc(dve_step.sem, 1)
                    for d in range(2):
                        link(dve.tensor_tensor(qin[:, d], qin[:, d], gq, ALU.mult))
            loaded.passed(16)
            pool_step.passed(2)
            pe_step.passed(9)
            act_step.passed(6)
            dve_step.passed(6)

        def gla():
            att = eb
            masks = (mat("gla_upto"), mat("gla_from"))
            C = GLA_CHUNK

            def chunk_sum(d, c):
                return ps[:, 1 + 2 * d + c % 2, (c // 2) * 2 * P:(c // 2 + 1) * 2 * P]

            with stage() as block:
                @block.tensor
                def _(pe):
                    for hh in range(GLA_HEADS):
                        if hh >= 1:
                            pe.wait_ge(act_step.sem, act_step.at(hh))
                        for d in range(2):
                            for t in range(ST):
                                o = (d * ST + t) * P
                                mm = pe.matmul(ps[:, 0, o:o + P], kout[:, d, hh, t * P:(t + 1) * P], qin[:, d, hh, t * P:(t + 1) * P], start=True, stop=True)
                        mm.then_inc(pe_step.sem, 1)
                        for d in range(2):
                            for n in range(N_CH - 1):
                                c = n if d == 0 else N_CH - 1 - n
                                p0 = C * (c % 2)
                                mm = pe.matmul(chunk_sum(d, c),
                                               kend_t[p0:p0 + C, (d * GLA_HEADS + hh) * ST + c // 2, :],
                                               gv[p0:p0 + C, c // 2, hh * 2 * P:(hh + 1) * 2 * P], start=True, stop=True)
                        mm.then_inc(pe_step.sem, 1)
                        pe.wait_ge(dve_step.sem, dve_step.at(8 * hh + 8))
                        for m in range(2):
                            for t in range(ST):
                                o = (m * ST + t) * P
                                run = []
                                for d in range(2):
                                    run.append((ps[:, 5, o:o + P], gv[:, t, hh * 2 * P + m * P:hh * 2 * P + (m + 1) * P],
                                                att[:, d, hh, t * P:(t + 1) * P]))
                                for d in range(2):
                                    for c in (2 * t, 2 * t + 1):
                                        n = c if d == 0 else N_CH - 1 - c
                                        if n:
                                            run.append((ps[:, 5, o + (c % 2) * C:o + (c % 2 + 1) * C], gst[:, d, n - 1, m * P:(m + 1) * P],
                                                        qin[:, d, hh, c * C:(c + 1) * C]))
                                for i, (to, stat, mov) in enumerate(run):
                                    mm = pe.matmul(to, stat, mov, start=(i == 0), stop=(i == len(run) - 1), skip_group_check=True)
                        mm.then_inc(pe_step.sem, 1)

                @block.scalar
                def _(act):
                    for hh in range(GLA_HEADS):
                        act.wait_ge(pe_step.sem, pe_step.at(3 * hh + 3))
                        act.activation(u32[:, 2 * hh:2 * hh + 2, :], ps[:, 5, :].rearrange("p (a b) -> p a b", a=2), ACT.Copy).then_inc(act_step.sem, 1)

                @block.vector
                def _(dve):
                    for hh in range(GLA_HEADS):
                        dve.wait_ge(pe_step.sem, pe_step.at(3 * hh + 1))
                        for d in range(2):
                            v = ps[:, 0, d * S:(d + 1) * S].rearrange("p (t l) -> p t l", t=ST)
                            dve.tensor_tensor(att[:, d, hh, :].rearrange("p (t l) -> p t l", t=ST), v,
                                              masks[d].unsqueeze(1).broadcast_to([P, ST, P]), ALU.mult).then_inc(dve_step.sem, 1)
                        dve.wait_ge(pe_step.sem, pe_step.at(3 * hh + 2))
                        if hh >= 1:
                            dve.wait_ge(pe_step.sem, pe_step.at(3 * hh))
                        for n in range(N_CH - 1):
                            for d in range(2):
                                c = n if d == 0 else N_CH - 1 - n
                                new = chunk_sum(d, c)
                                if n == 0:
                                    dve.tensor_copy(gst[:, d, 0, :], new).then_inc(dve_step.sem, 1)
                                else:
                                    dve.wait_ge(dve_step.sem, dve_step.at(8 * hh + 2 + 2 * (n - 1) + d + 1))
                                    dve.scalar_tensor_tensor(out=gst[:, d, n, :], in0=gst[:, d, n - 1, :], scalar=dec[:, d, hh, c:c + 1],
                                                             in1=new, op0=ALU.mult, op1=ALU.add).then_inc(dve_step.sem, 1)
            pe_step.passed(3 * GLA_HEADS)
            act_step.passed(GLA_HEADS)
            dve_step.passed(8 * GLA_HEADS)

        def flat16(v):
            return v[:, :, :].rearrange("p a b -> p (a b)").rearrange("p (a b) -> p a b", b=S)

        program = [setup]
        for l in range(DEPTH):
            program.append(lambda l=l: modulation(l))
        for l in range(DEPTH):
            T = S if l == DEPTH - 1 else T2
            program += [lambda l=l: pre(l, 0, 0), lambda l=l: ffn_up(("up", l, 0), T2, bands_of=l),
                        lambda l=l: ffn_down(("down", l, 0), mid, T2), lambda l=l: post1(l, 0, 1, 0.5),
                        rel_bias, lambda l=l: pre(l, 3, 2), lambda l=l: project(l),
                        lambda l=l: qk_norm(l), lambda l=l: attention(l),
                        lambda l=l, T=T: wide(("o", l), uh, ul, KD, T), lambda l=l, T=T: post1(l, 3, 3, 1.0, T),
                        lambda l=l, T=T: pre(l, 6, 4, T), lambda l=l, T=T: ffn_up(("up", l, 1), T),
                        lambda l=l, T=T: ffn_down(("down", l, 1), mid, T), lambda l=l, T=T: post1(l, 6, 5, 0.5, T)]
        program += [lambda: pre2(0, 0), ab_project, ssd_conv, ssd_prepare, ssd_scan, mlstm_prepare, mlstm,
                    lambda: head_norm(0, KD, 4, "ssd_norm", HN_AT, before=(ACT.Silu, z)),
                    lambda: head_norm(KD, KD, 1, "mlstm_norm", HN_AT, before=(ACT.Sigmoid, o_pre)),
                    lambda: wide("ab_out", flat16(uh), flat16(ul), 2 * KD, S), lambda: post2(0, 1),
                    lambda: pre2(0, 2), lambda: ffn_up2(0), lambda: ffn_down(("down2", 0), mid2, S), lambda: post2(0, 3),
                    lambda: pre2(1, 0), c_project, gla_prepare, gla,
                    lambda: head_norm(0, KD, 2, "gla_norm", GLA_SQ, after=(ACT.Silu, gr)),
                    lambda: wide("c_out", flat16(uh), flat16(ul), KD, S), lambda: post2(1, 1),
                    lambda: pre2(1, 2), lambda: ffn_up2(1), lambda: ffn_down(("down2", 1), mid2, S), lambda: post2(1, 3)]

        for step in program[:stop]:
            step()
        finish()


_INS = ['x', 'c', 'ctx', 'c_ctx', 'w_ada', 'b_ada', 'norm_g', 'w_in', 'qk_g', 'rpb', 'conv_w', 'w_o', 'ffn_wi', 'ffn_wo',
        'norm_g_2', 'ab_w_in_2', 'ab_conv_w_2', 'ab_conv_b_2', 'ab_dt_bias_2', 'ab_a_log_2', 'ab_d_skip_2',
        'ab_ssd_norm_2', 'ab_ig_bias_2', 'ab_fg_bias_2', 'ab_mlstm_norm_2', 'ab_w_out_2', 'c_w_in_2',
        'c_gate_w2_2', 'c_gate_b_2', 'c_norm_2', 'c_w_out_2', 'ffn_w_up_2', 'ffn_conv_w_2', 'ffn_conv_b_2',
        'ffn_w_down_2']


def kernel(**inputs):
    import numpy as _np
    import concourse.bacc as _bacc
    from concourse import mybir as _mybir
    from concourse.bass_utils import run_bass_kernel_spmd as _run

    nc = _bacc.Bacc("TRN2", target_bir_lowering=False, num_devices=1)
    arrays, aps = {}, {}
    for name in _INS + ["const"]:
        arr = constants() if name == "const" else _np.ascontiguousarray(inputs[name])
        arrays[f"in_{name}_dram"] = arr
        aps[name] = nc.dram_tensor(f"in_{name}_dram", arr.shape, _mybir.dt.from_np(arr.dtype), kind="ExternalInput").ap()
    n = (B_HEADS * RPB_H * RPB_PAD // P + 1) * P
    aps["padded"] = nc.dram_tensor("rpb_padded", (n,), F32, kind="Internal").ap().rearrange("(p n) -> p n", p=P)
    out = nc.dram_tensor("out_0_dram", (1, S, D), F32, kind="ExternalOutput").ap()
    two_blocks(nc, aps, out)
    r = _run(nc, [arrays], core_ids=[0])
    return r.results[0]["out_0_dram"]
```

```python
import math
from contextlib import ExitStack

import concourse.bass as bass
import numpy as np
from concourse import mybir

F32 = mybir.dt.float32
F32R = mybir.dt.float32r
ACT = mybir.ActivationFunctionType
ALU = mybir.AluOpType
AX_X = mybir.AxisListType.X
ds = bass.ds

P = 128
D = 1024
KD = D // P
S = 256
T2 = 2 * S
ST = S // P
DEPTH = 2
HD = 64
GRID_W, WIN_R, WIN_C = 64, 8, 16
ROWS = S // GRID_W
A_HEADS, A_KV, B_HEADS = 6, 2, 6
FFN = 2816
KF = FFN // P
N_MOD = 9
EPS = 1e-6
NEG = -1e30
RPB_H, RPB_W = 2 * WIN_R - 1, 2 * WIN_C - 1
RPB_PAD = 2 * GRID_W - 1
SSD_HEADS, SSD_GROUPS, SSD_CONV = 16, 2, 5
ML_HEADS = 8
GLA_HEADS, GLA_RANK, GLA_TAU, GLA_CHUNK = 4, 16, 16.0, 64
BANK = 512
RING = 2
ARENA = 20240
SLOT = 4096
ADA_COLS = 384
ADA_FIRST = 6
HALF = SLOT // 2

CONSTS = ["ident", "ones", "half_ones", "upto", "from_", "mask_upto", "mask_from", "rot", "swap",
          "gla_upto", "gla_from"]


def constants():
    k = np.arange(P)[:, None]
    m = np.arange(P)[None, :]
    c = {
        "ident": k == m,
        "ones": k >= 0 * m,
        "half_ones": k // HD == m // HD,
        "upto": k <= m,
        "from_": k >= m,
        "mask_upto": np.where(k <= m, 0.0, NEG),
        "mask_from": np.where(k >= m, 0.0, NEG),
        "swap": k == (m + HD) % P,
        "gla_upto": (k <= m) & (k // GLA_CHUNK == m // GLA_CHUNK),
        "gla_from": (k >= m) & (k // GLA_CHUNK == m // GLA_CHUNK),
    }
    rot = np.zeros((P, P))
    half = (np.arange(P) // 16) % 2
    for j in range(P):
        if half[j] == 0:
            rot[j + 16, j] = -1.0
        else:
            rot[j - 16, j] = 1.0
    c["rot"] = rot
    freqs = HD // 4
    pos = np.arange(S)
    freq = (1.0 / (np.float32(10000.0) ** (np.arange(freqs, dtype=np.float32) / np.float32(freqs)))).astype(np.float32)
    axis = (np.arange(P) % HD) // 32
    f = np.arange(P) % 16
    where = np.where(axis[:, None] == 0, (pos // GRID_W)[None, :], (pos % GRID_W)[None, :]).astype(np.float32)
    ang = (where * freq[f][:, None]).astype(np.float32)
    q = np.arange(P) % GRID_W
    key = np.arange(S) % GRID_W
    start = np.clip(q - WIN_C // 2, 0, GRID_W - WIN_C)
    inside = (key[None, :] >= start[:, None]) & (key[None, :] < start[:, None] + WIN_C)
    parts = [np.asarray(c[n], np.float32) * np.ones((P, P), np.float32) for n in CONSTS]
    parts += [np.cos(ang), np.sin(ang), np.where(inside, 0.0, NEG)]
    parts += [(k // GRID_W == m // GRID_W) & (k % GRID_W + m % GRID_W == GRID_W - 1)]
    parts += [k % 32 == np.arange(2)[None, :]]
    return np.ascontiguousarray(np.concatenate([np.asarray(p, np.float32) for p in parts], axis=1))


CONST_W = len(CONSTS) * P + 3 * S


class Signal:

    def __init__(self, sem):
        self.sem = sem
        self.base = 0

    def at(self, n):
        return self.base + n

    def passed(self, n):
        self.base += n


class Chain:

    def __init__(self, sem):
        self.sem = sem
        self.n = 0

    def link(self, eng, ins):
        ins.then_inc(self.sem, 1)
        self.n += 1
        eng.wait_ge(self.sem, self.n)


def turns(eng, n, period, body, first=0, most=None):
    def item(turn, k):
        body(turn + (first + k) // period if first + k >= period else turn, (first + k) % period)

    full = min(n - first, n if most is None else most) // period
    if full >= 2:
        with eng.Fori(0, full) as turn:
            for k in range(period):
                item(turn, k)
    else:
        for turn in range(full):
            for k in range(period):
                item(turn, k)
    for k in range(n - first - full * period):
        item(full + k // period, k % period)


def two_blocks(nc, a, out, stop=None):
    ctx = ExitStack()
    with ctx:
        place = [(nc.sbuf_base + 31) // 32 * 32]

        def sb(name, shape, dt=F32, at=None):
            size = 4 * int(np.prod(shape[1:]))
            offset = place[0] if at is None else at
            if at is None:
                place[0] += (size + 31) // 32 * 32
            return nc.alloc_sbuf_tensor_at(name, shape, dt, offset=offset)

        def signal(name):
            return Signal(ctx.enter_context(nc.semaphore(name)))

        def chain(name):
            return Chain(ctx.enter_context(nc.semaphore(name)))

        ring = [sb(f"ring{i}", [P, SLOT]) for i in range(RING)]
        h = sb("h", [P, KD, T2])
        uh_at = place[0]
        uh = sb("uh", [P, KD, T2], F32R)
        ul_at = place[0]
        ul = sb("ul", [P, KD, T2], F32R)
        u32 = sb("u32", [P, 2 * KD, S], F32, at=uh_at)
        ul32 = sb("ul32", [P, KD * T2], F32, at=ul_at)
        wh = [sb(f"wh{i}", [P, HALF], F32R) for i in range(2)]
        wl = [sb(f"wl{i}", [P, HALF], F32R) for i in range(2)]
        arena = sb("arena", [P, ARENA])
        const = sb("const", [P, CONST_W])
        ps = ctx.enter_context(nc.psum_tensor("ps", [P, 8, BANK], F32))

        def mat(name):
            i = CONSTS.index(name)
            return const[:, i * P:(i + 1) * P]

        tables = len(CONSTS) * P
        cos_t = const[:, tables:tables + S]
        sin_t = const[:, tables + S:tables + 2 * S]
        window = const[:, tables + 2 * S:tables + 3 * S]
        ident, ones = mat("ident"), mat("ones")

        class Arena:

            def __init__(self, start=0):
                self.at = start

            def take(self, *shape):
                n = int(np.prod(shape))
                v = arena[:, self.at:self.at + n]
                self.at += n
                assert self.at <= ARENA, self.at
                if len(shape) == 2:
                    v = v.rearrange("p (a b) -> p a b", a=shape[0])
                if len(shape) == 3:
                    v = v.rearrange("p (a b c) -> p a b c", a=shape[0], b=shape[1])
                return v

        vectors = [("b_ada", a["b_ada"].rearrange("l (r p) -> (l r) p", p=P)),
                   ("c", a["c"].rearrange("l (r p) -> (l r) p", p=P)),
                   ("c_ctx", a["c_ctx"].rearrange("(r p) -> r p", p=P)),
                   ("norm_g", a["norm_g"].rearrange("l i (r p) -> (l i r) p", p=P)),
                   ("conv_w", a["conv_w"].rearrange("l i (r p) -> (l i r) p", p=P)),
                   ("norm_g_2", a["norm_g_2"].rearrange("l i (r p) -> (l i r) p", p=P)),
                   ("ab_conv_w", a["ab_conv_w_2"].rearrange("l i (r p) -> (l i r) p", p=P)),
                   ("ab_conv_b", a["ab_conv_b_2"].rearrange("l (r p) -> (l r) p", p=P)),
                   ("ssd_norm", a["ab_ssd_norm_2"].rearrange("l (r p) -> (l r) p", p=P)),
                   ("mlstm_norm", a["ab_mlstm_norm_2"].rearrange("l (r p) -> (l r) p", p=P)),
                   ("gate_b", a["c_gate_b_2"].rearrange("l i (r p) -> (l i r) p", p=P)),
                   ("gla_norm", a["c_norm_2"].rearrange("l (r p) -> (l r) p", p=P)),
                   ("ffn_conv_w", a["ffn_conv_w_2"].rearrange("l i (r p) -> (l i r) p", p=P)),
                   ("ffn_conv_b", a["ffn_conv_b_2"].rearrange("l (r p) -> (l r) p", p=P))]
        col_at, pieces, n_rows = {}, [], 0
        for name, v in vectors:
            col_at[name] = n_rows
            r = 0
            while r < v.shape[0]:
                m = min(v.shape[0] - r, P - n_rows % P)
                pieces.append((v[r:r + m, :], n_rows // P, n_rows % P, m))
                r += m
                n_rows += m
        row_tiles = [min(P, n_rows - P * t) for t in range((n_rows + P - 1) // P)]
        cols = sb("cols", [P, n_rows])
        head_gain = sb("head_gain", [P, DEPTH * 2])
        d_skip = sb("d_skip", [P, KD])
        gate_bias = sb("gate_bias", [P, 64])
        a_log = sb("a_log", [P, 2 * SSD_HEADS])
        mod = sb("mod", [P, DEPTH, N_MOD * KD, 2])
        pre_scale = sb("pre_scale", [P, KD, 2])
        post_scale = sb("post_scale", [P, KD, 2])
        rstd = sb("rstd", [P, T2])
        eps = sb("eps", [P, 1])
        act_c = sb("act_c", [P, KD, 32])
        pick = sb("pick", [P, 2])
        mod_rows = Arena(12288).take(2, ADA_COLS)

        def col(name, i, n=1):
            return cols[:, col_at[name] + i:col_at[name] + i + n]

        ready = [signal(f"slot{i}_loaded") for i in range(RING)]
        high = signal("high_parts_done")
        split = signal("granules_split")
        prod = signal("products_done")
        band_load = signal("bands_loaded")
        flip_load = signal("flip_loaded")
        act_free = signal("act_evacuated")
        dve_free = signal("dve_evacuated")
        gate_done = signal("gate_done")
        loaded = signal("inputs_loaded")
        stored = signal("stored")
        pe_step, act_step, dve_step, pool_step = (signal(f"{e}_step") for e in ("pe", "act", "dve", "pool"))
        aux = signal("second_dve_step")
        sum_ready, h_squared, h_updated, h_updated2, h_scaled, u_high, u_ready, gains = (signal(n) for n in (
            "norm_sum_ready", "h_squared", "h_updated_by_vector", "h_updated_by_gpsimd", "h_scaled",
            "input_high_parts", "input_ready", "gains_ready"))
        conv_done = signal("pair_convolved")
        gelu_done = signal("gelu_done")
        ada_loaded, ada_multiplied, ada_copied, ada_turned, ada_taken = (signal(n) for n in (
            "ada_tile_loaded", "ada_tile_multiplied", "ada_rows_copied", "ada_columns_made", "ada_columns_taken"))
        act_chain, dve_chain, pool_chain = chain("act_chain"), chain("dve_chain"), chain("pool_chain")

        def stage():
            return nc.Block(no_gpsimd_drain=True)

        class Weights:

            def __init__(self, n, loads, parts=1, count=None, split=True, looped=True):
                self.n, self.loads, self.parts, self.split = n, loads, parts, split
                self.count = count or [2 if split else 1] * n
                self.looped = looped and count is None

        def column_tiles(w, k, width):
            v = w.rearrange("(k p) c -> p k c", p=P)

            def loads(i, slot):
                to = ring[slot][:, 0:k * width].rearrange("p (k c) -> p k c", k=k)
                return [(to, v[:, :, ds(i * width, width)])]
            return loads

        def pair_tiles(w, half, width):
            v = w.rearrange("(k p) c -> p k c", p=P)

            def loads(i, slot):
                to = ring[slot][:, 0:KD * 2 * width].rearrange("p (k c) -> p k c", k=KD)
                return [(to[:, :, 0:width], v[:, :, ds(i * width, width)]),
                        (to[:, :, width:2 * width], v[:, :, ds(i * width + half, width)])]
            return loads

        def listed_tiles(w, spans):
            v = w.rearrange("(k p) c -> p k c", p=P)

            def loads(i, slot):
                width = sum(n for _, n in spans[i])
                k = w.shape[0] // P
                to = ring[slot][:, 0:k * width].rearrange("p (k c) -> p k c", k=k)
                got, o = [], 0
                for c0, n in spans[i]:
                    got.append((to[:, :, o:o + n], v[:, :, c0:c0 + n]))
                    o += n
                return got
            return loads

        IN_SPANS = [[(0, 384)], [(384, 384)], [(768, 256)], [(1024, 384)], [(1408, 384)], [(1792, 512)], [(2304, 256)]]
        plan = {}
        order = []

        def planned(key, weights):
            plan[key] = weights
            order.append(key)

        def row_tiles_of(w, k):
            v = w.rearrange("(k p) c -> p k c", p=P)

            def loads(i, slot):
                n = min(4, k - 4 * i)
                return [(ring[slot][:, 0:n * D].rearrange("p (k c) -> p k c", k=n), v[:, 4 * i:4 * i + n, :])]
            return loads

        def granules(spans):
            return [(sum(n for _, n in span) + 255) // 256 for span in spans]

        planned("ada", Weights(ADA_FIRST, column_tiles(a["w_ada"][0], KD, ADA_COLS), split=False))
        for l in range(DEPTH):
            for f in range(2):
                if f == 1:
                    planned(("in", l), Weights(len(IN_SPANS), listed_tiles(a["w_in"][l], IN_SPANS), count=granules(IN_SPANS)))
                    planned(("o", l), Weights(2, column_tiles(a["w_o"][l], KD, 512)))
                planned(("up", l, f), Weights(KF // 2, pair_tiles(a["ffn_wi"][l, f], FFN, 256), parts=2))
                planned(("down", l, f), Weights((KF + 3) // 4, row_tiles_of(a["ffn_wo"][l, f], KF), count=[2] * 5 + [1]))
        AB_SPANS = [[(512 * i, 512)] for i in range(5)] + [[(2592 + 512 * i, 512)] for i in range(8)] + [[(2560, 32), (6688, 32)]]
        planned("ab_in", Weights(len(AB_SPANS), listed_tiles(a["ab_w_in_2"][0], AB_SPANS), count=granules(AB_SPANS)))
        planned("ab_out", Weights(4, column_tiles(a["ab_w_out_2"][0], 2 * KD, 256)))
        planned(("up2", 0), Weights(KF // 2, pair_tiles(a["ffn_w_up_2"][0], FFN, 256), parts=2))
        planned(("down2", 0), Weights((KF + 3) // 4, row_tiles_of(a["ffn_w_down_2"][0], KF), count=[2] * 5 + [1]))
        C_SPANS = [[(512 * i, 512)] for i in range(6)] + [[(3072, 32)]]
        planned("c_in", Weights(len(C_SPANS), listed_tiles(a["c_w_in_2"][0], C_SPANS), count=granules(C_SPANS)))
        planned("c_out", Weights(2, column_tiles(a["c_w_out_2"][0], KD, 512)))
        planned(("up2", 1), Weights(KF // 2, pair_tiles(a["ffn_w_up_2"][1], FFN, 256), parts=2))
        planned(("down2", 1), Weights((KF + 3) // 4, row_tiles_of(a["ffn_w_down_2"][1], KF), count=[2] * 5 + [1]))

        def parts_of(w, i):
            return len(w.loads(i, 0)) if not w.looped else w.parts

        def load_first(sp, key):
            w = plan[key]
            for k in range(min(RING, w.n)):
                yield k, lambda k=k: [sp.dma_start(to, fr).then_inc(ready[k].sem, 16) for to, fr in w.loads(k, k)]

        def stream(sp, key):
            w = plan[key]
            gone = split if w.split else prod
            done = np.cumsum([0] + w.count)
            if w.looped:
                def load(turn, k):
                    sp.wait_ge(gone.sem, gone.at((turn * RING + k + 1) * w.count[0]))
                    for to, fr in w.loads((turn + 1) * RING + k, k):
                        sp.dma_start(to, fr).then_inc(ready[k].sem, 16)
                turns(sp, max(w.n - RING, 0), RING, load)
            else:
                for i in range(RING, w.n):
                    sp.wait_ge(gone.sem, gone.at(int(done[i - RING + 1])))
                    for to, fr in w.loads(i, i % RING):
                        sp.dma_start(to, fr).then_inc(ready[i % RING].sem, 16)
            at = order.index(key) + 1
            if at < len(order):
                for k, load in load_first(sp, order[at]):
                    last = [i for i in range(w.n) if i % RING == k]
                    if last:
                        sp.wait_ge(gone.sem, gone.at(int(done[last[-1] + 1])))
                    load()

        def split_high(act, key, g, slot, tile_turn, raw, shape_of, b):
            tile_loaded(act, key, tile_turn, slot)
            act.wait_ge(prod.sem, prod.at(g - 1))
            act.activation(shape_of(wh[b]), raw, ACT.Copy).then_inc(high.sem, 1)

        def split_low(dve, g, raw, shape_of, b):
            dve.wait_ge(high.sem, high.at(g + 1))
            dve.tensor_tensor(shape_of(wl[b]), raw, shape_of(wh[b]), ALU.subtract).then_inc(split.sem, 1)

        def multiply(pe, to, terms, start=True, stop=True, before=None):
            for n, ((sh, sl), (mh, ml)) in enumerate(terms):
                if before is not None:
                    before(pe, n)
                last = n == len(terms) - 1
                pe.matmul(to, sh, mh, start=start and n == 0, stop=False)
                pe.matmul(to, sh, ml, start=False, stop=False)
                mm = pe.matmul(to, sl, mh, start=False, stop=stop and last)
            return mm

        def with_lead(eng, n, lead, body, first=0, most=None):
            turns(eng, n - lead, 4, lambda turn, k: body(turn, k, True), first, most)
            for g in range(n - lead, n):
                body(g // 4, g % 4, False)

        def tile_loaded(pe, key, turn, k):
            w = plan[key]
            if w.looped:
                pe.wait_ge(ready[k].sem, ready[k].at((turn + 1) * 16 * w.parts))
            else:
                n = sum(parts_of(w, i) for i in range(k, turn * RING + k + 1, RING))
                pe.wait_ge(ready[k].sem, ready[k].at(16 * n))

        def stage_done(key):
            w = plan[key]
            prod.passed(sum(w.count))
            if w.split:
                high.passed(sum(w.count))
                split.passed(sum(w.count))
            for k in range(RING):
                ready[k].passed(16 * sum(parts_of(w, i) for i in range(k, w.n, RING)))

        def slot_view(k, n_k, width):
            return ring[k][:, 0:n_k * width].rearrange("p (k c) -> p k c", k=n_k)

        def setup():
            mem = Arena()
            rows = mem.take(len(row_tiles), P)
            tokens = mem.take(2 * ST, D)
            groups = len(row_tiles) + KD
            n_loads = 1 + 1 + len(pieces) + 2 * ST + 4 + 4
            with stage() as block:
                @block.sync
                def _(sp):
                    sp.dma_start(const[:, :], a["const"][:, 0:CONST_W]).then_inc(loaded.sem, 16)
                    sp.dma_start(pick[:, :], a["const"][:, CONST_W + P:CONST_W + P + 2]).then_inc(loaded.sem, 16)
                    for v, t, r, m in pieces:
                        sp.dma_start(rows[r:r + m, t, :], v).then_inc(loaded.sem, 16)
                    for t in range(ST):
                        sp.dma_start(tokens[:, t, :], a["x"][0, t * P:(t + 1) * P, :]).then_inc(loaded.sem, 16)
                        sp.dma_start(tokens[:, ST + t, :], a["ctx"][0, t * P:(t + 1) * P, :]).then_inc(loaded.sem, 16)
                    for half in range(2):
                        sp.dma_start(head_gain[half * HD:(half + 1) * HD, :],
                                     a["qk_g"].rearrange("l i d -> d (l i)"),
                                     allow_slow_non_contiguous=True).then_inc(loaded.sem, 16)
                        sp.dma_start(d_skip[half * HD:(half + 1) * HD, :],
                                     bass.AP(a["ab_d_skip_2"].tensor, half, [[0, HD], [2, KD]]),
                                     allow_slow_non_contiguous=True).then_inc(loaded.sem, 16)
                    for v, at, n in ((a["ab_dt_bias_2"], 0, 32), (a["ab_ig_bias_2"], 32, 16), (a["ab_fg_bias_2"], 48, 16)):
                        sp.dma_start(gate_bias[:, at:at + n], bass.AP(v.tensor, 0, [[0, P], [1, n]])).then_inc(loaded.sem, 16)
                    sp.dma_start(a_log[:, :], bass.AP(a["ab_a_log_2"].tensor, 0, [[0, P], [1, 32]])).then_inc(loaded.sem, 16)
                    for _, load in load_first(sp, order[0]):
                        load()

                @block.tensor
                def _(pe):
                    pe.wait_ge(loaded.sem, loaded.at(16 * n_loads))
                    for t, m in enumerate(row_tiles):
                        pe.transpose(ps[:, t % 8, 0:m], rows[0:m, t, :], ident[0:m, 0:m]).then_inc(prod.sem, 1)
                    for j in range(KD):
                        g = len(row_tiles) + j
                        if g >= 8:
                            pe.wait_ge(dve_free.sem, dve_free.at(g - 7))
                        for t in range(2 * ST):
                            last = pe.transpose(ps[:, g % 8, t * P:(t + 1) * P], tokens[:, t, j * P:(j + 1) * P], ident)
                        last.then_inc(prod.sem, 1)

                @block.gpsimd
                def _(pool):
                    pool.memset(act_c[:, :, :], 0.0).then_inc(pool_step.sem, 1)

                @block.vector
                def _(dve):
                    dve.memset(eps[:, :], EPS).then_inc(ada_taken.sem, 1)
                    for t, m in enumerate(row_tiles):
                        dve.wait_ge(prod.sem, prod.at(t + 1))
                        dve.tensor_copy(cols[:, t * P:t * P + m], ps[:, t % 8, 0:m]).then_inc(dve_free.sem, 1)
                    for j in range(KD):
                        g = len(row_tiles) + j
                        dve.wait_ge(prod.sem, prod.at(g + 1))
                        dve.tensor_copy(h[:, j, :], ps[:, g % 8, :]).then_inc(dve_free.sem, 1)

                @block.scalar
                def _(act):
                    act.wait_ge(dve_free.sem, dve_free.at(len(row_tiles)))
                    act.wait_ge(pool_step.sem, pool_step.at(1))
                    act.activation(act_c[:, :, 0], col("c", 0, KD), ACT.Silu).then_inc(act_free.sem, 1)
                    act.activation(act_c[:, :, 1], col("c_ctx", 0, KD), ACT.Silu).then_inc(act_free.sem, 1)
                    for _ in range(6):
                        act.nop().then_inc(act_free.sem, 1)
            prod.passed(groups)
            dve_free.passed(groups)
            act_free.passed(8)
            pool_step.passed(1)
            ada_taken.passed(1)
            loaded.passed(16 * n_loads)

        def ada_rows(pe, bank, weights):
            for kk in range(KD):
                q = 32 * (kk % 4)
                last = pe.matmul(ps[q:q + 32, bank, 0:ADA_COLS], act_c[:, kk, :], weights[:, kk, :], start=(kk < 4), stop=(kk >= 4))
            return last

        def ada_columns(pe, bank, rows):
            for m in range(ADA_COLS // P):
                last = pe.matmul(ps[:, bank, 2 * m:2 * m + 2], rows[:, m * P:(m + 1) * P], pick[:, :], start=True, stop=True)
            return last

        def ada_take(dve, bank, chunk):
            n = ADA_COLS // P
            return dve.tensor_tensor(mod[:, :, :, :].rearrange("p l c s -> p (l c) s")[:, ds(chunk, n), :],
                                     ps[:, bank, 0:2 * n].rearrange("p (a b) -> p a b", a=n),
                                     cols[:, ds(col_at["b_ada"] + chunk, n)].unsqueeze(2).broadcast_to([P, n, 2]), ALU.add)

        def modulation():
            key = "ada"
            w = plan[key]
            with stage() as block:
                @block.sync
                def _(sp):
                    stream(sp, key)

                @block.tensor
                def _(pe):
                    def rows(turn, k):
                        tile_loaded(pe, key, turn, k)
                        pe.wait_ge(act_free.sem, act_free.at(turn * 2 + k - 1))
                        ada_rows(pe, k, slot_view(k, KD, ADA_COLS)).then_inc(prod.sem, 1)

                    def columns(turn, k):
                        pe.wait_ge(act_free.sem, act_free.at(turn * 2 + k + 1))
                        pe.wait_ge(dve_free.sem, dve_free.at(turn * 2 + k - 1))
                        ada_columns(pe, 2 + k, mod_rows[:, k, :]).then_inc(pe_step.sem, 1)

                    def step(turn, k):
                        rows(turn if k == 0 else turn + 1, 1 - k)
                        columns(turn, k)
                    rows(0, 0)
                    turns(pe, w.n - 1, 2, step)
                    columns((w.n - 1) // 2, (w.n - 1) % 2)

                @block.scalar
                def _(act):
                    def tile(turn, k):
                        act.wait_ge(prod.sem, prod.at(turn * 2 + k + 1))
                        act.wait_ge(dve_free.sem, dve_free.at(turn * 2 + k - 1))
                        act.activation(mod_rows[:, k, :], ps[:, k, 0:ADA_COLS], ACT.Copy).then_inc(act_free.sem, 1)
                    turns(act, w.n, 2, tile)

                @block.vector
                def _(dve):
                    def tile(turn, k):
                        i = turn * 2 + k
                        dve.wait_ge(pe_step.sem, pe_step.at(i + 1))
                        ada_take(dve, 2 + k, i * (ADA_COLS // P)).then_inc(dve_free.sem, 1)
                    turns(dve, w.n, 2, tile)
            stage_done(key)
            act_free.passed(w.n)
            pe_step.passed(w.n)
            dve_free.passed(w.n)

        class Ada:
            LOOPED = 16
            ROW_BANK, COLUMN_BANK = 4, 5

            def __init__(self, tiles):
                self.tiles, self.n = tiles, len(tiles)
                layer, tile = tiles[0]
                self.chunk = layer * N_MOD * KD + tile * (ADA_COLS // P)

            def load(self, act, layer, tile):
                v = a["w_ada"][layer].rearrange("(k p) c -> p k c", p=P)
                act.dma_start(ada_slot, v[:, :, ds(tile * ADA_COLS, ADA_COLS)]).then_inc(ada_loaded.sem, 16)

            def has(self, g):
                return not isinstance(g, int) or g < self.n

            def scalar(self, act, g):
                if not self.has(g):
                    return
                act.wait_ge(ada_multiplied.sem, ada_multiplied.at(g + 1))
                act.activation(ada_row, ps[:, self.ROW_BANK, 0:ADA_COLS], ACT.Copy).then_inc(ada_copied.sem, 1)
                if not isinstance(g, int):
                    layer, tile = self.tiles[0]
                    self.load(act, layer, tile + 1 + g)
                elif g + 1 < self.n:
                    self.load(act, *self.tiles[g + 1])

            def rows(self, pe, g):
                if self.has(g):
                    pe.wait_ge(ada_loaded.sem, ada_loaded.at(16 * (g + 1)))
                    ada_rows(pe, self.ROW_BANK, ada_slot).then_inc(ada_multiplied.sem, 1)

            def columns(self, pe, g):
                if self.has(g):
                    pe.wait_ge(ada_copied.sem, ada_copied.at(g + 1))
                    pe.wait_ge(ada_taken.sem, ada_taken.at(g))
                    ada_columns(pe, self.COLUMN_BANK, ada_row).then_inc(ada_turned.sem, 1)

            def vector(self, dve, g):
                if self.has(g):
                    dve.wait_ge(ada_turned.sem, ada_turned.at(g + 1))
                    ada_take(dve, self.COLUMN_BANK, self.chunk + g * (ADA_COLS // P)).then_inc(ada_taken.sem, 1)

            def done(self):
                ada_loaded.passed(16 * self.n)
                for s_ in (ada_multiplied, ada_copied, ada_turned, ada_taken):
                    s_.passed(self.n)

        class Norm:

            def __init__(self, T, scale, shift=None, scales=None, n_scales=0, post=None):
                self.T, self.scale, self.shift, self.scales, self.n_scales = T, scale, shift, scales, n_scales
                self.post = post
                self.n_s = T // S
                mem = Arena()
                self.sq, self.scaled = mem.take(KD, T), mem.take(KD, T)
                self.parts = [(k, s, slice(s * S, (s + 1) * S)) for k in range(KD) for s in range(self.n_s)]

            def scalar(self, act, high_of):
                T = self.T
                if self.post is not None:
                    self.post.scalar(act, lambda: high_of(0))
                    high_of(1)
                for k in range(KD):
                    if self.post is not None:
                        if k % 2:
                            act.wait_ge(h_updated.sem, h_updated.at(k // 2 + 1))
                        else:
                            act.wait_ge(h_updated2.sem, h_updated2.at(k // 2 + 1))
                    act.activation(self.sq[:, k, :], h[:, k, 0:T], ACT.Square).then_inc(h_squared.sem, 1)
                if self.post is None:
                    high_of(0)
                act.wait_ge(sum_ready.sem, sum_ready.at(1))
                act_chain.link(act, act.activation(rstd[:, 0:T], ps[:, 0, 0:T], ACT.Ln, scale=1.0 / D, bias=eps[:, 0:1]))
                act.activation(rstd[:, 0:T], rstd[:, 0:T], ACT.Exp, scale=-0.5).then_inc(h_squared.sem, 1)
                for n, (k, s, t) in enumerate(self.parts):
                    act.wait_ge(h_scaled.sem, h_scaled.at(n + 1))
                    if self.shift is None:
                        ins = act.activation(uh[:, k, t], self.scaled[:, k, t], ACT.Copy)
                    else:
                        ins = act.activation(uh[:, k, t], self.scaled[:, k, t], ACT.Identity, bias=self.shift(k, s))
                    ins.then_inc(u_high.sem, 1)
                if self.post is None:
                    high_of(1)

            def tensor(self, pe):
                if self.post is not None:
                    self.post.tensor(pe)
                for k in range(KD):
                    pe.wait_ge(h_squared.sem, h_squared.at(k + 1))
                    last = pe.matmul(ps[:, 0, 0:self.T], ones, self.sq[:, k, :], start=(k == 0), stop=(k == KD - 1))
                last.then_inc(sum_ready.sem, 1)

            def vector(self, dve, low_of):
                if self.post is not None:
                    self.post.vector(dve, lambda: low_of(0))
                    low_of(1)
                if self.scales is not None:
                    self.scales(dve)
                    dve.wait_ge(gains.sem, gains.at(self.n_scales))
                if self.post is None:
                    low_of(0)
                dve.wait_ge(h_squared.sem, h_squared.at(KD + 1))
                lag = 2
                for n in range(len(self.parts) + lag):
                    if n < len(self.parts):
                        k, s, t = self.parts[n]
                        dve.scalar_tensor_tensor(out=self.scaled[:, k, t], in0=h[:, k, t], scalar=self.scale(k, s),
                                                 in1=rstd[:, t], op0=ALU.mult, op1=ALU.mult).then_inc(h_scaled.sem, 1)
                    if n >= lag:
                        k, s, t = self.parts[n - lag]
                        dve.wait_ge(u_high.sem, u_high.at(n - lag + 1))
                        if self.shift is None:
                            ins = dve.tensor_tensor(ul[:, k, t], self.scaled[:, k, t], uh[:, k, t], ALU.subtract)
                        else:
                            ins = dve.scalar_tensor_tensor(out=ul[:, k, t], in0=self.scaled[:, k, t], scalar=self.shift(k, s),
                                                           in1=uh[:, k, t], op0=ALU.add, op1=ALU.subtract)
                        ins.then_inc(u_ready.sem, 1)
                if self.post is None:
                    low_of(1)

            def gpsimd(self, pool):
                if self.post is not None:
                    self.post.gpsimd(pool)

            def input_ready(self, pe, k):
                pe.wait_ge(u_ready.sem, u_ready.at(self.n_s * (k + 1)))

            def done(self):
                h_squared.passed(KD + 1)
                sum_ready.passed(1)
                gains.passed(self.n_scales)
                for s_ in (h_scaled, u_high, u_ready):
                    s_.passed(len(self.parts))
                if self.post is not None:
                    self.post.done()

        def norm1(l, i, gi, T=T2, post=None):
            def scales(dve):
                dve.tensor_scalar(pre_scale[:, :, :], mod[:, l, (i + 1) * KD:(i + 2) * KD, :], 1.0, None,
                                  ALU.add).then_inc(gains.sem, 1)
                dve.wait_ge(gains.sem, gains.at(1))
                g = col("norm_g", (l * 6 + gi) * KD, KD)
                dve.tensor_tensor(pre_scale[:, :, :], pre_scale[:, :, :], g.unsqueeze(2).broadcast_to([P, KD, 2]),
                                  ALU.mult).then_inc(gains.sem, 1)
            return Norm(T, lambda k, s: pre_scale[:, k, s:s + 1], lambda k, s: mod[:, l, i * KD + k, s:s + 1],
                        scales, 2, post)

        def norm2(i, which, post=None):
            return Norm(S, lambda k, s: col("norm_g_2", (i * 4 + which) * KD + k), post=post)

        class Residual:

            def __init__(self, T, scale, scales=None, n_scales=0):
                self.T, self.scale, self.scales, self.n_scales = T, scale, scales, n_scales
                self.n_s = T // S
                mem = Arena()
                self.sq, self.part, self.y0 = mem.take(KD, T), mem.take(KD, T), mem.take(T)
                self.order = [*range(1, KD), 0]

            def scalar(self, act, between=lambda: None):
                T = self.T
                for k in self.order:
                    if k == 0:
                        act.wait_ge(dve_step.sem, dve_step.at(1))
                    act.activation(self.sq[:, k, :], ps[:, k, 0:T] if k else self.y0, ACT.Square).then_inc(act_step.sem, 1)
                between()
                act.wait_ge(pe_step.sem, pe_step.at(1))
                act_chain.link(act, act.activation(rstd[:, 0:T], ps[:, 0, 0:T], ACT.Ln, scale=1.0 / D, bias=eps[:, 0:1]))
                act.activation(rstd[:, 0:T], rstd[:, 0:T], ACT.Exp, scale=-0.5).then_inc(act_step.sem, 1)

            def tensor(self, pe):
                pe.wait_ge(dve_step.sem, dve_step.at(1))
                for n, k in enumerate(self.order):
                    pe.wait_ge(act_step.sem, act_step.at(n + 1))
                    last = pe.matmul(ps[:, 0, 0:self.T], ones, self.sq[:, k, :], start=(n == 0), stop=(n == KD - 1))
                last.then_inc(pe_step.sem, 1)

            def vector(self, dve, between=lambda: None):
                T, n_s = self.T, self.n_s
                dve.tensor_copy(self.y0, ps[:, 0, 0:T]).then_inc(dve_step.sem, 1)
                if self.scales is not None:
                    self.scales(dve)
                between()
                dve.wait_ge(dve_step.sem, dve_step.at(1 + self.n_scales))
                dve.wait_ge(act_step.sem, act_step.at(KD + 1))
                for k in range(KD):
                    for s in range(n_s):
                        t = slice(s * S, (s + 1) * S)
                        dve.scalar_tensor_tensor(out=self.part[:, k, t], in0=ps[:, k, t] if k else self.y0[:, t], scalar=self.scale(k, s),
                                                 in1=rstd[:, t], op0=ALU.mult, op1=ALU.mult).then_inc(dve_step.sem, 1)
                    if k % 2:
                        dve.wait_ge(dve_step.sem, dve_step.at(1 + self.n_scales + n_s * (k + 1)))
                        dve.tensor_tensor(h[:, k, 0:T], h[:, k, 0:T], self.part[:, k, :], ALU.add).then_inc(h_updated.sem, 1)

            def gpsimd(self, pool):
                for k in range(0, KD, 2):
                    pool.wait_ge(dve_step.sem, dve_step.at(1 + self.n_scales + self.n_s * (k + 1)))
                    pool.tensor_tensor(h[:, k, 0:self.T], h[:, k, 0:self.T], self.part[:, k, :], ALU.add).then_inc(h_updated2.sem, 1)
                pool.wait_ge(h_updated2.sem, h_updated2.at(KD // 2))

            def done(self):
                act_step.passed(KD + 1)
                pe_step.passed(1)
                dve_step.passed(1 + self.n_scales + self.n_s * KD)
                h_updated.passed(KD // 2)
                h_updated2.passed(KD // 2)

        def residual1(l, i, gi, weight, T=T2):
            def scales(dve):
                dve.tensor_scalar(post_scale[:, :, :], mod[:, l, (i + 2) * KD:(i + 3) * KD, :], weight, None,
                                  ALU.mult).then_inc(dve_step.sem, 1)
                dve.wait_ge(dve_step.sem, dve_step.at(2))
                g = col("norm_g", (l * 6 + gi) * KD, KD)
                dve.tensor_tensor(post_scale[:, :, :], post_scale[:, :, :], g.unsqueeze(2).broadcast_to([P, KD, 2]),
                                  ALU.mult).then_inc(dve_step.sem, 1)
            return Residual(T, lambda k, s: post_scale[:, k, s:s + 1], scales, 2)

        def residual2(i, which):
            return Residual(S, lambda k, s: col("norm_g_2", (i * 4 + which) * KD + k))

        def residual(r):
            with stage() as block:
                @block.scalar
                def _(act):
                    r.scalar(act)

                @block.tensor
                def _(pe):
                    r.tensor(pe)

                @block.vector
                def _(dve):
                    r.vector(dve)

                @block.gpsimd
                def _(pool):
                    r.gpsimd(pool)
            r.done()

        MID = Arena()
        mid = MID.take(KF, T2)
        gates = MID.take(4, T2)
        ADA = Arena(ARENA - (KD + 1) * ADA_COLS)
        ada_slot = ADA.take(KD, ADA_COLS)
        ada_row = ADA.take(ADA_COLS)

        def pair_granule(k):
            raw = ring[k // 2][:, :].rearrange("p (k a f c) -> p k a f c", k=KD, a=2, f=2)[:, :, :, k % 2, :]
            return raw, lambda v: v[:, :].rearrange("p (k a c) -> p k a c", k=KD, a=2)

        def split_pairs(key, act=None, dve=None):
            def high_of(turn, k):
                raw, shaped = pair_granule(k)
                split_high(act, key, turn * 4 + k, k // 2, turn, raw, shaped, k % 2)

            def low_of(turn, k):
                raw, shaped = pair_granule(k)
                split_low(dve, turn * 4 + k, raw, shaped, k % 2)
            return high_of if act is not None else low_of

        def pair_products(pe, key, norm, free, ada=None):
            pairs = 4 if ada is None else 2
            def granule(turn, k):
                g = turn * 4 + k
                pe.wait_ge(split.sem, split.at(g + 1))
                pe.wait_ge(free.sem, free.at(g + 1 - pairs))
                if ada is not None:
                    ada.rows(pe, g)
                vh, vl = (v[k % 2][:, :].rearrange("p (k a c) -> p k a c", k=KD, a=2) for v in (wh, wl))
                T = norm.T
                for part in range(2):
                    last = multiply(pe, ps[:, 2 * (k % pairs) + part, 0:T],
                                    [((vh[:, kk, part, :], vl[:, kk, part, :]), (uh[:, kk, 0:T], ul[:, kk, 0:T])) for kk in range(KD)],
                                    before=norm.input_ready if k == 0 and part == 0 else None)
                last.then_inc(prod.sem, 1)
                if ada is not None:
                    ada.columns(pe, g)
            turns(pe, KF, 4, granule)

        def ahead(turn, k, lead=2):
            return (turn, k + lead) if k + lead < 4 else (turn + 1, k + lead - 4)

        def ffn_up(key, norm, bands_of=None, ada=None):
            T = norm.T
            pairs = 4 if ada is None else 2
            with stage() as block:
                @block.sync
                def _(sp):
                    stream(sp, key)

                @block.tensor
                def _(pe):
                    norm.tensor(pe)
                    pair_products(pe, key, norm, dve_free, ada)

                @block.scalar
                def _(act):
                    high_of = split_pairs(key, act=act)

                    def granule(turn, k, more):
                        g = turn * 4 + k
                        if ada is not None:
                            ada.scalar(act, g)
                        if more:
                            high_of(*ahead(turn, k))
                        act.wait_ge(prod.sem, prod.at(g + 1))
                        act.wait_ge(dve_free.sem, dve_free.at(g - 3))
                        act.activation(gates[:, k, 0:T], ps[:, 2 * (k % pairs), 0:T], ACT.Silu).then_inc(gate_done.sem, 1)
                    if ada is not None:
                        ada.load(act, *ada.tiles[0])
                    norm.scalar(act, lambda g: high_of(0, g))
                    with_lead(act, KF, 2, granule, most=Ada.LOOPED if ada is not None else KF)

                @block.vector
                def _(dve):
                    low_of = split_pairs(key, dve=dve)

                    def granule(turn, k, more):
                        g = turn * 4 + k
                        if more:
                            low_of(*ahead(turn, k))
                        dve.wait_ge(gate_done.sem, gate_done.at(g + 1))
                        dve.tensor_tensor(mid[:, ds(g, 1), 0:T].squeeze(1), gates[:, k, 0:T], ps[:, 2 * (k % pairs) + 1, 0:T],
                                          ALU.mult).then_inc(dve_free.sem, 1)
                        if ada is not None:
                            ada.vector(dve, g)
                    norm.vector(dve, lambda g: low_of(0, g))
                    with_lead(dve, KF, 2, granule)

                @block.gpsimd
                def _(pool):
                    norm.gpsimd(pool)
                    if bands_of is not None:
                        load_bands(pool, bands_of)
            norm.done()
            if ada is not None:
                ada.done()
            stage_done(key)
            dve_free.passed(KF)
            gate_done.passed(KF)
            if bands_of is not None:
                pool_step.passed(1)
                flip_load.passed(16)
                band_load.passed(16 * (2 + B_HEADS * ROWS))

        def ffn_down(key, x, T):
            w = plan[key]
            n = KF // 2
            with stage() as block:
                @block.sync
                def _(sp):
                    stream(sp, key)

                def views(g):
                    raw = ring[(g // 2) % RING][:, (g % 2) * HALF:(g % 2 + 1) * HALF]
                    c = (2 * g) % KD
                    return raw, x[:, 2 * g:2 * g + 2, 0:T], uh[:, c:c + 2, 0:T], ul[:, c:c + 2, 0:T]

                @block.scalar
                def _(act):
                    for g in range(n):
                        raw, of, to_h, _ = views(g)
                        tile_loaded(act, key, g // 4, (g // 2) % RING)
                        if g >= 2:
                            act.wait_ge(prod.sem, prod.at(g - 1))
                        act.activation(wh[g % 2][:, :], raw, ACT.Copy)
                        act.activation(to_h, of, ACT.Copy).then_inc(high.sem, 1)

                @block.vector
                def _(dve):
                    for g in range(n):
                        raw, of, to_h, to_l = views(g)
                        dve.wait_ge(high.sem, high.at(g + 1))
                        dve.tensor_tensor(wl[g % 2][:, :], raw, wh[g % 2][:, :], ALU.subtract)
                        dve.tensor_tensor(to_l, of, to_h, ALU.subtract).then_inc(split.sem, 1)

                @block.tensor
                def _(pe):
                    for g in range(n):
                        pe.wait_ge(split.sem, split.at(g + 1))
                        _, _, xh, xl = views(g)
                        for kk in range(2):
                            for j in range(KD):
                                c = slice(kk * D + j * P, kk * D + (j + 1) * P)
                                last = multiply(pe, ps[:, j, 0:T], [((wh[g % 2][:, c], wl[g % 2][:, c]), (xh[:, kk, :], xl[:, kk, :]))],
                                                start=(g == 0 and kk == 0), stop=(g == n - 1 and kk == 1))
                        last.then_inc(prod.sem, 1)
            stage_done(key)

        def wide(key, xh, xl, n_k, T):
            w = plan[key]
            G = HALF // (n_k * P)
            n = 2 * w.n
            with stage() as block:
                @block.sync
                def _(sp):
                    stream(sp, key)

                def granule(g):
                    raw = slot_view((g // 2) % RING, n_k, 2 * G * P)[:, :, (g % 2) * G * P:(g % 2 + 1) * G * P]
                    return raw, lambda v: v[:, :].rearrange("p (k c) -> p k c", k=n_k)

                @block.scalar
                def _(act):
                    for g in range(n):
                        split_high(act, key, g, (g // 2) % RING, g // 2 // RING, *granule(g), g % 2)

                @block.vector
                def _(dve):
                    for g in range(n):
                        split_low(dve, g, *granule(g), g % 2)

                @block.tensor
                def _(pe):
                    for g in range(n):
                        pe.wait_ge(split.sem, split.at(g + 1))
                        _, shaped = granule(g)
                        vh, vl = shaped(wh[g % 2]), shaped(wl[g % 2])
                        for m in range(G):
                            c = slice(m * P, (m + 1) * P)
                            last = multiply(pe, ps[:, g * G + m, 0:T], [((vh[:, kk, c], vl[:, kk, c]), (xh[:, kk, 0:T], xl[:, kk, 0:T]))
                                                                         for kk in range(n_k)])
                        last.then_inc(prod.sem, 1)
            stage_done(key)

        def listed(key, spans, items, norm):
            w = plan[key]
            widths = [sum(n for _, n in span) for span in spans]
            gran = [(i, q) for i in range(w.n) for q in range(w.count[i])]
            of_item = [gran.index((i, c0 // 256)) for i, c0, *_ in items]
            assert of_item == sorted(of_item)

            def granule(g):
                i, q = gran[g]
                n = min(256, widths[i] - 256 * q)
                raw = slot_view(i % RING, KD, widths[i])[:, :, 256 * q:256 * q + n]
                return raw, lambda v: v[:, 0:KD * n].rearrange("p (k c) -> p k c", k=KD)

            def steps(split_granule, take_items):
                for g in range(len(gran)):
                    if g + 2 < len(gran):
                        split_granule(g + 2)
                    take_items(g)

            with stage() as block:
                @block.sync
                def _(sp):
                    stream(sp, key)

                @block.tensor
                def _(pe):
                    norm.tensor(pe)
                    for g in range(len(gran)):
                        pe.wait_ge(split.sem, split.at(g + 1))
                        _, shaped = granule(g)
                        for n, (_, _, products, _) in enumerate(items):
                            if of_item[n] != g:
                                continue
                            free = (act_free, dve_free)[n % 2]
                            if n >= 8:
                                pe.wait_ge(free.sem, free.at(n // 2 - 3))
                            for to, terms in products(shaped(wh[g % 2]), shaped(wl[g % 2]), ps[:, n % 8, :]):
                                last = multiply(pe, to, terms, before=norm.input_ready if n == 0 else None)
                        last.then_inc(prod.sem, 1)

                def take(eng, odd, free, g):
                    for n, (_, _, _, taken) in enumerate(items):
                        if of_item[n] == g and n % 2 == odd:
                            eng.wait_ge(prod.sem, prod.at(g + 1))
                            to, of, scale = taken(ps[:, n % 8, :])
                            if odd:
                                eng.tensor_scalar(to, of, scale, None, ALU.mult).then_inc(free.sem, 1)
                            else:
                                eng.activation(to, of, ACT.Copy, scale=scale).then_inc(free.sem, 1)

                @block.scalar
                def _(act):
                    def split_one(g):
                        i = gran[g][0]
                        tile_loaded(act, key, i // RING, i % RING)
                        if g >= 2:
                            act.wait_ge(prod.sem, prod.at(g - 1))
                        raw, shaped = granule(g)
                        act.activation(shaped(wh[g % 2]), raw, ACT.Copy).then_inc(high.sem, 1)
                    norm.scalar(act, split_one)
                    steps(split_one, lambda g: take(act, 0, act_free, g))

                @block.vector
                def _(dve):
                    def split_one(g):
                        split_low(dve, g, *granule(g), g % 2)
                    norm.vector(dve, split_one)
                    steps(split_one, lambda g: take(dve, 1, dve_free, g))

                @block.gpsimd
                def _(pool):
                    norm.gpsimd(pool)
            norm.done()
            stage_done(key)
            act_free.passed((len(items) + 1) // 2)
            dve_free.passed(len(items) // 2)

        def chunk_item(tile, m, t0, t1, to, scale=1.0):
            def products(vh, vl, bank):
                c = slice((m % 2) * P, (m % 2 + 1) * P)
                return [(bank[:, 0:t1 - t0], [((vh[:, kk, c], vl[:, kk, c]), (uh[:, kk, t0:t1], ul[:, kk, t0:t1])) for kk in range(KD)])]
            return tile, m * P, products, lambda bank: (to, bank[:, 0:t1 - t0], scale)

        def token_item(tile, c0, n, tiles, to, scale=1.0):
            def products(vh, vl, bank):
                c = slice(c0 % 256, c0 % 256 + n)
                return [(bank[:, q * n:(q + 1) * n], [((uh[:, kk, t * P:(t + 1) * P], ul[:, kk, t * P:(t + 1) * P]),
                                                       (vh[:, kk, c], vl[:, kk, c])) for kk in range(KD)]) for q, t in enumerate(tiles)]
            return tile, c0, products, lambda bank: (to, bank[:, 0:n * len(tiles)].rearrange("p (t n) -> p t n", n=n)
                                                     if len(tiles) > 1 else bank[:, 0:n], scale)

        AM = Arena()
        qa = AM.take(3, T2)
        ka = AM.take(2, T2)
        qb = AM.take(3, T2)
        kb = AM.take(3, T2)
        va = AM.take(2 * ST, P)
        vb = AM.take(2 * ST, B_HEADS * HD)
        cx = AM.take(2, T2)
        cb = AM.take(2, T2)
        cc = AM.take(2, T2)
        SC = AM
        scores = SC.take(3, T2)
        probs = SC.take(3, T2)
        probs_t = SC.take(2, T2)
        conv_t = SC.take(2, T2)
        RB = Arena(MID.at)
        bands = RB.take(B_HEADS, ST * S)
        flip = RB.take(P)
        zero_rows = RB.take(B_HEADS * RPB_H * RPB_PAD // P + 1)
        assert RB.at <= ARENA - (KD + 1) * ADA_COLS and AM.at <= ARENA - B_HEADS * ST * S
        bias = Arena(ARENA - B_HEADS * ST * S).take(B_HEADS, ST, S)
        softs = sb("softs", [P, 12])

        def load_bands(pool, l):
            n = B_HEADS * RPB_H
            padded = a["padded"]
            pool.dma_start(flip, a["const"][:, CONST_W:CONST_W + P]).then_inc(flip_load.sem, 16)
            pool.memset(zero_rows, 0.0).then_inc(pool_step.sem, 1)
            pool.wait_ge(pool_step.sem, pool_step.at(1))
            pool.dma_start(padded, zero_rows).then_inc(band_load.sem, 16)
            pool.wait_ge(band_load.sem, band_load.at(16))
            middle = bass.AP(padded.tensor, GRID_W - WIN_C, [[RPB_PAD, n], [1, RPB_W]])
            pool.dma_start(middle, a["rpb"][l].rearrange("h r c -> (h r) c")).then_inc(band_load.sem, 16)
            pool.wait_ge(band_load.sem, band_load.at(32))
            for hh in range(B_HEADS):
                for r in range(ROWS):
                    at = (hh * RPB_H + WIN_R - 1 - r) * RPB_PAD
                    band = bass.AP(padded.tensor, at, [[1, GRID_W], [RPB_PAD, ROWS], [1, GRID_W]])
                    p0 = (r % 2) * GRID_W
                    to = bands[p0:p0 + GRID_W, hh, (r // 2) * S:(r // 2 + 1) * S].rearrange("p (r c) -> p r c", r=ROWS)
                    pool.dma_start(to, band).then_inc(band_load.sem, 16)
            pool.wait_ge(flip_load.sem, flip_load.at(16))
            pool.wait_ge(band_load.sem, band_load.at(16 * (2 + B_HEADS * ROWS)))

        def rel_bias():
            with stage() as block:
                @block.tensor
                def _(pe):
                    for hh in range(B_HEADS):
                        pe.matmul(ps[:, hh, :], flip, bands[:, hh, :], start=True, stop=True).then_inc(pe_step.sem, 1)

                @block.vector
                def _(dve):
                    for hh in range(B_HEADS):
                        dve.wait_ge(pe_step.sem, pe_step.at(hh + 1))
                        dve.tensor_tensor(bias[:, hh], ps[:, hh, :].rearrange("p (t k) -> p t k", t=ST),
                                          window.unsqueeze(1).broadcast_to([P, ST, S]), ALU.add)
            pe_step.passed(B_HEADS)

        def project(l, norm):
            key = ("in", l)
            last = l == DEPTH - 1
            T = S if last else T2
            items = []
            for m in range(3):
                items.append(chunk_item(0, m, 0, T, qa[:, m, 0:T]))
            for m in range(3):
                items.append(chunk_item(1, m, 0, T, qb[:, m, 0:T]))
            items.append(chunk_item(2, 0, 0, T2, ka[:, 0, :]))
            items.append(token_item(2, P, P, range(2 * ST), va))
            for m in range(3):
                items.append(chunk_item(3, m, 0, T2, kb[:, m, :]))
            for c0, n in ((0, 256), (256, 128)):
                for t in range(0, 2 * ST, 512 // n):
                    k = 512 // n
                    items.append(token_item(4, c0, n, range(t, t + k), vb[:, t:t + k, c0:c0 + n]))
            for m, to in enumerate((cx[:, 0], cx[:, 1], cb[:, 0], cb[:, 1])):
                items.append(chunk_item(5, m, 0, T, to[:, 0:T]))
            for m in range(2):
                items.append(chunk_item(6, m, 0, T, cc[:, m, 0:T]))
            listed(key, IN_SPANS, items, norm)

        def qk_norm(l):
            T = [S if l == DEPTH - 1 else T2] * 3 + [T2]
            xs = [qa[:, 0], qa[:, 1], qa[:, 2], ka[:, 0]]
            with stage() as block:
                @block.scalar
                def _(act):
                    for i in range(4):
                        act.activation(probs_t[:, i % 2, 0:T[i]] if i < 2 else scores[:, i % 2, 0:T[i]], xs[i][:, 0:T[i]],
                                       ACT.Square).then_inc(act_step.sem, 1)
                    for i in range(4):
                        act.wait_ge(pe_step.sem, pe_step.at(i + 1))
                        r = (probs if i < 2 else conv_t)[:, i % 2, 0:T[i]]
                        act_chain.link(act, act.activation(r, ps[:, i, 0:T[i]], ACT.Ln, scale=1.0 / HD, bias=eps[:, 0:1]))
                        act.activation(r, r, ACT.Exp, scale=-0.5).then_inc(act_step.sem, 1)
                    act.wait_ge(pe_step.sem, pe_step.at(9))
                    act.activation(ka[:, 1, :], ps[:, 0, :], ACT.Copy)

                @block.tensor
                def _(pe):
                    for i in range(4):
                        pe.wait_ge(act_step.sem, act_step.at(i + 1))
                        sq = (probs_t if i < 2 else scores)[:, i % 2, 0:T[i]]
                        pe.matmul(ps[:, i, 0:T[i]], mat("half_ones"), sq, start=True, stop=True).then_inc(pe_step.sem, 1)
                    for i in range(4):
                        pe.wait_ge(dve_step.sem, dve_step.at(i + 1))
                        pe.matmul(ps[:, 4 + i, 0:S], mat("rot"), xs[i][:, 0:S], start=True, stop=True).then_inc(pe_step.sem, 1)
                    pe.wait_ge(dve_step.sem, dve_step.at(16))
                    pe.matmul(ps[:, 0, :], mat("swap"), ka[:, 0, :], start=True, stop=True).then_inc(pe_step.sem, 1)

                @block.vector
                def _(dve):
                    for i in range(4):
                        dve.wait_ge(act_step.sem, act_step.at(5 + i))
                        r = (probs if i < 2 else conv_t)[:, i % 2, 0:T[i]]
                        gain = head_gain[:, 2 * l + (i == 3):2 * l + (i == 3) + 1]
                        dve.scalar_tensor_tensor(out=xs[i][:, 0:T[i]], in0=xs[i][:, 0:T[i]], scalar=gain, in1=r,
                                                 op0=ALU.mult, op1=ALU.mult).then_inc(dve_step.sem, 1)
                    for i in range(4):
                        dve.wait_ge(pe_step.sem, pe_step.at(5 + i))
                        turned = scores[:, i % 2, 0:S]
                        if i >= 1:
                            dve.wait_ge(dve_step.sem, dve_step.at(4 + 3 * i))
                        dve.tensor_tensor(turned, ps[:, 4 + i, 0:S], sin_t, ALU.mult).then_inc(dve_step.sem, 1)
                        dve.tensor_tensor(xs[i][:, 0:S], xs[i][:, 0:S], cos_t, ALU.mult).then_inc(dve_step.sem, 1)
                        dve.wait_ge(dve_step.sem, dve_step.at(4 + 3 * i + 2))
                        dve.tensor_tensor(xs[i][:, 0:S], xs[i][:, 0:S], turned, ALU.add).then_inc(dve_step.sem, 1)
            act_step.passed(8)
            pe_step.passed(9)
            dve_step.passed(16)

        def attention(l):
            last = l == DEPTH - 1
            units = []
            for hd in range(A_HEADS):
                b = HD * (hd % 2)
                kv = hd // (A_HEADS // A_KV)
                kt = ka[b:b + HD, 0 if kv == hd % 2 else 1, :]
                v = lambda t, kv=kv: va[:, t, kv * HD:(kv + 1) * HD]
                for t in range(ST):
                    units.append((qa[b:b + HD, hd // 2, t * P:(t + 1) * P], kt, 0, T2, None, v, hd // 2, b, t))
                    if not last:
                        tc = ST + t
                        units.append((qa[b:b + HD, hd // 2, tc * P:(tc + 1) * P], kt, S, T2, None, v, hd // 2, b, tc))
            for hd in range(B_HEADS):
                b = HD * (hd % 2)
                kt = kb[b:b + HD, hd // 2, :]
                v = lambda t, hd=hd: vb[:, t, hd * HD:(hd + 1) * HD]
                for t in range(ST):
                    units.append((qb[b:b + HD, hd // 2, t * P:(t + 1) * P], kt, 0, T2, bias[:, hd, t, :], v, 3 + hd // 2, b, t))
                    if not last:
                        tc = ST + t
                        units.append((qb[b:b + HD, hd // 2, tc * P:(tc + 1) * P], kt, S, T2, None, v, 3 + hd // 2, b, tc))
            n = len(units)
            scale = HD ** -0.5
            scored, softened, normed, turned_, moved, valued, taken, maxed = (
                pe_step, act_step, dve_step, prod, act_free, gate_done, dve_free, aux)
            soft = lambda what, i: softs[:, 3 * what + i % 3:3 * what + i % 3 + 1]
            with stage() as block:
                @block.tensor
                def _(pe):
                    for i in range(n + 3):
                        if i < n:
                            q, kt, k0, k1, bm, v, oc, b, t = units[i]
                            if i >= 4:
                                pe.wait_ge(softened.sem, softened.at(i - 3))
                            pe.matmul(ps[:, i % 4, 0:k1 - k0], q, kt[:, k0:k1], start=True, stop=True).then_inc(scored.sem, 1)
                        if 2 <= i <= n + 1:
                            j = i - 2
                            _, _, k0, k1, *_ = units[j]
                            pe.wait_ge(normed.sem, normed.at(j + 1))
                            if j >= 2:
                                pe.wait_ge(moved.sem, moved.at(j - 1))
                            for m in range((k1 - k0) // P):
                                tr = pe.transpose(ps[:, 4 + j % 2, m * P:(m + 1) * P], probs[:, j % 3, m * P:(m + 1) * P], ident)
                            tr.then_inc(turned_.sem, 1)
                        if i >= 3:
                            j = i - 3
                            _, _, k0, k1, _, v, oc, b, t = units[j]
                            pe.wait_ge(moved.sem, moved.at(j + 1))
                            if j >= 2:
                                pe.wait_ge(taken.sem, taken.at(j - 1))
                            m_n = (k1 - k0) // P
                            for m in range(m_n):
                                mm = pe.matmul(ps[b:b + HD, 6 + j % 2, 0:P], v(k0 // P + m), probs_t[:, j % 2, m * P:(m + 1) * P],
                                               start=(m == 0), stop=(m == m_n - 1))
                            mm.then_inc(valued.sem, 1)

                @block.scalar
                def _(act):
                    for i in range(n + 2):
                        if i < n:
                            _, _, k0, k1, bm, *_ = units[i]
                            act.wait_ge(maxed.sem, maxed.at(i + 1))
                            if i >= 3:
                                act.wait_ge(turned_.sem, turned_.at(i - 2))
                            of = scores[:, i % 3, 0:k1 - k0] if bm is not None else ps[:, i % 4, 0:k1 - k0]
                            act.activation(probs[:, i % 3, 0:k1 - k0], of, ACT.Exp, bias=soft(0, i),
                                           scale=1.0 if bm is not None else scale, accum_out=soft(1, i)).then_inc(softened.sem, 1)
                        if i >= 2:
                            j = i - 2
                            _, _, k0, k1, *_ = units[j]
                            act.wait_ge(turned_.sem, turned_.at(j + 1))
                            if j >= 2:
                                act.wait_ge(valued.sem, valued.at(j - 1))
                            act.activation(probs_t[:, j % 2, 0:k1 - k0], ps[:, 4 + j % 2, 0:k1 - k0], ACT.Copy).then_inc(moved.sem, 1)

                @block.vector
                def _(dve):
                    for i in range(n + 4):
                        if i < n:
                            _, _, k0, k1, bm, *_ = units[i]
                            N = k1 - k0
                            dve.wait_ge(scored.sem, scored.at(i + 1))
                            if i >= 3:
                                dve.wait_ge(softened.sem, softened.at(i - 2))
                            if bm is not None:
                                sc = scores[:, i % 3, 0:N]
                                dve.scalar_tensor_tensor(out=sc[:, 0:S], in0=ps[:, i % 4, 0:S], scalar=scale, in1=bm,
                                                         op0=ALU.mult, op1=ALU.add).then_inc(dve_chain.sem, 1)
                                dve.tensor_scalar(sc[:, S:N], ps[:, i % 4, S:N], scale, None, ALU.mult).then_inc(dve_chain.sem, 1)
                                dve_chain.n += 2
                                dve.wait_ge(dve_chain.sem, dve_chain.n)
                                dve_chain.link(dve, dve.tensor_reduce(soft(2, i), sc, AX_X, ALU.max))
                                dve.tensor_scalar(soft(0, i), soft(2, i), -1.0, None, ALU.mult).then_inc(maxed.sem, 1)
                            else:
                                dve_chain.link(dve, dve.tensor_reduce(soft(2, i), ps[:, i % 4, 0:N], AX_X, ALU.max))
                                dve.tensor_scalar(soft(0, i), soft(2, i), -scale, None, ALU.mult).then_inc(maxed.sem, 1)
                        if 1 <= i <= n:
                            j = i - 1
                            N = units[j][3] - units[j][2]
                            dve.wait_ge(softened.sem, softened.at(j + 1))
                            if j >= 3:
                                dve.wait_ge(normed.sem, normed.at(j - 2))
                            dve_chain.link(dve, dve.reciprocal(soft(3, j), soft(1, j)))
                            dve.tensor_scalar(probs[:, j % 3, 0:N], probs[:, j % 3, 0:N], soft(3, j), None,
                                              ALU.mult).then_inc(normed.sem, 1)
                        if i >= 4:
                            j = i - 4
                            *_, oc, b, t = units[j]
                            dve.wait_ge(valued.sem, valued.at(j + 1))
                            of = ps[b:b + HD, 6 + j % 2, 0:P]
                            oh, ol = (v[b:b + HD, oc, t * P:(t + 1) * P] for v in (uh, ul))
                            dve_chain.link(dve, dve.tensor_copy(oh, of))
                            dve.tensor_tensor(ol, of, oh, ALU.subtract).then_inc(taken.sem, 1)

                @block.gpsimd
                def _(pool):
                    link = lambda ins: pool_chain.link(pool, ins)
                    T = S if last else T2
                    for j in range(2):
                        tap = lambda w_: col("conv_w", (l * 3 + w_) * 2 + j)
                        z, y, t_ = cx[:, j, 0:T], conv_t[:, 0, 0:T], conv_t[:, 1, 0:T]
                        link(pool.tensor_tensor(z, cc[:, j, 0:T], z, ALU.mult))
                        link(pool.tensor_scalar(y, z, tap(1), None, ALU.mult))
                        link(pool.tensor_scalar(t_, z, tap(0), None, ALU.mult))
                        for s in range(T // S):
                            link(pool.tensor_tensor(y[:, s * S + 1:(s + 1) * S], y[:, s * S + 1:(s + 1) * S],
                                                    t_[:, s * S:(s + 1) * S - 1], ALU.add))
                        link(pool.tensor_scalar(t_, z, tap(2), None, ALU.mult))
                        for s in range(T // S):
                            link(pool.tensor_tensor(y[:, s * S:(s + 1) * S - 1], y[:, s * S:(s + 1) * S - 1],
                                                    t_[:, s * S + 1:(s + 1) * S], ALU.add))
                        link(pool.tensor_tensor(y, y, cb[:, j, 0:T], ALU.mult))
                        link(pool.tensor_copy(uh[:, 6 + j, 0:T], y))
                        link(pool.tensor_tensor(ul[:, 6 + j, 0:T], y, uh[:, 6 + j, 0:T], ALU.subtract))
            for s_ in (scored, softened, normed, turned_, moved, valued, taken, maxed):
                s_.passed(n)

        def finish():
            tokens = Arena().take(ST, D)
            with stage() as block:
                @block.tensor
                def _(pe):
                    for t in range(ST):
                        for half in range(2):
                            g = 2 * t + half
                            for m in range(4):
                                tr = pe.transpose(ps[:, g, m * P:(m + 1) * P], h[:, 4 * half + m, t * P:(t + 1) * P], ident)
                            tr.then_inc(pe_step.sem, 1)

                @block.vector
                def _(dve):
                    for g in range(2 * ST):
                        dve.wait_ge(pe_step.sem, pe_step.at(g + 1))
                        dve.tensor_copy(tokens[:, g // 2, (g % 2) * 512:(g % 2 + 1) * 512], ps[:, g, :]).then_inc(dve_step.sem, 1)

                @block.sync
                def _(sp):
                    for t in range(ST):
                        sp.wait_ge(dve_step.sem, dve_step.at(2 * t + 2))
                        sp.dma_start(out[0, t * P:(t + 1) * P, :], tokens[:, t, :]).then_inc(stored.sem, 16)
                    sp.wait_ge(stored.sem, stored.at(16 * ST))

        CF = Arena()
        mid2 = CF.take(KF, S)
        conv_buf = CF.take(4, 2, S)

        def ffn_up2(i, norm):
            key = ("up2", i)
            n_ch = 2 * KF
            with stage() as block:
                @block.sync
                def _(sp):
                    stream(sp, key)

                @block.tensor
                def _(pe):
                    norm.tensor(pe)
                    pair_products(pe, key, norm, dve_free)

                def channel(name, tap, part, g):
                    at = col_at[name] + (i * (3 if name == "ffn_conv_w" else 1) + tap) * n_ch + part * KF
                    return cols[:, ds(g + at, 1)]

                def before(turn, q):
                    return (turn, q - 1) if q else (turn - 1, 3)

                @block.scalar
                def _(act):
                    high_of = split_pairs(key, act=act)

                    def gelu(turn, q):
                        act.wait_ge(conv_done.sem, conv_done.at(turn * 4 + q + 1))
                        act.activation(conv_buf[:, q, 0, :], conv_buf[:, q, 0, :], ACT.Gelu_apprx_tanh).then_inc(gelu_done.sem, 1)

                    def granule(turn, q, more, first=False):
                        g = turn * 4 + q
                        if more:
                            high_of(*ahead(turn, q))
                        act.wait_ge(prod.sem, prod.at(g + 1))
                        act.wait_ge(dve_free.sem, dve_free.at(g - 3))
                        for part in range(2):
                            act.activation(conv_buf[:, q, part, :], ps[:, 2 * q + part, 0:S], ACT.Identity,
                                           bias=channel("ffn_conv_b", 0, part, g),
                                           scale=channel("ffn_conv_w", 1, part, g)).then_inc(gate_done.sem, 1)
                        if not first:
                            gelu(*before(turn, q))
                    norm.scalar(act, lambda g: high_of(0, g))
                    granule(0, 0, True, first=True)
                    with_lead(act, KF, 2, granule, 1)
                    gelu((KF - 1) // 4, (KF - 1) % 4)

                @block.vector
                def _(dve):
                    low_of = split_pairs(key, dve=dve)

                    def gated(turn, q):
                        g = turn * 4 + q
                        dve.wait_ge(gelu_done.sem, gelu_done.at(g + 1))
                        dve.wait_ge(conv_done.sem, conv_done.at(g + 1))
                        dve.tensor_tensor(mid2[:, ds(g, 1), :].squeeze(1), conv_buf[:, q, 0, :], conv_buf[:, q, 1, :],
                                          ALU.mult).then_inc(dve_free.sem, 1)

                    def granule(turn, q, more, first=False):
                        g = turn * 4 + q
                        if more:
                            low_of(*ahead(turn, q))
                        dve.wait_ge(gate_done.sem, gate_done.at(g * 2 + 2))
                        for tap, to, of in ((0, slice(1, S), slice(0, S - 1)), (2, slice(0, S - 1), slice(1, S))):
                            for part in range(2):
                                if tap == 2:
                                    dve.wait_ge(aux.sem, aux.at(g * 3 + 1 + part))
                                ins = dve.scalar_tensor_tensor(out=conv_buf[:, q, part, to], in0=ps[:, 2 * q + part, of],
                                                               scalar=channel("ffn_conv_w", tap, part, g),
                                                               in1=conv_buf[:, q, part, to], op0=ALU.mult, op1=ALU.add)
                                ins.then_inc(conv_done.sem if tap == 2 and part == 1 else aux.sem, 1)
                        if not first:
                            gated(*before(turn, q))
                    norm.vector(dve, lambda g: low_of(0, g))
                    granule(0, 0, True, first=True)
                    with_lead(dve, KF, 2, granule, 1)
                    gated((KF - 1) // 4, (KF - 1) % 4)

                @block.gpsimd
                def _(pool):
                    norm.gpsimd(pool)
            norm.done()
            stage_done(key)
            n = KF
            dve_free.passed(n)
            conv_done.passed(n)
            gate_done.passed(2 * n)
            gelu_done.passed(n)
            aux.passed(3 * n)

        def head_norm(base, n, per, gain, scratch, before=None, after=None):
            groups = n // per
            banks = groups // 2
            mem = Arena(scratch)
            sq = mem.take(n, S)
            rs = mem.take(groups, S)
            x = u32[:, base:base + n, :]
            xh, xl = (v[:, :, :].rearrange("p a b -> p (a b)").rearrange("p (a b) -> p a b", b=S)[:, base:base + n, :] for v in (uh, ul))
            pairs = range(n // 2)
            two = lambda v, q: v[:, 2 * q:2 * q + 2, :]
            with stage() as block:
                @block.scalar
                def _(act):
                    for of in (before, after):
                        if of is not None:
                            act.activation(of[1], of[1], of[0]).then_inc(gate_done.sem, 1)
                    for q in pairs:
                        if before is not None:
                            act.wait_ge(dve_step.sem, dve_step.at(q + 1))
                        act.activation(two(sq, q), two(x, q), ACT.Square).then_inc(act_step.sem, 1)
                    for b in range(banks):
                        act.wait_ge(pe_step.sem, pe_step.at(b + 1))
                        act.activation(two(rs, b), ps[:, b, :].rearrange("p (a b) -> p a b", a=2), ACT.Ln,
                                       scale=1.0 / (per * P), bias=eps[:, 0:1]).then_inc(act_chain.sem, 1)
                    act_chain.n += banks
                    act.wait_ge(act_chain.sem, act_chain.n)
                    for b in range(banks):
                        act.activation(two(rs, b), two(rs, b), ACT.Exp, scale=-0.5).then_inc(act_step.sem, 1)
                    for q in pairs:
                        act.wait_ge(aux.sem, aux.at(q + 1))
                        act.activation(two(xh, q), two(sq, q), ACT.Copy).then_inc(act_step.sem, 1)

                @block.tensor
                def _(pe):
                    for k in range(n):
                        pe.wait_ge(act_step.sem, act_step.at(k // 2 + 1))
                        g = k // per
                        last = pe.matmul(ps[:, g // 2, (g % 2) * S:(g % 2 + 1) * S], ones, sq[:, k, :], start=(k % per == 0), stop=(k % per == per - 1))
                        if k % (2 * per) == 2 * per - 1:
                            last.then_inc(pe_step.sem, 1)

                @block.vector
                def _(dve):
                    if before is not None:
                        dve.wait_ge(gate_done.sem, gate_done.at(1))
                        for q in pairs:
                            dve.tensor_tensor(two(x, q), two(x, q), two(before[1], q), ALU.mult).then_inc(dve_step.sem, 1)
                        dve.wait_ge(dve_step.sem, dve_step.at(n // 2))
                    lag = 2
                    for q in range(n // 2 + lag):
                        if q < n // 2:
                            for k in (2 * q, 2 * q + 1):
                                dve.wait_ge(act_step.sem, act_step.at(n // 2 + k // per // 2 + 1))
                                ins = dve.scalar_tensor_tensor(out=sq[:, k, :], in0=x[:, k, :], scalar=col(gain, k), in1=rs[:, k // per, :],
                                                               op0=ALU.mult, op1=ALU.mult)
                                if after is not None:
                                    ins.then_inc(dve_chain.sem, 1)
                            if after is not None:
                                dve_chain.n += 2
                                dve.wait_ge(dve_chain.sem, dve_chain.n)
                                ins = dve.tensor_tensor(two(sq, q), two(sq, q), two(after[1], q), ALU.mult)
                            ins.then_inc(aux.sem, 1)
                        if q >= lag:
                            dve.wait_ge(act_step.sem, act_step.at(n // 2 + banks + q - lag + 1))
                            dve.tensor_tensor(two(xl, q - lag), two(sq, q - lag), two(xh, q - lag), ALU.subtract)
            gate_done.passed((before is not None) + (after is not None))
            act_step.passed(n + banks)
            pe_step.passed(banks)
            dve_step.passed(n // 2 * (before is not None))
            aux.passed(n // 2)

        BM = Arena()
        z = h[:, :, S:T2]
        xbc = BM.take(12, S)
        mq = BM.take(ML_HEADS, S)
        mk = BM.take(ML_HEADS, S)
        mv = BM.take(ST, D)
        o_pre = BM.take(KD, S)
        gate_x = BM.take(ST, 64)
        soft = BM.take(ST, 64)
        dt = BM.take(ST, 32)
        dta = BM.take(ST, 32)
        ncs = BM.take(2, ST, SSD_HEADS)
        w_end = BM.take(2, SSD_HEADS)
        bcol = BM.take(6, ML_HEADS)
        HN_AT = BM.at
        SS = Arena(BM.at)
        xdt = ul32[:, :].rearrange("p (a b) -> p a b", b=D).rearrange("p (a b) c -> p a b c", a=2)
        xs_tok = SS.take(ST, D)
        b_tok = SS.take(ST, 2 * P)
        x_end = SS.take(2, D)
        state = SS.take(2, D)
        xbc_raw = Arena(BM.at).take(12, S)
        decays = x_end.rearrange("p a b -> p (a b)").rearrange("p (a b c) -> p a b c", a=2, b=8)
        cbt = xs_tok[:, 0, 0:512]
        carry = xs_tok[:, 1, :].rearrange("p (a b) -> p a b", a=2)
        FIRST = (0, ST - 1)
        tri = (mat("upto"), mat("from_"))
        tri_mask = (mat("mask_upto"), mat("mask_from"))
        mixed = u32

        def ab_project(norm):
            items = []
            for m in range(20):
                to = z[:, m, :] if m < 8 else xbc_raw[:, m - 8, :]
                items.append(chunk_item(m // 4, m % 4, 0, S, to))
            for m in range(8):
                items.append(chunk_item(5 + m // 4, m % 4, 0, S, mq[:, m, :]))
            for m in range(8):
                items.append(chunk_item(7 + m // 4, m % 4, 0, S, mk[:, m, :], scale=(D // ML_HEADS) ** -0.5))
            for q in range(4):
                items.append(token_item(9 + q // 2, (q % 2) * 256, 256, range(ST), mv[:, :, q * 256:(q + 1) * 256]))
            for m in range(8):
                items.append(chunk_item(11 + m // 4, m % 4, 0, S, o_pre[:, m, :]))
            items.append(token_item(13, 0, 64, range(ST), gate_x))
            listed("ab_in", AB_SPANS, items, norm)

        def ssd_conv():
            half = SSD_CONV // 2
            with stage() as block:
                @block.vector
                def _(dve):
                    link = lambda ins: dve_chain.link(dve, ins)
                    dve.tensor_tensor(gate_x, gate_x, gate_bias[:, :].unsqueeze(1).broadcast_to([P, ST, 64]), ALU.add).then_inc(dve_step.sem, 1)
                    for j0 in range(0, 12, 4):
                        for tap in [half] + [q for q in range(SSD_CONV) if q != half]:
                            s = tap - half
                            if s:
                                dve.wait_ge(dve_chain.sem, dve_chain.n)
                            for j in range(j0, j0 + 4):
                                w_ = col("ab_conv_w", tap * 12 + j)
                                x_, y_ = xbc_raw[:, j, :], xbc[:, j, :]
                                if s == 0:
                                    ins = dve.tensor_scalar(y_, x_, w_, col("ab_conv_b", j), ALU.mult, ALU.add)
                                else:
                                    to = slice(max(0, -s), S - max(0, s))
                                    of = slice(max(0, s), S - max(0, -s))
                                    ins = dve.scalar_tensor_tensor(out=y_[:, to], in0=x_[:, of], scalar=w_, in1=y_[:, to],
                                                                   op0=ALU.mult, op1=ALU.add)
                                if tap < SSD_CONV - 1:
                                    ins.then_inc(dve_chain.sem, 1)
                                else:
                                    ins.then_inc(dve_step.sem, 1)
                            if tap < SSD_CONV - 1:
                                dve_chain.n += 4
                    dve.wait_ge(act_step.sem, act_step.at(2))
                    link(dve.scalar_tensor_tensor(out=dt[:, :, :], in0=gate_x[:, :, 0:32], scalar=0.0, in1=soft[:, :, 0:32],
                                                  op0=ALU.max, op1=ALU.add))
                    link(dve.scalar_tensor_tensor(out=dta[:, :, :], in0=dt[:, :, :], scalar=-1.0,
                                                  in1=a_log[:, :].unsqueeze(1).broadcast_to([P, ST, 32]), op0=ALU.mult, op1=ALU.mult))
                    link(dve.scalar_tensor_tensor(out=gate_x[:, :, 48:64], in0=gate_x[:, :, 48:64], scalar=0.0,
                                                  in1=soft[:, :, 48:64], op0=ALU.min, op1=ALU.subtract))

                @block.scalar
                def _(act):
                    link = lambda ins: act_chain.link(act, ins)
                    act.activation(a_log[:, :], a_log[:, :], ACT.Exp).then_inc(act_step.sem, 1)
                    act.wait_ge(dve_step.sem, dve_step.at(1))
                    link(act.activation(soft, gate_x, ACT.Abs))
                    link(act.activation(soft, soft, ACT.Exp, scale=-1.0))
                    act.activation(soft, soft, ACT.Ln, bias=ones[:, 0:1]).then_inc(act_step.sem, 1)
                    for j in range(12):
                        act.wait_ge(dve_step.sem, dve_step.at(j + 2))
                        act.activation(xbc[:, j, :], xbc[:, j, :], ACT.Silu)
            act_step.passed(2)
            dve_step.passed(13)

        def ssd_prepare():
            with stage() as block:
                @block.tensor
                def _(pe):
                    for t in range(ST):
                        for q in range(2):
                            for m in range(4):
                                tr = pe.transpose(ps[:, 2 * t + q, m * P:(m + 1) * P], xbc[:, 4 * q + m, t * P:(t + 1) * P], ident)
                            tr.then_inc(pe_step.sem, 1)
                    for t in range(ST):
                        for g in range(2):
                            tr = pe.transpose(ps[:, 4, (2 * t + g) * P:(2 * t + g + 1) * P], xbc[:, 8 + g, t * P:(t + 1) * P], ident)
                    tr.then_inc(pe_step.sem, 1)
                    for d in range(2):
                        for t in range(ST):
                            o = (d * ST + t) * SSD_HEADS
                            pe.matmul(ps[:, 5, o:o + SSD_HEADS], tri[d], dta[:, t, d * SSD_HEADS:(d + 1) * SSD_HEADS], start=True, stop=True)
                    for t in range(ST):
                        mm = pe.matmul(ps[:, 5, 64 + t * 32:96 + t * 32], ones, dta[:, t, :], start=True, stop=True)
                    mm.then_inc(pe_step.sem, 1)
                    for t in range(ST):
                        for g in range(SSD_GROUPS):
                            o = (t * SSD_GROUPS + g) * P
                            mm = pe.matmul(ps[:, 6, o:o + P], xbc[:, 8 + g, t * P:(t + 1) * P], xbc[:, 10 + g, t * P:(t + 1) * P],
                                           start=True, stop=True)
                    mm.then_inc(pe_step.sem, 1)
                    pe.wait_ge(dve_step.sem, dve_step.at(10))
                    for d in range(2):
                        for g in range(SSD_GROUPS):
                            pe.matmul(ps[:, 2 * d + g, :], b_tok[:, FIRST[d], g * P:(g + 1) * P],
                                      x_end[:, d, g * 512:(g + 1) * 512], start=True, stop=True).then_inc(pe_step.sem, 1)

                @block.scalar
                def _(act):
                    for n in range(4):
                        act.wait_ge(pe_step.sem, pe_step.at(n + 1))
                        act.activation(xs_tok[:, n // 2, (n % 2) * 512:(n % 2 + 1) * 512], ps[:, n, :], ACT.Copy).then_inc(act_step.sem, 1)
                    act.wait_ge(pe_step.sem, pe_step.at(5))
                    act.activation(b_tok.rearrange("p a b -> p (a b)"), ps[:, 4, :], ACT.Copy).then_inc(act_step.sem, 1)
                    act.wait_ge(dve_step.sem, dve_step.at(3))
                    act.activation(w_end[:, :, :], w_end[:, :, :], ACT.Exp).then_inc(act_step.sem, 1)
                    for n in range(4):
                        act.wait_ge(pe_step.sem, pe_step.at(8 + n))
                        act.activation(state[:, n // 2, (n % 2) * 512:(n % 2 + 1) * 512], ps[:, n, :], ACT.Copy).then_inc(act_step.sem, 1)

                @block.vector
                def _(dve):
                    dve.wait_ge(pe_step.sem, pe_step.at(6))
                    dve.tensor_scalar(ncs.rearrange("p d t h -> p (d t h)"), ps[:, 5, 0:64], -1.0, None, ALU.mult).then_inc(dve_step.sem, 1)
                    dve.wait_ge(dve_step.sem, dve_step.at(1))
                    for d in range(2):
                        t = FIRST[d]
                        o = 64 + t * 32 + d * SSD_HEADS
                        dve.tensor_tensor(w_end[:, d, :], ps[:, 5, o:o + SSD_HEADS], ncs[:, d, t, :], ALU.add).then_inc(dve_step.sem, 1)
                    dve.wait_ge(act_step.sem, act_step.at(4))
                    for d in range(2):
                        for t in range(ST):
                            dve.tensor_tensor(xdt[:, d, t, :].rearrange("p (h e) -> p h e", e=HD),
                                              xs_tok[:, t, :].rearrange("p (h e) -> p h e", e=HD),
                                              dt[:, t, d * SSD_HEADS:(d + 1) * SSD_HEADS].unsqueeze(2).broadcast_to([P, SSD_HEADS, HD]),
                                              ALU.mult).then_inc(dve_step.sem, 1)
                    dve.wait_ge(act_step.sem, act_step.at(6))
                    dve.wait_ge(dve_step.sem, dve_step.at(7))
                    for d in range(2):
                        dve.tensor_tensor(x_end[:, d, :].rearrange("p (h e) -> p h e", e=HD),
                                          xdt[:, d, FIRST[d], :].rearrange("p (h e) -> p h e", e=HD),
                                          w_end[:, d, :].unsqueeze(2).broadcast_to([P, SSD_HEADS, HD]), ALU.mult).then_inc(dve_step.sem, 1)
                    dve.wait_ge(pe_step.sem, pe_step.at(7))
                    dve.tensor_copy(cbt, ps[:, 6, :]).then_inc(dve_step.sem, 1)
            pe_step.passed(11)
            act_step.passed(10)
            dve_step.passed(10)

        def ssd_scan():
            units = [(t, q) for t in range(ST) for q in range(4)]
            n = len(units)
            with stage() as block:
                @block.tensor
                def _(pe):
                    for i in range(n + 1):
                        if i < n:
                            t, q = units[i]
                            into = 1 - t
                            if i >= 2:
                                pe.wait_ge(act_step.sem, act_step.at(i - 1))
                            b0 = 3 * (i % 2)
                            for d in range(2):
                                for m in range(4):
                                    hh = d * SSD_HEADS + 4 * q + m
                                    o = m * P
                                    pe.matmul(ps[:, b0 + d, o:o + P], dta[:, t, hh:hh + 1].broadcast_to([P, P]), tri[d], start=True, stop=False)
                                    pe.matmul(ps[:, b0 + d, o:o + P], ident, tri_mask[d], start=False, stop=True)
                            d = 0 if t == 1 else 1
                            for m in range(4):
                                hh = d * SSD_HEADS + 4 * q + m
                                mm = pe.matmul(ps[:, b0 + 2, m * P:(m + 1) * P], dta[:, t, hh:hh + 1].broadcast_to([P, P]), tri[d],
                                               start=True, stop=True)
                            mm.then_inc(pe_step.sem, 1)
                        if i >= 1:
                            j = i - 1
                            t, q = units[j]
                            d_in = 0 if t == 1 else 1
                            pe.wait_ge(dve_step.sem, dve_step.at(j + 1))
                            if j >= 2:
                                pe.wait_ge(dve_free.sem, dve_free.at(j - 1))
                            for m in range(4):
                                c0 = (4 * q + m) * HD
                                b = HD * (m % 2)
                                to = ps[b:b + HD, 6 + j % 2, (m // 2) * P:(m // 2 + 1) * P]
                                for d in range(2):
                                    pe.matmul(to, xdt[:, d, t, c0:c0 + HD], decays[:, j % 2, 4 * d + m, :], start=(d == 0), stop=False)
                                mm = pe.matmul(to, state[:, d_in, c0:c0 + HD], carry[:, j % 2, m * P:(m + 1) * P], start=False, stop=True)
                            mm.then_inc(gate_done.sem, 1)

                @block.scalar
                def _(act):
                    for i in range(n):
                        t, q = units[i]
                        b0 = 3 * (i % 2)
                        act.wait_ge(pe_step.sem, pe_step.at(i + 1))
                        if i >= 2:
                            act.wait_ge(gate_done.sem, gate_done.at(i - 1))
                        for d in range(2):
                            for m in range(4):
                                hh = 4 * q + m
                                act.activation(decays[:, i % 2, 4 * d + m, :], ps[:, b0 + d, m * P:(m + 1) * P], ACT.Exp,
                                               bias=ncs[:, d, t, hh:hh + 1])
                        act.activation(carry[:, i % 2, :], ps[:, b0 + 2, :], ACT.Exp).then_inc(act_step.sem, 1)

                @block.vector
                def _(dve):
                    for i in range(n + 1):
                        if i < n:
                            t, q = units[i]
                            g = q // 2
                            dve.wait_ge(act_step.sem, act_step.at(i + 1))
                            o = (t * SSD_GROUPS + g) * P
                            dve.tensor_tensor(decays[:, i % 2, :, :], decays[:, i % 2, :, :],
                                              cbt[:, o:o + P].unsqueeze(1).broadcast_to([P, 8, P]), ALU.mult).then_inc(aux.sem, 1)
                            c4 = carry[:, i % 2, :].rearrange("p (m l) -> p m l", m=4)
                            dve.wait_ge(aux.sem, aux.at(i + 1))
                            dve.tensor_tensor(c4, c4, xbc[:, 10 + g, t * P:(t + 1) * P].unsqueeze(1).broadcast_to([P, 4, P]),
                                              ALU.mult).then_inc(dve_step.sem, 1)
                        if i >= 1:
                            j = i - 1
                            t, q = units[j]
                            dve.wait_ge(gate_done.sem, gate_done.at(j + 1))
                            for m in range(2):
                                c = 2 * q + m
                                ins = dve.scalar_tensor_tensor(out=mixed[:, c, t * P:(t + 1) * P], in0=xbc[:, c, t * P:(t + 1) * P],
                                                               scalar=d_skip[:, c:c + 1], in1=ps[:, 6 + j % 2, m * P:(m + 1) * P],
                                                               op0=ALU.mult, op1=ALU.add)
                            ins.then_inc(dve_free.sem, 1)
            pe_step.passed(n)
            act_step.passed(n)
            dve_step.passed(n)
            gate_done.passed(n)
            dve_free.passed(n)
            aux.passed(n)

        MM = Arena(HN_AT)
        k_tok = ul32[:, 0:ST * D].rearrange("p (a b) -> p a b", a=ST)
        IG, LF, FC, BB, MX, NM, FL, SI = [MM.take(2, S) for _ in range(8)]
        kwr = MM.take(2, P)
        wts = MM.take(2, 2, S)
        floors = MM.take(2, 2 * S)
        dens = LF
        nums = IG
        kws = MM.take(2, 2, P)
        cst = MM.take(2, 2 * P)
        qst = MM.take(2, 2, P)
        ml = sb("ml", [P, 8])
        nst = sb("nst", [P, 2, 2])

        def mlstm_prepare():
            H8 = ML_HEADS
            with stage() as block:
                @block.tensor
                def _(pe):
                    for kind, at in ((0, 32), (1, 48)):
                        for d in range(2):
                            for t in range(ST):
                                tr = pe.transpose(ps[0:H8, kind, (d * ST + t) * P:(d * ST + t + 1) * P],
                                                  gate_x[:, t, at + d * H8:at + (d + 1) * H8], ident)
                        tr.then_inc(pe_step.sem, 1)
                    for t in range(ST):
                        for q in range(2):
                            for m in range(4):
                                tr = pe.transpose(ps[:, 2 + 2 * t + q, m * P:(m + 1) * P], mk[:, 4 * q + m, t * P:(t + 1) * P], ident)
                            tr.then_inc(pe_step.sem, 1)
                    pe.wait_ge(dve_step.sem, dve_step.at(1))
                    for d in range(2):
                        for t in range(ST):
                            o = (d * ST + t) * H8
                            pe.transpose(ps[:, 6, o:o + H8], BB[0:H8, d, t * P:(t + 1) * P], ident[0:H8, 0:H8])
                    pe.wait_ge(act_step.sem, act_step.at(7))
                    for d in range(2):
                        tr = pe.transpose(ps[:, 6, (4 + d) * H8:(5 + d) * H8], kwr[0:H8, d, :], ident[0:H8, 0:H8])
                    tr.then_inc(pe_step.sem, 1)

                @block.scalar
                def _(act):
                    act.wait_ge(pe_step.sem, pe_step.at(1))
                    act.activation(IG[0:H8].rearrange("p a b -> p (a b)"), ps[0:H8, 0, :], ACT.Copy).then_inc(act_step.sem, 1)
                    for n in range(4):
                        act.wait_ge(pe_step.sem, pe_step.at(3 + n))
                        act.activation(k_tok[:, n // 2, (n % 2) * 512:(n % 2 + 1) * 512], ps[:, 2 + n, :], ACT.Copy).then_inc(act_step.sem, 1)
                    act.wait_ge(dve_step.sem, dve_step.at(2))
                    for d in range(2):
                        t = FIRST[d]
                        act.activation(kwr[0:H8, d, :], BB[0:H8, d, t * P:(t + 1) * P], ACT.Exp, bias=ml[0:H8, 2 + d:3 + d]).then_inc(act_step.sem, 1)
                    for d in range(2):
                        t = 1 - FIRST[d]
                        act.activation(SI[0:H8, d, t * P:(t + 1) * P], MX[0:H8, d, t * P:(t + 1) * P], ACT.Exp, scale=-1.0,
                                       bias=ml[0:H8, d:d + 1])
                    act.activation(FL[0:H8], FL[0:H8], ACT.Exp, scale=-1.0)

                @block.vector
                def _(dve):
                    link = lambda ins: dve_chain.link(dve, ins)
                    dve.wait_ge(pe_step.sem, pe_step.at(2))
                    link(dve.tensor_copy(LF[0:H8].rearrange("p a b -> p (a b)"), ps[0:H8, 1, :]))

                    def part(v, d, t):
                        s = v[0:H8, d, t * P:(t + 1) * P]
                        return s if d == 0 else s[:, ::-1]
                    one = ones[0:H8, :]
                    for d in range(2):
                        for t in range(ST):
                            link(dve.tensor_tensor_scan(part(FC, d, t), one, part(LF, d, t), 0.0, ALU.mult, ALU.add))
                    dve.wait_ge(act_step.sem, act_step.at(1))
                    link(dve.tensor_tensor(BB[0:H8], IG[0:H8], FC[0:H8], ALU.subtract))
                    for d in range(2):
                        t = FIRST[d]
                        b = part(BB, d, t)
                        link(dve.tensor_tensor_scan(part(MX, d, t), b, b, 0.0, ALU.max, ALU.max))
                        end = t * P + (P - 1 if d == 0 else 0)
                        link(dve.tensor_tensor(ml[0:H8, d:d + 1], FC[0:H8, d, end:end + 1], MX[0:H8, d, end:end + 1], ALU.add))
                        link(dve.tensor_scalar(ml[0:H8, 2 + d:3 + d], MX[0:H8, d, end:end + 1], -1.0, None, ALU.mult))
                        b = part(BB, d, 1 - t)
                        link(dve.tensor_tensor_scan(part(MX, d, 1 - t), b, b, ml[0:H8, d:d + 1], ALU.max, ALU.max))
                    dve.tensor_scalar(NM[0:H8], MX[0:H8], -1.0, None, ALU.mult).then_inc(dve_step.sem, 1)
                    dve.tensor_tensor(FL[0:H8], FC[0:H8], MX[0:H8], ALU.add).then_inc(dve_step.sem, 1)
                    dve.wait_ge(pe_step.sem, pe_step.at(7))
                    dve.tensor_copy(bcol.rearrange("p a b -> p (a b)"), ps[:, 6, 0:6 * H8])
            pe_step.passed(7)
            act_step.passed(7)
            dve_step.passed(2)

        def mlstm():
            H8 = ML_HEADS
            output, dens_ready = gate_done, act_free
            with stage() as block:
                @block.tensor
                def _(pe):
                    for i in range(H8 + 1):
                        if i < H8:
                            hh = i
                            sel = ident[0:H8, hh:hh + 1].broadcast_to([H8, P])
                            b0, b1 = (0, 1) if hh % 2 == 0 else (6, 7)
                            for t in range(ST):
                                pe.matmul(ps[:, b0, t * P:(t + 1) * P], mk[:, hh, t * P:(t + 1) * P], mq[:, hh, t * P:(t + 1) * P], start=True, stop=True)
                            for d in range(2):
                                t = 1 - FIRST[d]
                                pe.matmul(ps[:, b0, (2 + d) * P:(3 + d) * P], sel, SI[0:H8, d, t * P:(t + 1) * P], start=True, stop=True)
                            for d in range(2):
                                pe.matmul(ps[:, b1, d * S:(d + 1) * S], sel, NM[0:H8, d, :], start=True, stop=False)
                                mm = pe.matmul(ps[:, b1, d * S:(d + 1) * S], ident, tri_mask[d].unsqueeze(1).broadcast_to([P, ST, P]), start=False, stop=True)
                            mm.then_inc(pe_step.sem, 1)
                            if hh >= 1:
                                pe.wait_ge(act_step.sem, act_step.at(3 * hh))
                            mm = pe.matmul(ps[:, 2, :], sel, FL[0:H8, :, :], start=True, stop=True)
                            mm.then_inc(pe_step.sem, 1)
                            pe.wait_ge(dve_step.sem, dve_step.at(2 * hh + 1))
                            for d in range(2):
                                pe.matmul(ps[:, 3, d * P:(d + 1) * P], kws[:, hh % 2, d, :], mv[:, FIRST[d], hh * P:(hh + 1) * P], start=True, stop=True)
                                mm = pe.matmul(ps[:, 3, S + d:S + d + 1], kws[:, hh % 2, d, :], ones[:, 0:1], start=True, stop=True)
                            mm.then_inc(pe_step.sem, 1)
                        if i >= 1:
                            hh = i - 1
                            pe.wait_ge(dve_step.sem, dve_step.at(2 * hh + 2))
                            pe.wait_ge(act_step.sem, act_step.at(3 * hh + 3))
                            if hh >= 1:
                                pe.wait_ge(dve_free.sem, dve_free.at(hh))
                            for d in range(2):
                                for t in range(ST):
                                    o = (d * ST + t) * P
                                    wt = wts[:, hh % 2, d, t * P:(t + 1) * P]
                                    second = t != FIRST[d]
                                    pe.matmul(ps[:, 4, o:o + P], mv[:, t, hh * P:(hh + 1) * P], wt, start=True, stop=not second)
                                    if second:
                                        pe.matmul(ps[:, 4, o:o + P], cst[:, hh % 2, d * P:(d + 1) * P], qst[:, hh % 2, d, :], start=False, stop=True)
                                    mm = pe.matmul(ps[:, 5, o:o + P], ones, wt, start=True, stop=not second)
                                    if second:
                                        mm = pe.matmul(ps[:, 5, o:o + P], nst[:, hh % 2, d:d + 1].broadcast_to([P, P]), qst[:, hh % 2, d, :],
                                                       start=False, stop=True)
                            mm.then_inc(output.sem, 1)

                @block.scalar
                def _(act):
                    for i in range(H8 + 1):
                        if i < H8:
                            hh = i
                            b1 = 1 if hh % 2 == 0 else 7
                            act.wait_ge(pe_step.sem, pe_step.at(3 * hh + 1))
                            if hh >= 2:
                                act.wait_ge(output.sem, output.at(hh - 1))
                            for d in range(2):
                                for t in range(ST):
                                    ins = act.activation(wts[:, hh % 2, d, t * P:(t + 1) * P], ps[:, b1, (d * ST + t) * P:(d * ST + t + 1) * P],
                                                         ACT.Exp, bias=bcol[:, d * ST + t, hh:hh + 1])
                            ins.then_inc(act_step.sem, 1)
                            act.wait_ge(pe_step.sem, pe_step.at(3 * hh + 2))
                            if hh >= 2:
                                act.wait_ge(dve_free.sem, dve_free.at(hh - 1))
                            act.activation(floors[:, hh % 2, :], ps[:, 2, :], ACT.Copy).then_inc(act_step.sem, 1)
                            act.wait_ge(pe_step.sem, pe_step.at(3 * hh + 3))
                            act.activation(cst[:, hh % 2, :], ps[:, 3, 0:S], ACT.Copy)
                            act.activation(nst[:, hh % 2, :], ps[:, 3, S:S + 2], ACT.Copy).then_inc(act_step.sem, 1)
                        if i >= 1:
                            act.wait_ge(output.sem, output.at(i))
                            act.activation(dens.rearrange("p a b -> p (a b)"), ps[:, 5, :], ACT.Abs).then_inc(dens_ready.sem, 1)

                @block.vector
                def _(dve):
                    link = lambda ins: dve_chain.link(dve, ins)
                    flat = lambda v: v.rearrange("p a b -> p (a b)")

                    def scaled_keys(hh):
                        if hh >= 2:
                            dve.wait_ge(pe_step.sem, pe_step.at(3 * hh - 3))
                        for d in range(2):
                            ins = dve.tensor_scalar(kws[:, hh % 2, d, :], k_tok[:, FIRST[d], hh * P:(hh + 1) * P], bcol[:, 4 + d, hh:hh + 1], None, ALU.mult)
                        ins.then_inc(dve_step.sem, 1)

                    scaled_keys(0)
                    for i in range(H8 + 1):
                        if i < H8:
                            hh = i
                            b0 = 0 if hh % 2 == 0 else 6
                            dve.wait_ge(act_step.sem, act_step.at(3 * hh + 1))
                            dve.tensor_tensor(wts[:, hh % 2, :, :], wts[:, hh % 2, :, :],
                                              ps[:, b0, 0:S].unsqueeze(1).broadcast_to([P, 2, S]), ALU.mult)
                            for d in range(2):
                                t = 1 - FIRST[d]
                                ins = dve.tensor_tensor(qst[:, hh % 2, d, :], mq[:, hh, t * P:(t + 1) * P], ps[:, b0, (2 + d) * P:(3 + d) * P], ALU.mult)
                            ins.then_inc(dve_step.sem, 1)
                            if hh + 1 < H8:
                                scaled_keys(hh + 1)
                        if i >= 1:
                            hh = i - 1
                            dve.wait_ge(output.sem, output.at(hh + 1))
                            dve.wait_ge(dens_ready.sem, dens_ready.at(hh + 1))
                            link(dve.tensor_tensor(flat(dens), flat(dens), floors[:, hh % 2, :], ALU.max))
                            link(dve.reciprocal(flat(dens), flat(dens)))
                            link(dve.tensor_tensor(flat(nums), ps[:, 4, :], flat(dens), ALU.mult))
                            dve.tensor_tensor(mixed[:, KD + hh, :], nums[:, 0, :], nums[:, 1, :], ALU.add).then_inc(dve_free.sem, 1)
                            dve.wait_ge(dve_free.sem, dve_free.at(hh + 1))
            pe_step.passed(3 * H8)
            act_step.passed(3 * H8)
            dve_step.passed(2 * H8)
            output.passed(H8)
            dens_ready.passed(H8)
            dve_free.passed(H8)

        GM = Arena()
        gq = GM.take(GLA_HEADS, S)
        gk = GM.take(GLA_HEADS, S)
        gv = GM.take(ST, D)
        gr = h[:, :, S:T2]
        low = GM.take(ST, 32)
        low_t = GM.take(2, S)
        w2 = GM.take(2, 512)
        la = GM.take(2, GLA_HEADS, S)
        eb = GM.take(2, GLA_HEADS, S)
        qin = GM.take(2, GLA_HEADS, S)
        kout = GM.take(2, GLA_HEADS, S)
        kend_t = ul32[:, 0:2 * GLA_HEADS * ST * P].rearrange("p (a b) -> p a b", b=P)
        gst = GM.take(2, 3, 2 * P)
        restart = GM.take(2, S)
        N_CH = S // GLA_CHUNK
        dec = GM.take(2, GLA_HEADS, N_CH)
        GLA_SQ = GM.at

        def c_project(norm):
            items = []
            for m in range(4):
                items.append(chunk_item(0, m, 0, S, gq[:, m, :], scale=P ** -0.5))
            for m in range(4):
                items.append(chunk_item(1, m, 0, S, gk[:, m, :]))
            for q in range(4):
                items.append(token_item(2 + q // 2, (q % 2) * 256, 256, range(ST), gv[:, :, q * 256:(q + 1) * 256]))
            for m in range(8):
                items.append(chunk_item(4 + m // 4, m % 4, 0, S, gr[:, m, :]))
            items.append(token_item(6, 0, 32, range(ST), low))
            listed("c_in", C_SPANS, items, norm)

        def gla_prepare():
            flat = lambda v: v.rearrange("p a b c -> p (a b c)")
            with stage() as block:
                @block.sync
                def _(sp):
                    sp.dma_start(w2[0:GLA_RANK], a["c_gate_w2_2"][0].rearrange("i r c -> r i c")).then_inc(loaded.sem, 16)

                @block.gpsimd
                def _(pool):
                    pool_chain.link(pool, pool.memset(restart, 1.0))
                    pool.memset(restart[:, 0, 0::GLA_CHUNK], 0.0).then_inc(pool_step.sem, 1)
                    pool.memset(restart[:, 1, GLA_CHUNK - 1::GLA_CHUNK], 0.0).then_inc(pool_step.sem, 1)
                    pool.wait_ge(pool_step.sem, pool_step.at(2))

                @block.tensor
                def _(pe):
                    for d in range(2):
                        for t in range(ST):
                            tr = pe.transpose(ps[0:GLA_RANK, 0, (d * ST + t) * P:(d * ST + t + 1) * P],
                                              low[:, t, d * GLA_RANK:(d + 1) * GLA_RANK], ident)
                    tr.then_inc(pe_step.sem, 1)
                    pe.wait_ge(loaded.sem, loaded.at(16))
                    pe.wait_ge(act_step.sem, act_step.at(1))
                    for d in range(2):
                        for hh in range(GLA_HEADS):
                            mm = pe.matmul(ps[:, 1 + 2 * d + hh // 2, (hh % 2) * S:(hh % 2 + 1) * S],
                                           w2[0:GLA_RANK, d, hh * P:(hh + 1) * P], low_t[0:GLA_RANK, d, :], start=True, stop=True)
                            if hh % 2:
                                mm.then_inc(pe_step.sem, 1)
                    for n in range(4):
                        pe.wait_ge(dve_step.sem, dve_step.at(3 + n))
                        for m in range(4):
                            b = 4 * n + m
                            d, hh, t = b // 8, (b // 2) % 4, b % 2
                            tr = pe.transpose(ps[:, 4 + n if n < 4 else 0, m * P:(m + 1) * P], eb[:, d, hh, t * P:(t + 1) * P], ident)
                        tr.then_inc(pe_step.sem, 1)

                @block.scalar
                def _(act):
                    link = lambda ins: act_chain.link(act, ins)
                    act.wait_ge(pe_step.sem, pe_step.at(1))
                    act.activation(low_t[0:GLA_RANK].rearrange("p a b -> p (a b)"), ps[0:GLA_RANK, 0, :], ACT.Copy).then_inc(act_step.sem, 1)
                    act.wait_ge(dve_step.sem, dve_step.at(1))
                    link(act.activation(flat(eb), flat(la), ACT.Abs))
                    link(act.activation(flat(eb), flat(eb), ACT.Exp, scale=-1.0))
                    act.activation(flat(eb), flat(eb), ACT.Ln, bias=ones[:, 0:1]).then_inc(act_step.sem, 1)
                    act.wait_ge(dve_step.sem, dve_step.at(2))
                    act.activation(flat(qin), flat(la), ACT.Exp).then_inc(act_step.sem, 1)
                    act.activation(flat(kout), flat(la), ACT.Exp, scale=-1.0).then_inc(act_step.sem, 1)
                    for d in range(2):
                        end = la[:, d, :, (GLA_CHUNK - 1 if d == 0 else 0)::GLA_CHUNK]
                        act.activation(dec[:, d, :, :], end, ACT.Exp).then_inc(act_step.sem, 1)
                    for n in range(4):
                        act.wait_ge(pe_step.sem, pe_step.at(6 + n))
                        act.activation(kend_t[:, 4 * n:4 * n + 4, :].rearrange("p a b -> p (a b)"), ps[:, 4 + n, :], ACT.Copy)

                @block.vector
                def _(dve):
                    link = lambda ins: dve_chain.link(dve, ins)
                    for d in range(2):
                        for hh in range(GLA_HEADS):
                            dve.wait_ge(pe_step.sem, pe_step.at(2 + 2 * d + hh // 2))
                            ins = dve.tensor_scalar(la[:, d, hh, :], ps[:, 1 + 2 * d + hh // 2, (hh % 2) * S:(hh % 2 + 1) * S],
                                                    col("gate_b", d * GLA_HEADS + hh), None, ALU.add)
                            if d == 1 and hh == GLA_HEADS - 1:
                                ins.then_inc(dve_step.sem, 1)
                            else:
                                link(ins)
                    dve.wait_ge(act_step.sem, act_step.at(2))
                    dve.wait_ge(dve_step.sem, dve_step.at(1))
                    link(dve.scalar_tensor_tensor(out=flat(la), in0=flat(la), scalar=0.0, in1=flat(eb), op0=ALU.min, op1=ALU.subtract))
                    link(dve.tensor_scalar(flat(la), flat(la), 1.0 / GLA_TAU, None, ALU.mult))
                    dve.wait_ge(pool_step.sem, pool_step.at(2))
                    for d in range(2):
                        for hh in range(GLA_HEADS):
                            x_, r_ = la[:, d, hh, :], restart[:, d, :]
                            if d == 1:
                                x_, r_ = x_[:, ::-1], r_[:, ::-1]
                            ins = dve.tensor_tensor_scan(x_, r_, x_, 0.0, ALU.mult, ALU.add)
                            if d == 1 and hh == GLA_HEADS - 1:
                                ins.then_inc(dve_step.sem, 1)
                            else:
                                link(ins)
                    dve.wait_ge(act_step.sem, act_step.at(6))
                    for d in range(2):
                        link(dve.tensor_tensor(kout[:, d], kout[:, d], gk, ALU.mult))
                        for half in range(2):
                            v = kout[:, d, 2 * half:2 * half + 2, :].rearrange("p h (c l) -> p (h c) l", c=N_CH)
                            to = eb[:, d, 2 * half:2 * half + 2, :].rearrange("p h (c l) -> p (h c) l", c=N_CH)
                            by = dec[:, d, 2 * half:2 * half + 2, :].rearrange("p h c -> p (h c)")
                            dve.tensor_tensor(to, v, by.unsqueeze(2).broadcast_to([P, 2 * N_CH, GLA_CHUNK]), ALU.mult).then_inc(dve_step.sem, 1)
                    for d in range(2):
                        link(dve.tensor_tensor(qin[:, d], qin[:, d], gq, ALU.mult))
            loaded.passed(16)
            pool_step.passed(2)
            pe_step.passed(9)
            act_step.passed(6)
            dve_step.passed(6)

        def gla():
            att = eb
            masks = (mat("gla_upto"), mat("gla_from"))
            C = GLA_CHUNK

            def chunk_sum(d, c):
                return ps[:, 1 + 2 * d + c % 2, (c // 2) * 2 * P:(c // 2 + 1) * 2 * P]

            with stage() as block:
                @block.tensor
                def _(pe):
                    for hh in range(GLA_HEADS):
                        if hh >= 1:
                            pe.wait_ge(act_step.sem, act_step.at(hh))
                        for d in range(2):
                            for t in range(ST):
                                o = (d * ST + t) * P
                                mm = pe.matmul(ps[:, 0, o:o + P], kout[:, d, hh, t * P:(t + 1) * P], qin[:, d, hh, t * P:(t + 1) * P], start=True, stop=True)
                        mm.then_inc(pe_step.sem, 1)
                        for d in range(2):
                            for n in range(N_CH - 1):
                                c = n if d == 0 else N_CH - 1 - n
                                p0 = C * (c % 2)
                                mm = pe.matmul(chunk_sum(d, c),
                                               kend_t[p0:p0 + C, (d * GLA_HEADS + hh) * ST + c // 2, :],
                                               gv[p0:p0 + C, c // 2, hh * 2 * P:(hh + 1) * 2 * P], start=True, stop=True)
                        mm.then_inc(pe_step.sem, 1)
                        pe.wait_ge(dve_step.sem, dve_step.at(8 * hh + 8))
                        for m in range(2):
                            for t in range(ST):
                                o = (m * ST + t) * P
                                run = []
                                for d in range(2):
                                    run.append((ps[:, 5, o:o + P], gv[:, t, hh * 2 * P + m * P:hh * 2 * P + (m + 1) * P],
                                                att[:, d, hh, t * P:(t + 1) * P]))
                                for d in range(2):
                                    for c in (2 * t, 2 * t + 1):
                                        n = c if d == 0 else N_CH - 1 - c
                                        if n:
                                            run.append((ps[:, 5, o + (c % 2) * C:o + (c % 2 + 1) * C], gst[:, d, n - 1, m * P:(m + 1) * P],
                                                        qin[:, d, hh, c * C:(c + 1) * C]))
                                for i, (to, stat, mov) in enumerate(run):
                                    mm = pe.matmul(to, stat, mov, start=(i == 0), stop=(i == len(run) - 1), skip_group_check=True)
                        mm.then_inc(pe_step.sem, 1)

                @block.scalar
                def _(act):
                    for hh in range(GLA_HEADS):
                        act.wait_ge(pe_step.sem, pe_step.at(3 * hh + 3))
                        act.activation(u32[:, 2 * hh:2 * hh + 2, :], ps[:, 5, :].rearrange("p (a b) -> p a b", a=2), ACT.Copy).then_inc(act_step.sem, 1)

                @block.vector
                def _(dve):
                    for hh in range(GLA_HEADS):
                        dve.wait_ge(pe_step.sem, pe_step.at(3 * hh + 1))
                        for d in range(2):
                            v = ps[:, 0, d * S:(d + 1) * S].rearrange("p (t l) -> p t l", t=ST)
                            dve.tensor_tensor(att[:, d, hh, :].rearrange("p (t l) -> p t l", t=ST), v,
                                              masks[d].unsqueeze(1).broadcast_to([P, ST, P]), ALU.mult).then_inc(dve_step.sem, 1)
                        dve.wait_ge(pe_step.sem, pe_step.at(3 * hh + 2))
                        if hh >= 1:
                            dve.wait_ge(pe_step.sem, pe_step.at(3 * hh))
                        for n in range(N_CH - 1):
                            for d in range(2):
                                c = n if d == 0 else N_CH - 1 - n
                                new = chunk_sum(d, c)
                                if n == 0:
                                    dve.tensor_copy(gst[:, d, 0, :], new).then_inc(dve_step.sem, 1)
                                else:
                                    dve.wait_ge(dve_step.sem, dve_step.at(8 * hh + 2 + 2 * (n - 1) + d + 1))
                                    dve.scalar_tensor_tensor(out=gst[:, d, n, :], in0=gst[:, d, n - 1, :], scalar=dec[:, d, hh, c:c + 1],
                                                             in1=new, op0=ALU.mult, op1=ALU.add).then_inc(dve_step.sem, 1)
            pe_step.passed(3 * GLA_HEADS)
            act_step.passed(GLA_HEADS)
            dve_step.passed(8 * GLA_HEADS)

        def flat16(v):
            return v[:, :, :].rearrange("p a b -> p (a b)").rearrange("p (a b) -> p a b", b=S)

        program = [setup, modulation]
        tiles = [(l, t) for l in range(DEPTH) for t in range(N_MOD * D // ADA_COLS)][ADA_FIRST:]
        adas = {(0, 0): Ada(tiles[:KF]), (0, 1): Ada(tiles[KF:])}
        for l in range(DEPTH):
            T = S if l == DEPTH - 1 else T2
            before = residual1(l - 1, 6, 5, 0.5) if l else None
            program += [lambda l=l, r=before: ffn_up(("up", l, 0), norm1(l, 0, 0, post=r), l, adas.get((l, 0))),
                        lambda l=l: ffn_down(("down", l, 0), mid, T2),
                        lambda l=l: residual(residual1(l, 0, 1, 0.5)), rel_bias,
                        lambda l=l: project(l, norm1(l, 3, 2)), lambda l=l: qk_norm(l), lambda l=l: attention(l),
                        lambda l=l, T=T: wide(("o", l), uh, ul, KD, T),
                        lambda l=l, T=T: ffn_up(("up", l, 1), norm1(l, 6, 4, T, residual1(l, 3, 3, 1.0, T)),
                                                ada=adas.get((l, 1))),
                        lambda l=l, T=T: ffn_down(("down", l, 1), mid, T)]
        program += [lambda: ab_project(norm2(0, 0, residual1(DEPTH - 1, 6, 5, 0.5, S))),
                    ssd_conv, ssd_prepare, ssd_scan, mlstm_prepare, mlstm,
                    lambda: head_norm(0, KD, 4, "ssd_norm", HN_AT, before=(ACT.Silu, z)),
                    lambda: head_norm(KD, KD, 1, "mlstm_norm", HN_AT, before=(ACT.Sigmoid, o_pre)),
                    lambda: wide("ab_out", flat16(uh), flat16(ul), 2 * KD, S),
                    lambda: ffn_up2(0, norm2(0, 2, residual2(0, 1))), lambda: ffn_down(("down2", 0), mid2, S),
                    lambda: c_project(norm2(1, 0, residual2(0, 3))), gla_prepare, gla,
                    lambda: head_norm(0, KD, 2, "gla_norm", GLA_SQ, after=(ACT.Silu, gr)),
                    lambda: wide("c_out", flat16(uh), flat16(ul), KD, S),
                    lambda: ffn_up2(1, norm2(1, 2, residual2(1, 1))), lambda: ffn_down(("down2", 1), mid2, S),
                    lambda: residual(residual2(1, 3))]
        for step in program[:stop]:
            step()
        finish()


_INS = ['x', 'c', 'ctx', 'c_ctx', 'w_ada', 'b_ada', 'norm_g', 'w_in', 'qk_g', 'rpb', 'conv_w', 'w_o', 'ffn_wi', 'ffn_wo',
        'norm_g_2', 'ab_w_in_2', 'ab_conv_w_2', 'ab_conv_b_2', 'ab_dt_bias_2', 'ab_a_log_2', 'ab_d_skip_2',
        'ab_ssd_norm_2', 'ab_ig_bias_2', 'ab_fg_bias_2', 'ab_mlstm_norm_2', 'ab_w_out_2', 'c_w_in_2',
        'c_gate_w2_2', 'c_gate_b_2', 'c_norm_2', 'c_w_out_2', 'ffn_w_up_2', 'ffn_conv_w_2', 'ffn_conv_b_2',
        'ffn_w_down_2']


def kernel(**inputs):
    import numpy as _np
    import concourse.bacc as _bacc
    from concourse import mybir as _mybir
    from concourse.bass_utils import run_bass_kernel_spmd as _run

    nc = _bacc.Bacc("TRN2", target_bir_lowering=False, num_devices=1)
    arrays, aps = {}, {}
    for name in _INS + ["const"]:
        arr = constants() if name == "const" else _np.ascontiguousarray(inputs[name])
        arrays[f"in_{name}_dram"] = arr
        aps[name] = nc.dram_tensor(f"in_{name}_dram", arr.shape, _mybir.dt.from_np(arr.dtype), kind="ExternalInput").ap()
    n = (B_HEADS * RPB_H * RPB_PAD // P + 1) * P
    aps["padded"] = nc.dram_tensor("rpb_padded", (n,), F32, kind="Internal").ap().rearrange("(p n) -> p n", p=P)
    out = nc.dram_tensor("out_0_dram", (1, S, D), F32, kind="ExternalOutput").ap()
    two_blocks(nc, aps, out)
    r = _run(nc, [arrays], core_ids=[0])
    return r.results[0]["out_0_dram"]
```

```python
import math
from contextlib import ExitStack, contextmanager

import concourse.bass as bass
import numpy as np
from concourse import mybir

F32 = mybir.dt.float32
LN_EXP = "natural_log_exp_and_others"
F32R = mybir.dt.float32r
ACT = mybir.ActivationFunctionType
ALU = mybir.AluOpType
AX_X = mybir.AxisListType.X
ds = bass.ds

P = 128
D = 1024
KD = D // P
S = 256
T2 = 2 * S
ST = S // P
DEPTH = 2
HD = 64
GRID_W, WIN_R, WIN_C = 64, 8, 16
ROWS = S // GRID_W
A_HEADS, A_KV, B_HEADS = 6, 2, 6
FFN = 2816
KF = FFN // P
N_MOD = 9
EPS = 1e-6
NEG = -1e30
RPB_H, RPB_W = 2 * WIN_R - 1, 2 * WIN_C - 1
RPB_PAD = 2 * GRID_W - 1
SSD_HEADS, SSD_GROUPS, SSD_CONV = 16, 2, 5
ML_HEADS = 8
GLA_HEADS, GLA_RANK, GLA_TAU, GLA_CHUNK = 4, 16, 16.0, 64
BANK = 512
RING = 2
ARENA = 20240
SLOT = 4096
ADA_COLS = 384
ADA_FIRST = 6
HALF = SLOT // 2

CONSTS = ["ident", "ones", "half_ones", "upto", "from_", "mask_upto", "mask_from", "rot", "swap",
          "gla_upto", "gla_from"]


def constants():
    k = np.arange(P)[:, None]
    m = np.arange(P)[None, :]
    c = {
        "ident": k == m,
        "ones": k >= 0 * m,
        "half_ones": k // HD == m // HD,
        "upto": k <= m,
        "from_": k >= m,
        "mask_upto": np.where(k <= m, 0.0, NEG),
        "mask_from": np.where(k >= m, 0.0, NEG),
        "swap": k == (m + HD) % P,
        "gla_upto": (k <= m) & (k // GLA_CHUNK == m // GLA_CHUNK),
        "gla_from": (k >= m) & (k // GLA_CHUNK == m // GLA_CHUNK),
    }
    rot = np.zeros((P, P))
    half = (np.arange(P) // 16) % 2
    for j in range(P):
        if half[j] == 0:
            rot[j + 16, j] = -1.0
        else:
            rot[j - 16, j] = 1.0
    c["rot"] = rot
    freqs = HD // 4
    pos = np.arange(S)
    freq = (1.0 / (np.float32(10000.0) ** (np.arange(freqs, dtype=np.float32) / np.float32(freqs)))).astype(np.float32)
    axis = (np.arange(P) % HD) // 32
    f = np.arange(P) % 16
    where = np.where(axis[:, None] == 0, (pos // GRID_W)[None, :], (pos % GRID_W)[None, :]).astype(np.float32)
    ang = (where * freq[f][:, None]).astype(np.float32)
    q = np.arange(P) % GRID_W
    key = np.arange(S) % GRID_W
    start = np.clip(q - WIN_C // 2, 0, GRID_W - WIN_C)
    inside = (key[None, :] >= start[:, None]) & (key[None, :] < start[:, None] + WIN_C)
    parts = [np.asarray(c[n], np.float32) * np.ones((P, P), np.float32) for n in CONSTS]
    parts += [np.cos(ang), np.sin(ang), np.where(inside, 0.0, NEG)]
    parts += [(k // GRID_W == m // GRID_W) & (k % GRID_W + m % GRID_W == GRID_W - 1)]
    parts += [k % 32 == np.arange(2)[None, :]]
    return np.ascontiguousarray(np.concatenate([np.asarray(p, np.float32) for p in parts], axis=1))


CONST_W = len(CONSTS) * P + 3 * S


class Signal:

    def __init__(self, sem):
        self.sem = sem
        self.base = 0

    def at(self, n):
        return self.base + n

    def passed(self, n):
        self.base += n


class Chain:

    def __init__(self, sem):
        self.sem = sem
        self.n = 0

    def link(self, eng, ins):
        ins.then_inc(self.sem, 1)
        self.n += 1
        eng.wait_ge(self.sem, self.n)


def turns(eng, n, period, body, first=0, most=None):
    def item(turn, k):
        body(turn + (first + k) // period if first + k >= period else turn, (first + k) % period)

    full = min(n - first, n if most is None else most) // period
    if full >= 2:
        with eng.Fori(0, full) as turn:
            for k in range(period):
                item(turn, k)
    else:
        for turn in range(full):
            for k in range(period):
                item(turn, k)
    for k in range(n - first - full * period):
        item(full + k // period, k % period)


def two_blocks(nc, a, out, stop=None):
    ctx = ExitStack()
    with ctx:
        place = [(nc.sbuf_base + 31) // 32 * 32]

        def sb(name, shape, dt=F32, at=None):
            size = 4 * int(np.prod(shape[1:]))
            offset = place[0] if at is None else at
            if at is None:
                place[0] += (size + 31) // 32 * 32
            return nc.alloc_sbuf_tensor_at(name, shape, dt, offset=offset)

        def signal(name):
            return Signal(ctx.enter_context(nc.semaphore(name)))

        def chain(name):
            return Chain(ctx.enter_context(nc.semaphore(name)))

        ring = [sb(f"ring{i}", [P, SLOT]) for i in range(RING)]
        h = sb("h", [P, KD, T2])
        uh_at = place[0]
        uh = sb("uh", [P, KD, T2], F32R)
        ul_at = place[0]
        ul = sb("ul", [P, KD, T2], F32R)
        u32 = sb("u32", [P, 2 * KD, S], F32, at=uh_at)
        ul32 = sb("ul32", [P, KD * T2], F32, at=ul_at)
        wh = [sb(f"wh{i}", [P, HALF], F32R) for i in range(2)]
        wl = [sb(f"wl{i}", [P, HALF], F32R) for i in range(2)]
        arena = sb("arena", [P, ARENA])
        const = sb("const", [P, CONST_W])
        ps = ctx.enter_context(nc.psum_tensor("ps", [P, 8, BANK], F32))

        def mat(name):
            i = CONSTS.index(name)
            return const[:, i * P:(i + 1) * P]

        tables = len(CONSTS) * P
        cos_t = const[:, tables:tables + S]
        sin_t = const[:, tables + S:tables + 2 * S]
        window = const[:, tables + 2 * S:tables + 3 * S]
        ident, ones = mat("ident"), mat("ones")

        class Arena:

            def __init__(self, start=0):
                self.at = start

            def take(self, *shape):
                n = int(np.prod(shape))
                v = arena[:, self.at:self.at + n]
                self.at += n
                assert self.at <= ARENA, self.at
                if len(shape) == 2:
                    v = v.rearrange("p (a b) -> p a b", a=shape[0])
                if len(shape) == 3:
                    v = v.rearrange("p (a b c) -> p a b c", a=shape[0], b=shape[1])
                return v

        vectors = [("b_ada", a["b_ada"].rearrange("l (r p) -> (l r) p", p=P)),
                   ("c", a["c"].rearrange("l (r p) -> (l r) p", p=P)),
                   ("c_ctx", a["c_ctx"].rearrange("(r p) -> r p", p=P)),
                   ("norm_g", a["norm_g"].rearrange("l i (r p) -> (l i r) p", p=P)),
                   ("conv_w", a["conv_w"].rearrange("l i (r p) -> (l i r) p", p=P)),
                   ("norm_g_2", a["norm_g_2"].rearrange("l i (r p) -> (l i r) p", p=P)),
                   ("ab_conv_w", a["ab_conv_w_2"].rearrange("l i (r p) -> (l i r) p", p=P)),
                   ("ab_conv_b", a["ab_conv_b_2"].rearrange("l (r p) -> (l r) p", p=P)),
                   ("ssd_norm", a["ab_ssd_norm_2"].rearrange("l (r p) -> (l r) p", p=P)),
                   ("mlstm_norm", a["ab_mlstm_norm_2"].rearrange("l (r p) -> (l r) p", p=P)),
                   ("gate_b", a["c_gate_b_2"].rearrange("l i (r p) -> (l i r) p", p=P)),
                   ("gla_norm", a["c_norm_2"].rearrange("l (r p) -> (l r) p", p=P)),
                   ("ffn_conv_w", a["ffn_conv_w_2"].rearrange("l i (r p) -> (l i r) p", p=P)),
                   ("ffn_conv_b", a["ffn_conv_b_2"].rearrange("l (r p) -> (l r) p", p=P))]
        col_at, pieces, n_rows = {}, [], 0
        for name, v in vectors:
            col_at[name] = n_rows
            r = 0
            while r < v.shape[0]:
                m = min(v.shape[0] - r, P - n_rows % P)
                pieces.append((v[r:r + m, :], n_rows // P, n_rows % P, m))
                r += m
                n_rows += m
        row_tiles = [min(P, n_rows - P * t) for t in range((n_rows + P - 1) // P)]
        cols = sb("cols", [P, n_rows])
        head_gain = sb("head_gain", [P, DEPTH * 2])
        d_skip = sb("d_skip", [P, KD])
        gate_bias = sb("gate_bias", [P, 64])
        a_log = sb("a_log", [P, 2 * SSD_HEADS])
        mod = sb("mod", [P, DEPTH, N_MOD * KD, 2])
        pre_scale = sb("pre_scale", [P, KD, 2])
        post_scale = sb("post_scale", [P, KD, 2])
        rstd = sb("rstd", [P, T2])
        eps = sb("eps", [P, 1])
        act_c = sb("act_c", [P, KD, 32])
        pick = sb("pick", [P, 2])
        mod_rows = Arena(12288).take(2, ADA_COLS)

        def col(name, i, n=1):
            return cols[:, col_at[name] + i:col_at[name] + i + n]

        ready = [signal(f"slot{i}_loaded") for i in range(RING)]
        high = signal("high_parts_done")
        split = signal("granules_split")
        prod = signal("products_done")
        band_load = signal("bands_loaded")
        flip_load = signal("flip_loaded")
        act_free = signal("act_evacuated")
        dve_free = signal("dve_evacuated")
        gate_done = signal("gate_done")
        loaded = signal("inputs_loaded")
        stored = signal("stored")
        pe_step, act_step, dve_step, pool_step = (signal(f"{e}_step") for e in ("pe", "act", "dve", "pool"))
        aux = signal("second_dve_step")
        sum_ready, h_squared, h_updated, h_updated2, h_scaled, u_high, u_ready, gains = (signal(n) for n in (
            "norm_sum_ready", "h_squared", "h_updated_by_vector", "h_updated_by_gpsimd", "h_scaled",
            "input_high_parts", "input_ready", "gains_ready"))
        conv_done = signal("pair_convolved")
        ahead_high = signal("weights_high_ahead")
        gelu_done = signal("gelu_done")
        ada_loaded, ada_multiplied, ada_copied, ada_turned, ada_taken = (signal(n) for n in (
            "ada_tile_loaded", "ada_tile_multiplied", "ada_rows_copied", "ada_columns_made", "ada_columns_taken"))
        act_chain, dve_chain, pool_chain = chain("act_chain"), chain("dve_chain"), chain("pool_chain")

        def stage():
            return nc.Block(no_gpsimd_drain=True)

        class Weights:

            def __init__(self, n, loads, parts=1, count=None, split=True, looped=True, first=0):
                self.first = first
                self.n, self.loads, self.parts, self.split = n, loads, parts, split
                self.count = count or [2 if split else 1] * n
                self.looped = looped and count is None

            def slot(self, i):
                return (i + self.first) % RING

            def same_slot(self, slot, n):
                return [i for i in range(n) if self.slot(i) == slot]

        def column_tiles(w, k, width):
            v = w.rearrange("(k p) c -> p k c", p=P)

            def loads(i, slot):
                to = ring[slot][:, 0:k * width].rearrange("p (k c) -> p k c", k=k)
                return [(to, v[:, :, ds(i * width, width)])]
            return loads

        def pair_tiles(w, half, width):
            v = w.rearrange("(k p) c -> p k c", p=P)

            def loads(i, slot):
                to = ring[slot][:, 0:KD * 2 * width].rearrange("p (k c) -> p k c", k=KD)
                return [(to[:, :, 0:width], v[:, :, ds(i * width, width)]),
                        (to[:, :, width:2 * width], v[:, :, ds(i * width + half, width)])]
            return loads

        def listed_tiles(w, spans):
            v = w.rearrange("(k p) c -> p k c", p=P)

            def loads(i, slot):
                width = sum(n for _, n in spans[i])
                k = w.shape[0] // P
                to = ring[slot][:, 0:k * width].rearrange("p (k c) -> p k c", k=k)
                got, o = [], 0
                for c0, n in spans[i]:
                    got.append((to[:, :, o:o + n], v[:, :, c0:c0 + n]))
                    o += n
                return got
            return loads

        IN_SPANS = [[(0, 384)], [(384, 384)], [(768, 256)], [(1024, 384)], [(1408, 384)], [(1792, 512)], [(2304, 256)]]
        plan = {}
        order = []

        def planned(key, weights):
            plan[key] = weights
            order.append(key)

        def row_tiles_of(w, k):
            v = w.rearrange("(k p) c -> p k c", p=P)

            def loads(i, slot):
                n = min(4, k - 4 * i)
                return [(ring[slot][:, 0:n * D].rearrange("p (k c) -> p k c", k=n), v[:, 4 * i:4 * i + n, :])]
            return loads

        def granules(spans):
            return [(sum(n for _, n in span) + 255) // 256 for span in spans]

        planned("ada", Weights(ADA_FIRST, column_tiles(a["w_ada"][0], KD, ADA_COLS), split=False))
        for l in range(DEPTH):
            for f in range(2):
                if f == 1:
                    planned(("in", l), Weights(len(IN_SPANS), listed_tiles(a["w_in"][l], IN_SPANS), count=granules(IN_SPANS)))
                    planned(("o", l), Weights(2, column_tiles(a["w_o"][l], KD, 512)))
                planned(("up", l, f), Weights(KF // 2, pair_tiles(a["ffn_wi"][l, f], FFN, 256), parts=2))
                planned(("down", l, f), Weights((KF + 3) // 4, row_tiles_of(a["ffn_wo"][l, f], KF), count=[2] * 5 + [1], first=KF // 2 % RING))
        AB_SPANS = [[(512 * i, 512)] for i in range(5)] + [[(2592 + 512 * i, 512)] for i in range(8)] + [[(2560, 32), (6688, 32)]]
        planned("ab_in", Weights(len(AB_SPANS), listed_tiles(a["ab_w_in_2"][0], AB_SPANS), count=granules(AB_SPANS)))
        planned("ab_out", Weights(4, column_tiles(a["ab_w_out_2"][0], 2 * KD, 256)))
        planned(("up2", 0), Weights(KF // 2, pair_tiles(a["ffn_w_up_2"][0], FFN, 256), parts=2))
        planned(("down2", 0), Weights((KF + 3) // 4, row_tiles_of(a["ffn_w_down_2"][0], KF), count=[2] * 5 + [1], first=KF // 2 % RING))
        C_SPANS = [[(512 * i, 512)] for i in range(6)] + [[(3072, 32)]]
        planned("c_in", Weights(len(C_SPANS), listed_tiles(a["c_w_in_2"][0], C_SPANS), count=granules(C_SPANS)))
        planned("c_out", Weights(2, column_tiles(a["c_w_out_2"][0], KD, 512)))
        planned(("up2", 1), Weights(KF // 2, pair_tiles(a["ffn_w_up_2"][1], FFN, 256), parts=2))
        planned(("down2", 1), Weights((KF + 3) // 4, row_tiles_of(a["ffn_w_down_2"][1], KF), count=[2] * 5 + [1], first=KF // 2 % RING))

        def parts_of(w, i):
            return len(w.loads(i, 0)) if not w.looped else w.parts

        def load(sp, w, i, slot):
            for to, fr in w.loads(i, slot):
                sp.dma_start(to, fr).then_inc(ready[slot].sem, 16)

        def stream(sp, key):
            w = plan[key]
            gone = split if w.split else prod
            done = np.cumsum([0] + w.count)
            if w.looped:
                def next_tile(turn, k):
                    sp.wait_ge(gone.sem, gone.at((turn * RING + k + 1) * w.count[0]))
                    load(sp, w, (turn + 1) * RING + k, k)
                turns(sp, max(w.n - RING, 0), RING, next_tile)
            else:
                for i in range(RING, w.n):
                    sp.wait_ge(gone.sem, gone.at(int(done[i - RING + 1])))
                    load(sp, w, i, w.slot(i))
            at = order.index(key) + 1
            if at < len(order):
                following = plan[order[at]]
                last = {i: max(w.same_slot(following.slot(i), w.n)) for i in range(RING)}
                for i in sorted(range(RING), key=last.get):
                    sp.wait_ge(gone.sem, gone.at(int(done[last[i] + 1])))
                    load(sp, following, i, following.slot(i))

        def split_high(act, key, g, slot, tile_turn, raw, shape_of, b):
            tile_loaded(act, key, tile_turn, slot)
            act.wait_ge(prod.sem, prod.at(g - 1))
            act.activation(shape_of(wh[b]), raw, ACT.Copy).then_inc(high.sem, 1)

        def split_low(dve, g, raw, shape_of, b):
            dve.wait_ge(high.sem, high.at(g + 1))
            dve.tensor_tensor(shape_of(wl[b]), raw, shape_of(wh[b]), ALU.subtract).then_inc(split.sem, 1)

        def multiply(pe, to, terms, start=True, stop=True, before=None):
            for n, ((sh, sl), (mh, ml)) in enumerate(terms):
                if before is not None:
                    before(pe, n)
                last = n == len(terms) - 1
                pe.matmul(to, sh, mh, start=start and n == 0, stop=False)
                pe.matmul(to, sh, ml, start=False, stop=False)
                mm = pe.matmul(to, sl, mh, start=False, stop=stop and last)
            return mm

        def with_lead(eng, n, lead, body, first=0, most=None):
            turns(eng, n - lead, 4, lambda turn, k: body(turn, k, True), first, most)
            for g in range(n - lead, n):
                body(g // 4, g % 4, False)

        def tile_loaded(pe, key, turn, k):
            w = plan[key]
            if w.looped:
                pe.wait_ge(ready[k].sem, ready[k].at((turn + 1) * 16 * w.parts))
            else:
                i = turn * RING + k
                n = sum(parts_of(w, j) for j in w.same_slot(w.slot(i), i + 1))
                pe.wait_ge(ready[w.slot(i)].sem, ready[w.slot(i)].at(16 * n))

        def stage_done(key, times=1):
            w = plan[key]
            prod.passed(times * sum(w.count))
            if w.split:
                high.passed(times * sum(w.count))
                split.passed(times * sum(w.count))
            for k in range(RING):
                ready[k].passed(times * 16 * sum(parts_of(w, i) for i in w.same_slot(k, w.n)))

        @contextmanager
        def after(key):
            stage_done(key)
            yield
            stage_done(key, -1)

        def slot_view(k, n_k, width):
            return ring[k][:, 0:n_k * width].rearrange("p (k c) -> p k c", k=n_k)

        def setup():
            mem = Arena()
            rows = mem.take(len(row_tiles), P)
            tokens = mem.take(2 * ST, D)
            groups = len(row_tiles) + KD
            n_loads = 1 + 1 + len(pieces) + 2 * ST + 4 + 4
            with stage() as block:
                @block.sync
                def _(sp):
                    sp.dma_start(const[:, :], a["const"][:, 0:CONST_W]).then_inc(loaded.sem, 16)
                    sp.dma_start(pick[:, :], a["const"][:, CONST_W + P:CONST_W + P + 2]).then_inc(loaded.sem, 16)
                    for v, t, r, m in pieces:
                        sp.dma_start(rows[r:r + m, t, :], v).then_inc(loaded.sem, 16)
                    for t in range(ST):
                        sp.dma_start(tokens[:, t, :], a["x"][0, t * P:(t + 1) * P, :]).then_inc(loaded.sem, 16)
                        sp.dma_start(tokens[:, ST + t, :], a["ctx"][0, t * P:(t + 1) * P, :]).then_inc(loaded.sem, 16)
                    for half in range(2):
                        sp.dma_start(head_gain[half * HD:(half + 1) * HD, :],
                                     a["qk_g"].rearrange("l i d -> d (l i)"),
                                     allow_slow_non_contiguous=True).then_inc(loaded.sem, 16)
                        sp.dma_start(d_skip[half * HD:(half + 1) * HD, :],
                                     bass.AP(a["ab_d_skip_2"].tensor, half, [[0, HD], [2, KD]]),
                                     allow_slow_non_contiguous=True).then_inc(loaded.sem, 16)
                    for v, at, n in ((a["ab_dt_bias_2"], 0, 32), (a["ab_ig_bias_2"], 32, 16), (a["ab_fg_bias_2"], 48, 16)):
                        sp.dma_start(gate_bias[:, at:at + n], bass.AP(v.tensor, 0, [[0, P], [1, n]])).then_inc(loaded.sem, 16)
                    sp.dma_start(a_log[:, :], bass.AP(a["ab_a_log_2"].tensor, 0, [[0, P], [1, 32]])).then_inc(loaded.sem, 16)
                    for i in range(RING):
                        load(sp, plan[order[0]], i, i)

                @block.tensor
                def _(pe):
                    pe.wait_ge(loaded.sem, loaded.at(16 * n_loads))
                    for t, m in enumerate(row_tiles):
                        pe.transpose(ps[:, t % 8, 0:m], rows[0:m, t, :], ident[0:m, 0:m]).then_inc(prod.sem, 1)
                    for j in range(KD):
                        g = len(row_tiles) + j
                        if g >= 8:
                            pe.wait_ge(dve_free.sem, dve_free.at(g - 7))
                        for t in range(2 * ST):
                            last = pe.transpose(ps[:, g % 8, t * P:(t + 1) * P], tokens[:, t, j * P:(j + 1) * P], ident)
                        last.then_inc(prod.sem, 1)

                @block.gpsimd
                def _(pool):
                    pool.memset(act_c[:, :, :], 0.0).then_inc(pool_step.sem, 1)

                @block.vector
                def _(dve):
                    dve.memset(eps[:, :], EPS).then_inc(ada_taken.sem, 1)
                    for t, m in enumerate(row_tiles):
                        dve.wait_ge(prod.sem, prod.at(t + 1))
                        dve.tensor_copy(cols[:, t * P:t * P + m], ps[:, t % 8, 0:m]).then_inc(dve_free.sem, 1)
                    for j in range(KD):
                        g = len(row_tiles) + j
                        dve.wait_ge(prod.sem, prod.at(g + 1))
                        dve.tensor_copy(h[:, j, :], ps[:, g % 8, :]).then_inc(dve_free.sem, 1)

                @block.scalar
                def _(act):
                    act.wait_ge(dve_free.sem, dve_free.at(len(row_tiles)))
                    act.wait_ge(pool_step.sem, pool_step.at(1))
                    act.activation(act_c[:, :, 0], col("c", 0, KD), ACT.Silu).then_inc(act_free.sem, 1)
                    act.activation(act_c[:, :, 1], col("c_ctx", 0, KD), ACT.Silu).then_inc(act_free.sem, 1)
                    for _ in range(6):
                        act.nop().then_inc(act_free.sem, 1)
            prod.passed(groups)
            dve_free.passed(groups)
            act_free.passed(8)
            pool_step.passed(1)
            ada_taken.passed(1)
            loaded.passed(16 * n_loads)

        def ada_rows(pe, bank, weights):
            for kk in range(KD):
                q = 32 * (kk % 4)
                last = pe.matmul(ps[q:q + 32, bank, 0:ADA_COLS], act_c[:, kk, :], weights[:, kk, :], start=(kk < 4), stop=(kk >= 4))
            return last

        def ada_columns(pe, bank, rows):
            for m in range(ADA_COLS // P):
                last = pe.matmul(ps[:, bank, 2 * m:2 * m + 2], rows[:, m * P:(m + 1) * P], pick[:, :], start=True, stop=True)
            return last

        def ada_take(dve, bank, chunk):
            n = ADA_COLS // P
            return dve.tensor_tensor(mod[:, :, :, :].rearrange("p l c s -> p (l c) s")[:, ds(chunk, n), :],
                                     ps[:, bank, 0:2 * n].rearrange("p (a b) -> p a b", a=n),
                                     cols[:, ds(col_at["b_ada"] + chunk, n)].unsqueeze(2).broadcast_to([P, n, 2]), ALU.add)

        def modulation():
            key = "ada"
            w = plan[key]
            with stage() as block:
                @block.sync
                def _(sp):
                    stream(sp, key)

                @block.tensor
                def _(pe):
                    def rows(turn, k):
                        tile_loaded(pe, key, turn, k)
                        pe.wait_ge(act_free.sem, act_free.at(turn * 2 + k - 1))
                        ada_rows(pe, k, slot_view(k, KD, ADA_COLS)).then_inc(prod.sem, 1)

                    def columns(turn, k):
                        pe.wait_ge(act_free.sem, act_free.at(turn * 2 + k + 1))
                        pe.wait_ge(dve_free.sem, dve_free.at(turn * 2 + k - 1))
                        ada_columns(pe, 2 + k, mod_rows[:, k, :]).then_inc(pe_step.sem, 1)

                    def step(turn, k):
                        rows(turn if k == 0 else turn + 1, 1 - k)
                        columns(turn, k)
                    rows(0, 0)
                    turns(pe, w.n - 1, 2, step)
                    columns((w.n - 1) // 2, (w.n - 1) % 2)

                @block.scalar
                def _(act):
                    def tile(turn, k):
                        act.wait_ge(prod.sem, prod.at(turn * 2 + k + 1))
                        act.wait_ge(dve_free.sem, dve_free.at(turn * 2 + k - 1))
                        act.activation(mod_rows[:, k, :], ps[:, k, 0:ADA_COLS], ACT.Copy).then_inc(act_free.sem, 1)
                    turns(act, w.n, 2, tile)

                @block.vector
                def _(dve):
                    def tile(turn, k):
                        i = turn * 2 + k
                        dve.wait_ge(pe_step.sem, pe_step.at(i + 1))
                        ada_take(dve, 2 + k, i * (ADA_COLS // P)).then_inc(dve_free.sem, 1)
                    turns(dve, w.n, 2, tile)
            stage_done(key)
            act_free.passed(w.n)
            pe_step.passed(w.n)
            dve_free.passed(w.n)

        class Ada:
            LOOPED = 16
            ROW_BANK, COLUMN_BANK = 4, 5

            def __init__(self, tiles):
                self.tiles, self.n = tiles, len(tiles)
                layer, tile = tiles[0]
                self.chunk = layer * N_MOD * KD + tile * (ADA_COLS // P)

            def load(self, act, layer, tile):
                v = a["w_ada"][layer].rearrange("(k p) c -> p k c", p=P)
                act.dma_start(ada_slot, v[:, :, ds(tile * ADA_COLS, ADA_COLS)]).then_inc(ada_loaded.sem, 16)

            def has(self, g):
                return not isinstance(g, int) or g < self.n

            def scalar(self, act, g):
                if not self.has(g):
                    return
                act.wait_ge(ada_multiplied.sem, ada_multiplied.at(g + 1))
                act.activation(ada_row, ps[:, self.ROW_BANK, 0:ADA_COLS], ACT.Copy).then_inc(ada_copied.sem, 1)
                if not isinstance(g, int):
                    layer, tile = self.tiles[0]
                    self.load(act, layer, tile + 1 + g)
                elif g + 1 < self.n:
                    self.load(act, *self.tiles[g + 1])

            def rows(self, pe, g):
                if self.has(g):
                    pe.wait_ge(ada_loaded.sem, ada_loaded.at(16 * (g + 1)))
                    ada_rows(pe, self.ROW_BANK, ada_slot).then_inc(ada_multiplied.sem, 1)

            def columns(self, pe, g):
                if self.has(g):
                    pe.wait_ge(ada_copied.sem, ada_copied.at(g + 1))
                    pe.wait_ge(ada_taken.sem, ada_taken.at(g))
                    ada_columns(pe, self.COLUMN_BANK, ada_row).then_inc(ada_turned.sem, 1)

            def vector(self, dve, g):
                if self.has(g):
                    dve.wait_ge(ada_turned.sem, ada_turned.at(g + 1))
                    ada_take(dve, self.COLUMN_BANK, self.chunk + g * (ADA_COLS // P)).then_inc(ada_taken.sem, 1)

            def done(self):
                ada_loaded.passed(16 * self.n)
                for s_ in (ada_multiplied, ada_copied, ada_turned, ada_taken):
                    s_.passed(self.n)

        class Norm:

            def __init__(self, T, scale, shift=None, scales=None, n_scales=0, post=None):
                self.T, self.scale, self.shift, self.scales, self.n_scales = T, scale, shift, scales, n_scales
                self.post = post
                self.n_s = T // S
                mem = Arena()
                self.sq, self.scaled = mem.take(KD, T), mem.take(KD, T)
                self.parts = [(k, s, slice(s * S, (s + 1) * S)) for k in range(KD) for s in range(self.n_s)]

            def scalar(self, act, high_of):
                T = self.T
                if self.post is None:
                    act.preload_act_table_set(LN_EXP)
                if self.post is not None:
                    self.post.scalar(act, lambda: high_of(0))
                    high_of(1)
                for k in range(KD):
                    if self.post is not None:
                        if k % 2:
                            act.wait_ge(h_updated.sem, h_updated.at(k // 2 + 1))
                        else:
                            act.wait_ge(h_updated2.sem, h_updated2.at(k // 2 + 1))
                    act.activation(self.sq[:, k, :], h[:, k, 0:T], ACT.Square).then_inc(h_squared.sem, 1)
                if self.post is None:
                    high_of(0)
                act.wait_ge(sum_ready.sem, sum_ready.at(1))
                act_chain.link(act, act.activation(rstd[:, 0:T], ps[:, 0, 0:T], ACT.Ln, scale=1.0 / D, bias=eps[:, 0:1]))
                act.activation(rstd[:, 0:T], rstd[:, 0:T], ACT.Exp, scale=-0.5).then_inc(h_squared.sem, 1)
                for n, (k, s, t) in enumerate(self.parts):
                    act.wait_ge(h_scaled.sem, h_scaled.at(n + 1))
                    if self.shift is None:
                        ins = act.activation(uh[:, k, t], self.scaled[:, k, t], ACT.Copy)
                    else:
                        ins = act.activation(uh[:, k, t], self.scaled[:, k, t], ACT.Identity, bias=self.shift(k, s))
                    ins.then_inc(u_high.sem, 1)
                if self.post is None:
                    high_of(1)

            def tensor(self, pe):
                if self.post is not None:
                    self.post.tensor(pe)
                for k in range(KD):
                    pe.wait_ge(h_squared.sem, h_squared.at(k + 1))
                    last = pe.matmul(ps[:, 0, 0:self.T], ones, self.sq[:, k, :], start=(k == 0), stop=(k == KD - 1))
                last.then_inc(sum_ready.sem, 1)

            def vector(self, dve, low_of):
                if self.post is not None:
                    self.post.vector(dve, lambda: low_of(0))
                    low_of(1)
                if self.scales is not None:
                    self.scales(dve)
                    dve.wait_ge(gains.sem, gains.at(self.n_scales))
                if self.post is None:
                    low_of(0)
                dve.wait_ge(h_squared.sem, h_squared.at(KD + 1))
                lag = 2
                for n in range(len(self.parts) + lag):
                    if n < len(self.parts):
                        k, s, t = self.parts[n]
                        dve.scalar_tensor_tensor(out=self.scaled[:, k, t], in0=h[:, k, t], scalar=self.scale(k, s),
                                                 in1=rstd[:, t], op0=ALU.mult, op1=ALU.mult).then_inc(h_scaled.sem, 1)
                    if n >= lag:
                        k, s, t = self.parts[n - lag]
                        dve.wait_ge(u_high.sem, u_high.at(n - lag + 1))
                        if self.shift is None:
                            ins = dve.tensor_tensor(ul[:, k, t], self.scaled[:, k, t], uh[:, k, t], ALU.subtract)
                        else:
                            ins = dve.scalar_tensor_tensor(out=ul[:, k, t], in0=self.scaled[:, k, t], scalar=self.shift(k, s),
                                                           in1=uh[:, k, t], op0=ALU.add, op1=ALU.subtract)
                        ins.then_inc(u_ready.sem, 1)
                if self.post is None:
                    low_of(1)

            def gpsimd(self, pool):
                if self.post is not None:
                    self.post.gpsimd(pool)

            def input_ready(self, pe, k):
                pe.wait_ge(u_ready.sem, u_ready.at(self.n_s * (k + 1)))

            def done(self):
                h_squared.passed(KD + 1)
                sum_ready.passed(1)
                gains.passed(self.n_scales)
                for s_ in (h_scaled, u_high, u_ready):
                    s_.passed(len(self.parts))
                if self.post is not None:
                    self.post.done()

        def norm1(l, i, gi, T=T2, post=None):
            def scales(dve):
                dve.tensor_scalar(pre_scale[:, :, :], mod[:, l, (i + 1) * KD:(i + 2) * KD, :], 1.0, None,
                                  ALU.add).then_inc(gains.sem, 1)
                dve.wait_ge(gains.sem, gains.at(1))
                g = col("norm_g", (l * 6 + gi) * KD, KD)
                dve.tensor_tensor(pre_scale[:, :, :], pre_scale[:, :, :], g.unsqueeze(2).broadcast_to([P, KD, 2]),
                                  ALU.mult).then_inc(gains.sem, 1)
            return Norm(T, lambda k, s: pre_scale[:, k, s:s + 1], lambda k, s: mod[:, l, i * KD + k, s:s + 1],
                        scales, 2, post)

        def norm2(i, which, post=None):
            return Norm(S, lambda k, s: col("norm_g_2", (i * 4 + which) * KD + k), post=post)

        class Residual:

            def __init__(self, T, scale, scales=None, n_scales=0):
                self.T, self.scale, self.scales, self.n_scales = T, scale, scales, n_scales
                self.n_s = T // S
                mem = Arena()
                self.sq, self.part, self.y0 = mem.take(KD, T), mem.take(KD, T), mem.take(T)
                self.order = [*range(1, KD), 0]

            def scalar(self, act, between=lambda: None):
                T = self.T
                act.preload_act_table_set(LN_EXP)
                for k in self.order:
                    if k == 0:
                        act.wait_ge(dve_step.sem, dve_step.at(1))
                    act.activation(self.sq[:, k, :], ps[:, k, 0:T] if k else self.y0, ACT.Square).then_inc(act_step.sem, 1)
                between()
                act.wait_ge(pe_step.sem, pe_step.at(1))
                act_chain.link(act, act.activation(rstd[:, 0:T], ps[:, 0, 0:T], ACT.Ln, scale=1.0 / D, bias=eps[:, 0:1]))
                act.activation(rstd[:, 0:T], rstd[:, 0:T], ACT.Exp, scale=-0.5).then_inc(act_step.sem, 1)

            def tensor(self, pe):
                pe.wait_ge(dve_step.sem, dve_step.at(1))
                for n, k in enumerate(self.order):
                    pe.wait_ge(act_step.sem, act_step.at(n + 1))
                    last = pe.matmul(ps[:, 0, 0:self.T], ones, self.sq[:, k, :], start=(n == 0), stop=(n == KD - 1))
                last.then_inc(pe_step.sem, 1)

            def vector(self, dve, between=lambda: None):
                T, n_s = self.T, self.n_s
                dve.tensor_copy(self.y0, ps[:, 0, 0:T]).then_inc(dve_step.sem, 1)
                if self.scales is not None:
                    self.scales(dve)
                between()
                dve.wait_ge(dve_step.sem, dve_step.at(1 + self.n_scales))
                dve.wait_ge(act_step.sem, act_step.at(KD + 1))
                for k in range(KD):
                    for s in range(n_s):
                        t = slice(s * S, (s + 1) * S)
                        dve.scalar_tensor_tensor(out=self.part[:, k, t], in0=ps[:, k, t] if k else self.y0[:, t], scalar=self.scale(k, s),
                                                 in1=rstd[:, t], op0=ALU.mult, op1=ALU.mult).then_inc(dve_step.sem, 1)
                    if k % 2:
                        dve.wait_ge(dve_step.sem, dve_step.at(1 + self.n_scales + n_s * (k + 1)))
                        dve.tensor_tensor(h[:, k, 0:T], h[:, k, 0:T], self.part[:, k, :], ALU.add).then_inc(h_updated.sem, 1)

            def gpsimd(self, pool):
                for k in range(0, KD, 2):
                    pool.wait_ge(dve_step.sem, dve_step.at(1 + self.n_scales + self.n_s * (k + 1)))
                    pool.tensor_tensor(h[:, k, 0:self.T], h[:, k, 0:self.T], self.part[:, k, :], ALU.add).then_inc(h_updated2.sem, 1)
                pool.wait_ge(h_updated2.sem, h_updated2.at(KD // 2))

            def done(self):
                act_step.passed(KD + 1)
                pe_step.passed(1)
                dve_step.passed(1 + self.n_scales + self.n_s * KD)
                h_updated.passed(KD // 2)
                h_updated2.passed(KD // 2)

        def residual1(l, i, gi, weight, T=T2):
            def scales(dve):
                dve.tensor_scalar(post_scale[:, :, :], mod[:, l, (i + 2) * KD:(i + 3) * KD, :], weight, None,
                                  ALU.mult).then_inc(dve_step.sem, 1)
                dve.wait_ge(dve_step.sem, dve_step.at(2))
                g = col("norm_g", (l * 6 + gi) * KD, KD)
                dve.tensor_tensor(post_scale[:, :, :], post_scale[:, :, :], g.unsqueeze(2).broadcast_to([P, KD, 2]),
                                  ALU.mult).then_inc(dve_step.sem, 1)
            return Residual(T, lambda k, s: post_scale[:, k, s:s + 1], scales, 2)

        def residual2(i, which):
            return Residual(S, lambda k, s: col("norm_g_2", (i * 4 + which) * KD + k))

        def residual(r):
            with stage() as block:
                @block.scalar
                def _(act):
                    r.scalar(act)

                @block.tensor
                def _(pe):
                    r.tensor(pe)

                @block.vector
                def _(dve):
                    r.vector(dve)

                @block.gpsimd
                def _(pool):
                    r.gpsimd(pool)
            r.done()

        MID = Arena()
        mid = MID.take(KF, T2)
        gates = MID.take(4, T2)
        ADA = Arena(ARENA - (KD + 1) * ADA_COLS)
        ada_slot = ADA.take(KD, ADA_COLS)
        ada_row = ADA.take(ADA_COLS)

        class Down:

            def __init__(self, up_key, key, x, T, ada=None):
                self.up_key, self.key, self.x, self.T, self.ada = up_key, key, x, T, ada
                self.n = KF // 2

            def weights(self, g):
                return ring[plan[self.key].slot(g // 2)][:, (g % 2) * HALF:(g % 2 + 1) * HALF]

            def inputs(self, g):
                c = (2 * g) % KD
                return self.x[:, 2 * g:2 * g + 2, 0:self.T], uh[:, c:c + 2, 0:self.T], ul[:, c:c + 2, 0:self.T]

            def weights_high(self, act, g):
                tile_loaded(act, self.key, g // 2 // RING, (g // 2) % RING)
                act.wait_ge(prod.sem, prod.at(g - 1))
                return act.activation(wh[g % 2][:, :], self.weights(g), ACT.Copy)

            def weights_low(self, dve, g):
                return dve.tensor_tensor(wl[g % 2][:, :], self.weights(g), wh[g % 2][:, :], ALU.subtract)

            def high_ahead(self, act, g):
                with after(self.up_key):
                    self.weights_high(act, g).then_inc(ahead_high.sem, 1)

            def low_ahead(self, dve, g):
                dve.wait_ge(ahead_high.sem, ahead_high.at(g + 1))
                self.weights_low(dve, g)

            def input_high(self, act, g):
                with after(self.up_key):
                    if g < 2:
                        act.wait_ge(prod.sem, prod.at(0))
                    act.wait_ge(dve_free.sem, dve_free.at(2 * g + 2))
                    of, to_h, _ = self.inputs(g)
                    act.activation(to_h, of, ACT.Copy).then_inc(high.sem, 1)

            def input_low(self, dve, g):
                with after(self.up_key):
                    if g < 2:
                        dve.wait_ge(high.sem, high.at(g + 1))
                    of, to_h, to_l = self.inputs(g)
                    dve.tensor_tensor(to_l, of, to_h, ALU.subtract).then_inc(split.sem, 1)

            def scalar(self, act):
                self.input_high(act, 1)
                for g in range(2, self.n):
                    with after(self.up_key):
                        self.weights_high(act, g)
                    self.input_high(act, g)

            def vector(self, dve):
                self.input_low(dve, 1)
                for g in range(2, self.n):
                    with after(self.up_key):
                        dve.wait_ge(high.sem, high.at(g + 1))
                    self.weights_low(dve, g)
                    self.input_low(dve, g)

            def tensor(self, pe):
                left = {6: (dve_free, KF - 2), 0: (dve_free, KF - 1), 2: (dve_free, KF)}
                if self.ada is not None:
                    left[4] = (ada_taken, self.ada.n)
                with after(self.up_key):
                    for g in range(self.n):
                        pe.wait_ge(split.sem, split.at(g + 1))
                        _, xh, xl = self.inputs(g)
                        for kk in range(2):
                            for j in (6, 7, 0, 1, 4, 5, 2, 3):
                                if g == 0 and kk == 0 and j in left:
                                    sem, count = left[j]
                                    pe.wait_ge(sem.sem, sem.at(count))
                                c = slice(kk * D + j * P, kk * D + (j + 1) * P)
                                last = multiply(pe, ps[:, j, 0:self.T], [((wh[g % 2][:, c], wl[g % 2][:, c]), (xh[:, kk, :], xl[:, kk, :]))],
                                                start=(g == 0 and kk == 0), stop=(g == self.n - 1 and kk == 1))
                        last.then_inc(prod.sem, 1)

            def sync(self, sp):
                with after(self.up_key):
                    stream(sp, self.key)

            def done(self):
                stage_done(self.key)
                ahead_high.passed(2)

        def pair_granule(k):
            raw = ring[k // 2][:, :].rearrange("p (k a f c) -> p k a f c", k=KD, a=2, f=2)[:, :, :, k % 2, :]
            return raw, lambda v: v[:, :].rearrange("p (k a c) -> p k a c", k=KD, a=2)

        def split_pairs(key, act=None, dve=None):
            def high_of(turn, k):
                raw, shaped = pair_granule(k)
                split_high(act, key, turn * 4 + k, k // 2, turn, raw, shaped, k % 2)

            def low_of(turn, k):
                raw, shaped = pair_granule(k)
                split_low(dve, turn * 4 + k, raw, shaped, k % 2)
            return high_of if act is not None else low_of

        def pair_products(pe, key, norm, free, ada=None):
            pairs = 4 if ada is None else 2
            def granule(turn, k):
                g = turn * 4 + k
                pe.wait_ge(split.sem, split.at(g + 1))
                pe.wait_ge(free.sem, free.at(g + 1 - pairs))
                if ada is not None:
                    ada.rows(pe, g)
                vh, vl = (v[k % 2][:, :].rearrange("p (k a c) -> p k a c", k=KD, a=2) for v in (wh, wl))
                T = norm.T
                for part in range(2):
                    last = multiply(pe, ps[:, 2 * (k % pairs) + part, 0:T],
                                    [((vh[:, kk, part, :], vl[:, kk, part, :]), (uh[:, kk, 0:T], ul[:, kk, 0:T])) for kk in range(KD)],
                                    before=norm.input_ready if k == 0 and part == 0 else None)
                last.then_inc(prod.sem, 1)
                if ada is not None:
                    ada.columns(pe, g)
            turns(pe, KF, 4, granule)

        def ahead(turn, k, lead=2):
            return (turn, k + lead) if k + lead < 4 else (turn + 1, k + lead - 4)

        def ffn1(l, f, norm, bands_of=None, ada=None):
            T = norm.T
            key = ("up", l, f)
            down = Down(key, ("down", l, f), mid, T, ada)
            pairs = 4 if ada is None else 2
            with stage() as block:
                @block.sync
                def _(sp):
                    stream(sp, key)
                    down.sync(sp)

                @block.tensor
                def _(pe):
                    norm.tensor(pe)
                    pair_products(pe, key, norm, dve_free, ada)
                    down.tensor(pe)

                @block.scalar
                def _(act):
                    high_of = split_pairs(key, act=act)

                    def granule(turn, k, more):
                        g = turn * 4 + k
                        if ada is not None:
                            ada.scalar(act, g)
                        if more:
                            high_of(*ahead(turn, k))
                        else:
                            if g == KF - 1:
                                down.input_high(act, 0)
                            down.high_ahead(act, g - (KF - 2))
                        act.wait_ge(prod.sem, prod.at(g + 1))
                        act.wait_ge(dve_free.sem, dve_free.at(g - 3))
                        act.activation(gates[:, k, 0:T], ps[:, 2 * (k % pairs), 0:T], ACT.Silu).then_inc(gate_done.sem, 1)
                    if ada is not None:
                        ada.load(act, *ada.tiles[0])
                    norm.scalar(act, lambda g: high_of(0, g))
                    with_lead(act, KF, 2, granule, most=Ada.LOOPED if ada is not None else KF)
                    down.scalar(act)

                @block.vector
                def _(dve):
                    low_of = split_pairs(key, dve=dve)

                    def granule(turn, k, more):
                        g = turn * 4 + k
                        if more:
                            low_of(*ahead(turn, k))
                        else:
                            if g == KF - 1:
                                down.input_low(dve, 0)
                            down.low_ahead(dve, g - (KF - 2))
                        dve.wait_ge(gate_done.sem, gate_done.at(g + 1))
                        dve.tensor_tensor(mid[:, ds(g, 1), 0:T].squeeze(1), gates[:, k, 0:T], ps[:, 2 * (k % pairs) + 1, 0:T],
                                          ALU.mult).then_inc(dve_free.sem, 1)
                        if ada is not None:
                            ada.vector(dve, g)
                    norm.vector(dve, lambda g: low_of(0, g))
                    with_lead(dve, KF, 2, granule)
                    down.vector(dve)

                @block.gpsimd
                def _(pool):
                    norm.gpsimd(pool)
                    if bands_of is not None:
                        load_bands(pool, bands_of)
            norm.done()
            if ada is not None:
                ada.done()
            stage_done(key)
            down.done()
            dve_free.passed(KF)
            gate_done.passed(KF)
            if bands_of is not None:
                pool_step.passed(1)
                flip_load.passed(16)
                band_load.passed(16 * (2 + B_HEADS * ROWS))

        class Wide:

            def __init__(self, key, xh, xl, n_k, T, input_ready=None):
                self.key, self.xh, self.xl, self.n_k, self.T, self.input_ready = key, xh, xl, n_k, T, input_ready
                self.G = HALF // (n_k * P)
                self.n = 2 * plan[key].n

            def granule(self, g):
                w = self.G * P
                raw = slot_view((g // 2) % RING, self.n_k, 2 * w)[:, :, (g % 2) * w:(g % 2 + 1) * w]
                return raw, lambda v: v[:, :].rearrange("p (k c) -> p k c", k=self.n_k)

            def high(self, act, g):
                split_high(act, self.key, g, (g // 2) % RING, g // 2 // RING, *self.granule(g), g % 2)

            def low(self, dve, g):
                split_low(dve, g, *self.granule(g), g % 2)

            def tensor(self, pe):
                for g in range(self.n):
                    pe.wait_ge(split.sem, split.at(g + 1))
                    _, shaped = self.granule(g)
                    vh, vl = shaped(wh[g % 2]), shaped(wl[g % 2])
                    for m in range(self.G):
                        c = slice(m * P, (m + 1) * P)
                        last = multiply(pe, ps[:, g * self.G + m, 0:self.T],
                                        [((vh[:, kk, c], vl[:, kk, c]), (self.xh[:, kk, 0:self.T], self.xl[:, kk, 0:self.T]))
                                         for kk in range(self.n_k)], before=self.input_ready if g == 0 and m == 0 else None)
                    last.then_inc(prod.sem, 1)

        def wide(w):
            with stage() as block:
                @block.sync
                def _(sp):
                    stream(sp, w.key)

                @block.scalar
                def _(act):
                    for g in range(w.n):
                        w.high(act, g)

                @block.vector
                def _(dve):
                    for g in range(w.n):
                        w.low(dve, g)

                @block.tensor
                def _(pe):
                    w.tensor(pe)
            stage_done(w.key)

        def listed(key, spans, items, norm, beside=None):
            w = plan[key]
            widths = [sum(n for _, n in span) for span in spans]
            gran = [(i, q) for i in range(w.n) for q in range(w.count[i])]
            of_item = [gran.index((i, c0 // 256)) for i, c0, *_ in items]
            assert of_item == sorted(of_item)

            def granule(g):
                i, q = gran[g]
                n = min(256, widths[i] - 256 * q)
                raw = slot_view(i % RING, KD, widths[i])[:, :, 256 * q:256 * q + n]
                return raw, lambda v: v[:, 0:KD * n].rearrange("p (k c) -> p k c", k=KD)

            def steps(split_granule, take_items, then):
                for g in range(len(gran)):
                    if g + 2 < len(gran):
                        split_granule(g + 2)
                    take_items(g)
                    then(g)
                then(len(gran))

            with stage() as block:
                @block.sync
                def _(sp):
                    stream(sp, key)

                @block.tensor
                def _(pe):
                    norm.tensor(pe)
                    for g in range(len(gran)):
                        pe.wait_ge(split.sem, split.at(g + 1))
                        _, shaped = granule(g)
                        for n, (_, _, products, _) in enumerate(items):
                            if of_item[n] != g:
                                continue
                            free = (act_free, dve_free)[n % 2]
                            if n >= 8:
                                pe.wait_ge(free.sem, free.at(n // 2 - 3))
                            for to, terms in products(shaped(wh[g % 2]), shaped(wl[g % 2]), ps[:, n % 8, :]):
                                last = multiply(pe, to, terms, before=norm.input_ready if n == 0 else None)
                        last.then_inc(prod.sem, 1)

                def take(eng, odd, free, g):
                    for n, (_, _, _, taken) in enumerate(items):
                        if of_item[n] == g and n % 2 == odd:
                            eng.wait_ge(prod.sem, prod.at(g + 1))
                            to, of, scale = taken(ps[:, n % 8, :])
                            if odd:
                                eng.tensor_scalar(to, of, scale, None, ALU.mult).then_inc(free.sem, 1)
                            else:
                                eng.activation(to, of, ACT.Copy, scale=scale).then_inc(free.sem, 1)

                @block.scalar
                def _(act):
                    def split_one(g):
                        i = gran[g][0]
                        tile_loaded(act, key, i // RING, i % RING)
                        if g >= 2:
                            act.wait_ge(prod.sem, prod.at(g - 1))
                        raw, shaped = granule(g)
                        act.activation(shaped(wh[g % 2]), raw, ACT.Copy).then_inc(high.sem, 1)
                    norm.scalar(act, split_one)
                    steps(split_one, lambda g: take(act, 0, act_free, g), beside.scalar(act) if beside else lambda g: None)

                @block.vector
                def _(dve):
                    def split_one(g):
                        split_low(dve, g, *granule(g), g % 2)
                    norm.vector(dve, split_one)
                    steps(split_one, lambda g: take(dve, 1, dve_free, g), beside.vector(dve) if beside else lambda g: None)

                @block.gpsimd
                def _(pool):
                    norm.gpsimd(pool)
            norm.done()
            stage_done(key)
            act_free.passed((len(items) + 1) // 2)
            dve_free.passed(len(items) // 2)

        def chunk_item(tile, m, t0, t1, to, scale=1.0):
            def products(vh, vl, bank):
                c = slice((m % 2) * P, (m % 2 + 1) * P)
                return [(bank[:, 0:t1 - t0], [((vh[:, kk, c], vl[:, kk, c]), (uh[:, kk, t0:t1], ul[:, kk, t0:t1])) for kk in range(KD)])]
            return tile, m * P, products, lambda bank: (to, bank[:, 0:t1 - t0], scale)

        def token_item(tile, c0, n, tiles, to, scale=1.0):
            def products(vh, vl, bank):
                c = slice(c0 % 256, c0 % 256 + n)
                return [(bank[:, q * n:(q + 1) * n], [((uh[:, kk, t * P:(t + 1) * P], ul[:, kk, t * P:(t + 1) * P]),
                                                       (vh[:, kk, c], vl[:, kk, c])) for kk in range(KD)]) for q, t in enumerate(tiles)]
            return tile, c0, products, lambda bank: (to, bank[:, 0:n * len(tiles)].rearrange("p (t n) -> p t n", n=n)
                                                     if len(tiles) > 1 else bank[:, 0:n], scale)

        AM = Arena()
        qa = AM.take(3, T2)
        ka = AM.take(2, T2)
        qb = AM.take(3, T2)
        kb = AM.take(3, T2)
        va = AM.take(2 * ST, P)
        vb = AM.take(2 * ST, B_HEADS * HD)
        cx = AM.take(2, T2)
        cb = AM.take(2, T2)
        cc = AM.take(2, T2)
        CC_END = AM.at
        SC = AM
        scores = SC.take(3, T2)
        probs = SC.take(3, T2)
        probs_t = SC.take(2, T2)
        conv_t = SC.take(2, T2)
        RB = Arena(MID.at)
        bands = RB.take(B_HEADS, ST * S)
        flip = RB.take(P)
        zero_rows = RB.take(B_HEADS * RPB_H * RPB_PAD // P + 1)
        assert CC_END <= MID.at and RB.at <= ARENA - (KD + 1) * ADA_COLS and AM.at <= ARENA - B_HEADS * ST * S
        bias = Arena(ARENA - B_HEADS * ST * S).take(B_HEADS, ST, S)
        softs = sb("softs", [P, 12])

        def load_bands(pool, l):
            n = B_HEADS * RPB_H
            padded = a["padded"]
            pool.dma_start(flip, a["const"][:, CONST_W:CONST_W + P]).then_inc(flip_load.sem, 16)
            pool.memset(zero_rows, 0.0).then_inc(pool_step.sem, 1)
            pool.wait_ge(pool_step.sem, pool_step.at(1))
            pool.dma_start(padded, zero_rows).then_inc(band_load.sem, 16)
            pool.wait_ge(band_load.sem, band_load.at(16))
            middle = bass.AP(padded.tensor, GRID_W - WIN_C, [[RPB_PAD, n], [1, RPB_W]])
            pool.dma_start(middle, a["rpb"][l].rearrange("h r c -> (h r) c")).then_inc(band_load.sem, 16)
            pool.wait_ge(band_load.sem, band_load.at(32))
            for hh in range(B_HEADS):
                for r in range(ROWS):
                    at = (hh * RPB_H + WIN_R - 1 - r) * RPB_PAD
                    band = bass.AP(padded.tensor, at, [[1, GRID_W], [RPB_PAD, ROWS], [1, GRID_W]])
                    p0 = (r % 2) * GRID_W
                    to = bands[p0:p0 + GRID_W, hh, (r // 2) * S:(r // 2 + 1) * S].rearrange("p (r c) -> p r c", r=ROWS)
                    pool.dma_start(to, band).then_inc(band_load.sem, 16)
            pool.wait_ge(flip_load.sem, flip_load.at(16))
            pool.wait_ge(band_load.sem, band_load.at(16 * (2 + B_HEADS * ROWS)))

        def rel_bias():
            with stage() as block:
                @block.tensor
                def _(pe):
                    for hh in range(B_HEADS):
                        pe.matmul(ps[:, hh, :], flip, bands[:, hh, :], start=True, stop=True).then_inc(pe_step.sem, 1)

                @block.vector
                def _(dve):
                    for hh in range(B_HEADS):
                        dve.wait_ge(pe_step.sem, pe_step.at(hh + 1))
                        dve.tensor_tensor(bias[:, hh], ps[:, hh, :].rearrange("p (t k) -> p t k", t=ST),
                                          window.unsqueeze(1).broadcast_to([P, ST, S]), ALU.add)
            pe_step.passed(B_HEADS)

        def project(l, norm):
            key = ("in", l)
            last = l == DEPTH - 1
            T = S if last else T2
            items = []
            for m in range(3):
                items.append(chunk_item(0, m, 0, T, qa[:, m, 0:T]))
            for m in range(3):
                items.append(chunk_item(1, m, 0, T, qb[:, m, 0:T]))
            items.append(chunk_item(2, 0, 0, T2, ka[:, 0, :]))
            items.append(token_item(2, P, P, range(2 * ST), va))
            for m in range(3):
                items.append(chunk_item(3, m, 0, T2, kb[:, m, :]))
            for c0, n in ((0, 256), (256, 128)):
                for t in range(0, 2 * ST, 512 // n):
                    k = 512 // n
                    items.append(token_item(4, c0, n, range(t, t + k), vb[:, t:t + k, c0:c0 + n]))
            for m, to in enumerate((cx[:, 0], cx[:, 1], cb[:, 0], cb[:, 1])):
                items.append(chunk_item(5, m, 0, T, to[:, 0:T]))
            for m in range(2):
                items.append(chunk_item(6, m, 0, T, cc[:, m, 0:T]))
            listed(key, IN_SPANS, items, norm)

        def qk_norm(l):
            T = [S if l == DEPTH - 1 else T2] * 3 + [T2]
            xs = [qa[:, 0], qa[:, 1], qa[:, 2], ka[:, 0]]
            with stage() as block:
                @block.scalar
                def _(act):
                    act.preload_act_table_set(LN_EXP)
                    for i in range(4):
                        act.activation(probs_t[:, i % 2, 0:T[i]] if i < 2 else scores[:, i % 2, 0:T[i]], xs[i][:, 0:T[i]],
                                       ACT.Square).then_inc(act_step.sem, 1)
                    for i in range(4):
                        act.wait_ge(pe_step.sem, pe_step.at(i + 1))
                        r = (probs if i < 2 else conv_t)[:, i % 2, 0:T[i]]
                        act_chain.link(act, act.activation(r, ps[:, i, 0:T[i]], ACT.Ln, scale=1.0 / HD, bias=eps[:, 0:1]))
                        act.activation(r, r, ACT.Exp, scale=-0.5).then_inc(act_step.sem, 1)
                    act.wait_ge(pe_step.sem, pe_step.at(9))
                    act.activation(ka[:, 1, :], ps[:, 0, :], ACT.Copy)

                @block.tensor
                def _(pe):
                    for i in range(4):
                        pe.wait_ge(act_step.sem, act_step.at(i + 1))
                        sq = (probs_t if i < 2 else scores)[:, i % 2, 0:T[i]]
                        pe.matmul(ps[:, i, 0:T[i]], mat("half_ones"), sq, start=True, stop=True).then_inc(pe_step.sem, 1)
                    for i in range(4):
                        pe.wait_ge(dve_step.sem, dve_step.at(i + 1))
                        pe.matmul(ps[:, 4 + i, 0:S], mat("rot"), xs[i][:, 0:S], start=True, stop=True).then_inc(pe_step.sem, 1)
                    pe.wait_ge(dve_step.sem, dve_step.at(16))
                    pe.matmul(ps[:, 0, :], mat("swap"), ka[:, 0, :], start=True, stop=True).then_inc(pe_step.sem, 1)

                @block.vector
                def _(dve):
                    for i in range(4):
                        dve.wait_ge(act_step.sem, act_step.at(5 + i))
                        r = (probs if i < 2 else conv_t)[:, i % 2, 0:T[i]]
                        gain = head_gain[:, 2 * l + (i == 3):2 * l + (i == 3) + 1]
                        dve.scalar_tensor_tensor(out=xs[i][:, 0:T[i]], in0=xs[i][:, 0:T[i]], scalar=gain, in1=r,
                                                 op0=ALU.mult, op1=ALU.mult).then_inc(dve_step.sem, 1)
                    for i in range(4):
                        dve.wait_ge(pe_step.sem, pe_step.at(5 + i))
                        turned = scores[:, i % 2, 0:S]
                        if i >= 1:
                            dve.wait_ge(dve_step.sem, dve_step.at(4 + 3 * i))
                        dve.tensor_tensor(turned, ps[:, 4 + i, 0:S], sin_t, ALU.mult).then_inc(dve_step.sem, 1)
                        dve.tensor_tensor(xs[i][:, 0:S], xs[i][:, 0:S], cos_t, ALU.mult).then_inc(dve_step.sem, 1)
                        dve.wait_ge(dve_step.sem, dve_step.at(4 + 3 * i + 2))
                        dve.tensor_tensor(xs[i][:, 0:S], xs[i][:, 0:S], turned, ALU.add).then_inc(dve_step.sem, 1)
            act_step.passed(8)
            pe_step.passed(9)
            dve_step.passed(16)

        def attention(l):
            last = l == DEPTH - 1
            units = []
            for hd in range(A_HEADS):
                b = HD * (hd % 2)
                kv = hd // (A_HEADS // A_KV)
                kt = ka[b:b + HD, 0 if kv == hd % 2 else 1, :]
                v = lambda t, kv=kv: va[:, t, kv * HD:(kv + 1) * HD]
                for t in range(ST):
                    units.append((qa[b:b + HD, hd // 2, t * P:(t + 1) * P], kt, 0, T2, None, v, hd // 2, b, t))
                    if not last:
                        tc = ST + t
                        units.append((qa[b:b + HD, hd // 2, tc * P:(tc + 1) * P], kt, S, T2, None, v, hd // 2, b, tc))
            for hd in range(B_HEADS):
                b = HD * (hd % 2)
                kt = kb[b:b + HD, hd // 2, :]
                v = lambda t, hd=hd: vb[:, t, hd * HD:(hd + 1) * HD]
                for t in range(ST):
                    units.append((qb[b:b + HD, hd // 2, t * P:(t + 1) * P], kt, 0, T2, bias[:, hd, t, :], v, 3 + hd // 2, b, t))
                    if not last:
                        tc = ST + t
                        units.append((qb[b:b + HD, hd // 2, tc * P:(tc + 1) * P], kt, S, T2, None, v, 3 + hd // 2, b, tc))
            n = len(units)
            scale = HD ** -0.5
            scored, softened, normed, turned_, moved, valued, taken, maxed = (
                pe_step, act_step, dve_step, prod, act_free, gate_done, dve_free, aux)
            soft = lambda what, i: softs[:, 3 * what + i % 3:3 * what + i % 3 + 1]
            with stage() as block:
                @block.tensor
                def _(pe):
                    for i in range(n + 3):
                        if i < n:
                            q, kt, k0, k1, bm, v, oc, b, t = units[i]
                            if i >= 4:
                                pe.wait_ge(softened.sem, softened.at(i - 3))
                            pe.matmul(ps[:, i % 4, 0:k1 - k0], q, kt[:, k0:k1], start=True, stop=True).then_inc(scored.sem, 1)
                        if 2 <= i <= n + 1:
                            j = i - 2
                            _, _, k0, k1, *_ = units[j]
                            pe.wait_ge(normed.sem, normed.at(j + 1))
                            if j >= 2:
                                pe.wait_ge(moved.sem, moved.at(j - 1))
                            for m in range((k1 - k0) // P):
                                tr = pe.transpose(ps[:, 4 + j % 2, m * P:(m + 1) * P], probs[:, j % 3, m * P:(m + 1) * P], ident)
                            tr.then_inc(turned_.sem, 1)
                        if i >= 3:
                            j = i - 3
                            _, _, k0, k1, _, v, oc, b, t = units[j]
                            pe.wait_ge(moved.sem, moved.at(j + 1))
                            if j >= 2:
                                pe.wait_ge(taken.sem, taken.at(j - 1))
                            m_n = (k1 - k0) // P
                            for m in range(m_n):
                                mm = pe.matmul(ps[b:b + HD, 6 + j % 2, 0:P], v(k0 // P + m), probs_t[:, j % 2, m * P:(m + 1) * P],
                                               start=(m == 0), stop=(m == m_n - 1))
                            mm.then_inc(valued.sem, 1)

                @block.scalar
                def _(act):
                    act.preload_act_table_set(LN_EXP)
                    for i in range(n + 2):
                        if i < n:
                            _, _, k0, k1, bm, *_ = units[i]
                            act.wait_ge(maxed.sem, maxed.at(i + 1))
                            if i >= 3:
                                act.wait_ge(turned_.sem, turned_.at(i - 2))
                            of = scores[:, i % 3, 0:k1 - k0] if bm is not None else ps[:, i % 4, 0:k1 - k0]
                            act.activation(probs[:, i % 3, 0:k1 - k0], of, ACT.Exp, bias=soft(0, i),
                                           scale=1.0 if bm is not None else scale, accum_out=soft(1, i)).then_inc(softened.sem, 1)
                        if i >= 2:
                            j = i - 2
                            _, _, k0, k1, *_ = units[j]
                            act.wait_ge(turned_.sem, turned_.at(j + 1))
                            if j >= 2:
                                act.wait_ge(valued.sem, valued.at(j - 1))
                            act.activation(probs_t[:, j % 2, 0:k1 - k0], ps[:, 4 + j % 2, 0:k1 - k0], ACT.Copy).then_inc(moved.sem, 1)

                @block.vector
                def _(dve):
                    for i in range(n + 4):
                        if i < n:
                            _, _, k0, k1, bm, *_ = units[i]
                            N = k1 - k0
                            dve.wait_ge(scored.sem, scored.at(i + 1))
                            if i >= 3:
                                dve.wait_ge(softened.sem, softened.at(i - 2))
                            if bm is not None:
                                sc = scores[:, i % 3, 0:N]
                                dve.scalar_tensor_tensor(out=sc[:, 0:S], in0=ps[:, i % 4, 0:S], scalar=scale, in1=bm,
                                                         op0=ALU.mult, op1=ALU.add).then_inc(dve_chain.sem, 1)
                                dve.tensor_scalar(sc[:, S:N], ps[:, i % 4, S:N], scale, None, ALU.mult).then_inc(dve_chain.sem, 1)
                                dve_chain.n += 2
                                dve.wait_ge(dve_chain.sem, dve_chain.n)
                                dve_chain.link(dve, dve.tensor_reduce(soft(2, i), sc, AX_X, ALU.max))
                                dve.tensor_scalar(soft(0, i), soft(2, i), -1.0, None, ALU.mult).then_inc(maxed.sem, 1)
                            else:
                                dve_chain.link(dve, dve.tensor_reduce(soft(2, i), ps[:, i % 4, 0:N], AX_X, ALU.max))
                                dve.tensor_scalar(soft(0, i), soft(2, i), -scale, None, ALU.mult).then_inc(maxed.sem, 1)
                        if 1 <= i <= n:
                            j = i - 1
                            N = units[j][3] - units[j][2]
                            dve.wait_ge(softened.sem, softened.at(j + 1))
                            if j >= 3:
                                dve.wait_ge(normed.sem, normed.at(j - 2))
                            dve_chain.link(dve, dve.reciprocal(soft(3, j), soft(1, j)))
                            dve.tensor_scalar(probs[:, j % 3, 0:N], probs[:, j % 3, 0:N], soft(3, j), None,
                                              ALU.mult).then_inc(normed.sem, 1)
                        if i >= 4:
                            j = i - 4
                            *_, oc, b, t = units[j]
                            dve.wait_ge(valued.sem, valued.at(j + 1))
                            of = ps[b:b + HD, 6 + j % 2, 0:P]
                            oh, ol = (v[b:b + HD, oc, t * P:(t + 1) * P] for v in (uh, ul))
                            dve_chain.link(dve, dve.tensor_copy(oh, of))
                            dve.tensor_tensor(ol, of, oh, ALU.subtract).then_inc(taken.sem, 1)

                @block.gpsimd
                def _(pool):
                    link = lambda ins: pool_chain.link(pool, ins)
                    T = S if last else T2
                    for j in range(2):
                        tap = lambda w_: col("conv_w", (l * 3 + w_) * 2 + j)
                        z, y, t_ = cx[:, j, 0:T], conv_t[:, 0, 0:T], conv_t[:, 1, 0:T]
                        link(pool.tensor_tensor(z, cc[:, j, 0:T], z, ALU.mult))
                        link(pool.tensor_scalar(y, z, tap(1), None, ALU.mult))
                        link(pool.tensor_scalar(t_, z, tap(0), None, ALU.mult))
                        for s in range(T // S):
                            link(pool.tensor_tensor(y[:, s * S + 1:(s + 1) * S], y[:, s * S + 1:(s + 1) * S],
                                                    t_[:, s * S:(s + 1) * S - 1], ALU.add))
                        link(pool.tensor_scalar(t_, z, tap(2), None, ALU.mult))
                        for s in range(T // S):
                            link(pool.tensor_tensor(y[:, s * S:(s + 1) * S - 1], y[:, s * S:(s + 1) * S - 1],
                                                    t_[:, s * S + 1:(s + 1) * S], ALU.add))
                        link(pool.tensor_tensor(y, y, cb[:, j, 0:T], ALU.mult))
                        link(pool.tensor_copy(uh[:, 6 + j, 0:T], y))
                        link(pool.tensor_tensor(ul[:, 6 + j, 0:T], y, uh[:, 6 + j, 0:T], ALU.subtract))
            for s_ in (scored, softened, normed, turned_, moved, valued, taken, maxed):
                s_.passed(n)

        def finish():
            tokens = Arena().take(ST, D)
            with stage() as block:
                @block.tensor
                def _(pe):
                    for t in range(ST):
                        for half in range(2):
                            g = 2 * t + half
                            for m in range(4):
                                tr = pe.transpose(ps[:, g, m * P:(m + 1) * P], h[:, 4 * half + m, t * P:(t + 1) * P], ident)
                            tr.then_inc(pe_step.sem, 1)

                @block.vector
                def _(dve):
                    for g in range(2 * ST):
                        dve.wait_ge(pe_step.sem, pe_step.at(g + 1))
                        dve.tensor_copy(tokens[:, g // 2, (g % 2) * 512:(g % 2 + 1) * 512], ps[:, g, :]).then_inc(dve_step.sem, 1)

                @block.sync
                def _(sp):
                    for t in range(ST):
                        sp.wait_ge(dve_step.sem, dve_step.at(2 * t + 2))
                        sp.dma_start(out[0, t * P:(t + 1) * P, :], tokens[:, t, :]).then_inc(stored.sem, 16)
                    sp.wait_ge(stored.sem, stored.at(16 * ST))

        CF = Arena()
        mid2 = CF.take(KF, S)
        conv_buf = CF.take(4, 2, S)

        def ffn2(i, norm):
            key = ("up2", i)
            down = Down(key, ("down2", i), mid2, S)
            n_ch = 2 * KF
            with stage() as block:
                @block.sync
                def _(sp):
                    stream(sp, key)
                    down.sync(sp)

                @block.tensor
                def _(pe):
                    norm.tensor(pe)
                    pair_products(pe, key, norm, dve_free)
                    down.tensor(pe)

                def channel(name, tap, part, g):
                    at = col_at[name] + (i * (3 if name == "ffn_conv_w" else 1) + tap) * n_ch + part * KF
                    return cols[:, ds(g + at, 1)]

                def before(turn, q):
                    return (turn, q - 1) if q else (turn - 1, 3)

                @block.scalar
                def _(act):
                    high_of = split_pairs(key, act=act)

                    def gelu(turn, q):
                        act.wait_ge(conv_done.sem, conv_done.at(turn * 4 + q + 1))
                        act.activation(conv_buf[:, q, 0, :], conv_buf[:, q, 0, :], ACT.Gelu_apprx_tanh).then_inc(gelu_done.sem, 1)

                    def granule(turn, q, more, first=False):
                        g = turn * 4 + q
                        if more:
                            high_of(*ahead(turn, q))
                        else:
                            if g == KF - 1:
                                down.input_high(act, 0)
                            down.high_ahead(act, g - (KF - 2))
                        act.wait_ge(prod.sem, prod.at(g + 1))
                        act.wait_ge(dve_free.sem, dve_free.at(g - 3))
                        for part in range(2):
                            act.activation(conv_buf[:, q, part, :], ps[:, 2 * q + part, 0:S], ACT.Identity,
                                           bias=channel("ffn_conv_b", 0, part, g),
                                           scale=channel("ffn_conv_w", 1, part, g)).then_inc(gate_done.sem, 1)
                        if not first:
                            gelu(*before(turn, q))
                    norm.scalar(act, lambda g: high_of(0, g))
                    granule(0, 0, True, first=True)
                    with_lead(act, KF, 2, granule, 1)
                    gelu((KF - 1) // 4, (KF - 1) % 4)
                    down.scalar(act)

                @block.vector
                def _(dve):
                    low_of = split_pairs(key, dve=dve)

                    def gated(turn, q):
                        g = turn * 4 + q
                        dve.wait_ge(gelu_done.sem, gelu_done.at(g + 1))
                        dve.wait_ge(conv_done.sem, conv_done.at(g + 1))
                        dve.tensor_tensor(mid2[:, ds(g, 1), :].squeeze(1), conv_buf[:, q, 0, :], conv_buf[:, q, 1, :],
                                          ALU.mult).then_inc(dve_free.sem, 1)

                    def granule(turn, q, more, first=False):
                        g = turn * 4 + q
                        if more:
                            low_of(*ahead(turn, q))
                        else:
                            if g == KF - 1:
                                down.input_low(dve, 0)
                            down.low_ahead(dve, g - (KF - 2))
                        dve.wait_ge(gate_done.sem, gate_done.at(g * 2 + 2))
                        for tap, to, of in ((0, slice(1, S), slice(0, S - 1)), (2, slice(0, S - 1), slice(1, S))):
                            for part in range(2):
                                if tap == 2:
                                    dve.wait_ge(aux.sem, aux.at(g * 3 + 1 + part))
                                ins = dve.scalar_tensor_tensor(out=conv_buf[:, q, part, to], in0=ps[:, 2 * q + part, of],
                                                               scalar=channel("ffn_conv_w", tap, part, g),
                                                               in1=conv_buf[:, q, part, to], op0=ALU.mult, op1=ALU.add)
                                ins.then_inc(conv_done.sem if tap == 2 and part == 1 else aux.sem, 1)
                        if not first:
                            gated(*before(turn, q))
                    norm.vector(dve, lambda g: low_of(0, g))
                    granule(0, 0, True, first=True)
                    with_lead(dve, KF, 2, granule, 1)
                    gated((KF - 1) // 4, (KF - 1) % 4)
                    down.vector(dve)

                @block.gpsimd
                def _(pool):
                    norm.gpsimd(pool)
            norm.done()
            stage_done(key)
            down.done()
            n = KF
            dve_free.passed(n)
            conv_done.passed(n)
            gate_done.passed(2 * n)
            gelu_done.passed(n)
            aux.passed(3 * n)

        def head_norm(key, scratch, *jobs):
            mem = Arena(scratch)
            sqs = [mem.take(n, S) for _, n, *_ in jobs]
            rss = [mem.take(n // per, S) for _, n, per, *_ in jobs]
            flat_h, flat_l = (v[:, :, :].rearrange("p a b -> p (a b)").rearrange("p (a b) -> p a b", b=S) for v in (uh, ul))
            two = lambda v, q: v[:, 2 * q:2 * q + 2, :]
            pairs = [(i, q) for i, (_, n, *_) in enumerate(jobs) for q in range(n // 2)]
            banks = [(i, b) for i, (_, n, per, *_) in enumerate(jobs) for b in range(n // per // 2)]
            funcs = [(i, of) for i, (*_, before, after) in enumerate(jobs) for of in (before, after) if of is not None]
            weighted = [p_ for p_ in pairs if jobs[p_[0]][4] is not None]

            def pair(v, i, q):
                return v[:, jobs[i][0] + 2 * q:jobs[i][0] + 2 * q + 2, :]

            w = Wide(key, flat_h, flat_l, 2 * len(pairs), S, lambda pe, k: pe.wait_ge(u_ready.sem, u_ready.at(k // 2 + 1)))
            with stage() as block:
                @block.sync
                def _(sp):
                    stream(sp, key)

                @block.scalar
                def _(act):
                    for _, of in funcs:
                        act.activation(of[1], of[1], of[0]).then_inc(gate_done.sem, 1)
                    act.preload_act_table_set(LN_EXP)
                    for i, q in pairs:
                        if (i, q) in weighted:
                            act.wait_ge(dve_step.sem, dve_step.at(weighted.index((i, q)) + 1))
                        act.activation(two(sqs[i], q), pair(u32, i, q), ACT.Square).then_inc(act_step.sem, 1)
                    w.high(act, 0)
                    for m, (i, b) in enumerate(banks):
                        act.wait_ge(pe_step.sem, pe_step.at(m + 1))
                        r = two(rss[i], b)
                        act_chain.link(act, act.activation(r, ps[:, m, :].rearrange("p (a b) -> p a b", a=2), ACT.Ln,
                                                           scale=1.0 / (jobs[i][2] * P), bias=eps[:, 0:1]))
                        act.activation(r, r, ACT.Exp, scale=-0.5).then_inc(act_step.sem, 1)
                    for m, (i, q) in enumerate(pairs):
                        act.wait_ge(aux.sem, aux.at(m + 1))
                        act.activation(pair(flat_h, i, q), two(sqs[i], q), ACT.Copy).then_inc(act_step.sem, 1)
                    for g in range(1, w.n):
                        w.high(act, g)

                @block.tensor
                def _(pe):
                    for m, (i, b) in enumerate(banks):
                        per = jobs[i][2]
                        for k in range(2 * per * b, 2 * per * (b + 1)):
                            pe.wait_ge(act_step.sem, act_step.at(pairs.index((i, k // 2)) + 1))
                            g = k // per % 2
                            last = pe.matmul(ps[:, m, g * S:(g + 1) * S], ones, sqs[i][:, k, :], start=(k % per == 0), stop=(k % per == per - 1))
                        last.then_inc(pe_step.sem, 1)
                    w.tensor(pe)

                @block.vector
                def _(dve):
                    for i, q in weighted:
                        dve.wait_ge(gate_done.sem, gate_done.at(funcs.index((i, jobs[i][4])) + 1))
                        x = pair(u32, i, q)
                        dve.tensor_tensor(x, x, two(jobs[i][4][1], q), ALU.mult).then_inc(dve_step.sem, 1)
                    dve.wait_ge(dve_step.sem, dve_step.at(len(weighted)))
                    w.low(dve, 0)
                    lag = 2
                    for m in range(len(pairs) + lag):
                        if m < len(pairs):
                            i, q = pairs[m]
                            base, _, per, gain, _, after = jobs[i]
                            for k in (2 * q, 2 * q + 1):
                                dve.wait_ge(act_step.sem, act_step.at(len(pairs) + banks.index((i, k // per // 2)) + 1))
                                ins = dve.scalar_tensor_tensor(out=sqs[i][:, k, :], in0=u32[:, base + k, :], scalar=col(gain, k),
                                                               in1=rss[i][:, k // per, :], op0=ALU.mult, op1=ALU.mult)
                                if after is not None:
                                    ins.then_inc(dve_chain.sem, 1)
                            if after is not None:
                                dve_chain.n += 2
                                dve.wait_ge(dve_chain.sem, dve_chain.n)
                                ins = dve.tensor_tensor(two(sqs[i], q), two(sqs[i], q), two(after[1], q), ALU.mult)
                            ins.then_inc(aux.sem, 1)
                        if m >= lag:
                            i, q = pairs[m - lag]
                            dve.wait_ge(act_step.sem, act_step.at(len(pairs) + len(banks) + m - lag + 1))
                            dve.tensor_tensor(pair(flat_l, i, q), two(sqs[i], q), pair(flat_h, i, q),
                                              ALU.subtract).then_inc(u_ready.sem, 1)
                    for g in range(1, w.n):
                        w.low(dve, g)
            gate_done.passed(len(funcs))
            act_step.passed(2 * len(pairs) + len(banks))
            pe_step.passed(len(banks))
            dve_step.passed(len(weighted))
            aux.passed(len(pairs))
            u_ready.passed(len(pairs))
            stage_done(key)

        BM = Arena()
        z = h[:, :, S:T2]
        xbc = BM.take(12, S)
        mq = BM.take(ML_HEADS, S)
        mk = BM.take(ML_HEADS, S)
        mv = BM.take(ST, D)
        o_pre = BM.take(KD, S)
        gate_x = BM.take(ST, 64)
        soft = BM.take(ST, 64)
        dt = BM.take(ST, 32)
        dta = BM.take(ST, 32)
        ncs = BM.take(2, ST, SSD_HEADS)
        w_end = BM.take(2, SSD_HEADS)
        bcol = BM.take(6, ML_HEADS)
        HN_AT = BM.at
        SS = Arena(BM.at)
        xdt = ul32[:, :].rearrange("p (a b) -> p a b", b=D).rearrange("p (a b) c -> p a b c", a=2)
        xs_tok = SS.take(ST, D)
        b_tok = SS.take(ST, 2 * P)
        x_end = SS.take(2, D)
        state = SS.take(2, D)
        xbc_raw = Arena(BM.at).take(12, S)
        decays = x_end.rearrange("p a b -> p (a b)").rearrange("p (a b c) -> p a b c", a=2, b=8)
        cbt = xs_tok[:, 0, 0:512]
        carry = xs_tok[:, 1, :].rearrange("p (a b) -> p a b", a=2)
        FIRST = (0, ST - 1)
        tri = (mat("upto"), mat("from_"))
        tri_mask = (mat("mask_upto"), mat("mask_from"))
        mixed = u32

        class ShortConv:
            START, TAPS = 7, 3

            def __init__(self):
                middle = SSD_CONV // 2
                order = [middle] + [t for t in range(SSD_CONV) if t != middle]
                self.ops = [(j + m, tap) for j in range(0, 12, 2) for tap in order for m in range(2)]
                self.last = order[-1]

            def of(self, g, end):
                i = self.TAPS * (g - self.START)
                return self.ops[max(i, 0):max(len(self.ops) if end else i + self.TAPS, 0)]

            def vector(self, dve):
                n_gran = sum(plan["ab_in"].count)

                def then(g):
                    for j, tap in self.of(g, g == n_gran):
                        s = tap - SSD_CONV // 2
                        w_ = col("ab_conv_w", tap * 12 + j)
                        x_, y_ = xbc_raw[:, j, :], xbc[:, j, :]
                        if s == 0:
                            free = (act_free, dve_free)[j % 2]
                            dve.wait_ge(free.sem, free.at((8 + j) // 2 + 1))
                            ins = dve.tensor_scalar(y_, x_, w_, col("ab_conv_b", j), ALU.mult, ALU.add)
                        else:
                            dve.wait_ge(dve_chain.sem, dve_chain.n - (0 if tap == self.last and j % 2 else 1))
                            to = slice(max(0, -s), S - max(0, s))
                            of = slice(max(0, s), S - max(0, -s))
                            ins = dve.scalar_tensor_tensor(out=y_[:, to], in0=x_[:, of], scalar=w_, in1=y_[:, to],
                                                           op0=ALU.mult, op1=ALU.add)
                        if tap == self.last:
                            ins.then_inc(conv_done.sem, 1)
                        else:
                            ins.then_inc(dve_chain.sem, 1)
                            dve_chain.n += 1
                return then

            def scalar(self, act):
                n_gran = sum(plan["ab_in"].count)

                def then(g):
                    ready_now = self.of(g - 1, False) + (self.of(g, True) if g == n_gran else [])
                    for j in [j for j, tap in ready_now if tap == self.last]:
                        act.wait_ge(conv_done.sem, conv_done.at(j + 1))
                        act.activation(xbc[:, j, :], xbc[:, j, :], ACT.Silu)
                return then

        def ab_project(norm):
            items = []
            for m in range(20):
                to = z[:, m, :] if m < 8 else xbc_raw[:, m - 8, :]
                items.append(chunk_item(m // 4, m % 4, 0, S, to))
            for m in range(8):
                items.append(chunk_item(5 + m // 4, m % 4, 0, S, mq[:, m, :]))
            for m in range(8):
                items.append(chunk_item(7 + m // 4, m % 4, 0, S, mk[:, m, :], scale=(D // ML_HEADS) ** -0.5))
            for q in range(4):
                items.append(token_item(9 + q // 2, (q % 2) * 256, 256, range(ST), mv[:, :, q * 256:(q + 1) * 256]))
            for m in range(8):
                items.append(chunk_item(11 + m // 4, m % 4, 0, S, o_pre[:, m, :]))
            items.append(token_item(13, 0, 64, range(ST), gate_x))
            listed("ab_in", AB_SPANS, items, norm, ShortConv())
            conv_done.passed(12)

        def ssd_gates():
            with stage() as block:
                @block.vector
                def _(dve):
                    link = lambda ins: dve_chain.link(dve, ins)
                    dve.tensor_tensor(gate_x, gate_x, gate_bias[:, :].unsqueeze(1).broadcast_to([P, ST, 64]), ALU.add).then_inc(dve_step.sem, 1)
                    dve.wait_ge(act_step.sem, act_step.at(2))
                    link(dve.scalar_tensor_tensor(out=dt[:, :, :], in0=gate_x[:, :, 0:32], scalar=0.0, in1=soft[:, :, 0:32],
                                                  op0=ALU.max, op1=ALU.add))
                    link(dve.scalar_tensor_tensor(out=dta[:, :, :], in0=dt[:, :, :], scalar=-1.0,
                                                  in1=a_log[:, :].unsqueeze(1).broadcast_to([P, ST, 32]), op0=ALU.mult, op1=ALU.mult))
                    link(dve.scalar_tensor_tensor(out=gate_x[:, :, 48:64], in0=gate_x[:, :, 48:64], scalar=0.0,
                                                  in1=soft[:, :, 48:64], op0=ALU.min, op1=ALU.subtract))

                @block.scalar
                def _(act):
                    act.preload_act_table_set(LN_EXP)
                    link = lambda ins: act_chain.link(act, ins)
                    act.activation(a_log[:, :], a_log[:, :], ACT.Exp).then_inc(act_step.sem, 1)
                    act.wait_ge(dve_step.sem, dve_step.at(1))
                    link(act.activation(soft, gate_x, ACT.Abs))
                    link(act.activation(soft, soft, ACT.Exp, scale=-1.0))
                    act.activation(soft, soft, ACT.Ln, bias=ones[:, 0:1]).then_inc(act_step.sem, 1)
            act_step.passed(2)
            dve_step.passed(1)

        def ssd_prepare():
            with stage() as block:
                @block.tensor
                def _(pe):
                    for t in range(ST):
                        for q in range(2):
                            for m in range(4):
                                tr = pe.transpose(ps[:, 2 * t + q, m * P:(m + 1) * P], xbc[:, 4 * q + m, t * P:(t + 1) * P], ident)
                            tr.then_inc(pe_step.sem, 1)
                    for t in range(ST):
                        for g in range(2):
                            tr = pe.transpose(ps[:, 4, (2 * t + g) * P:(2 * t + g + 1) * P], xbc[:, 8 + g, t * P:(t + 1) * P], ident)
                    tr.then_inc(pe_step.sem, 1)
                    for d in range(2):
                        for t in range(ST):
                            o = (d * ST + t) * SSD_HEADS
                            pe.matmul(ps[:, 5, o:o + SSD_HEADS], tri[d], dta[:, t, d * SSD_HEADS:(d + 1) * SSD_HEADS], start=True, stop=True)
                    for t in range(ST):
                        mm = pe.matmul(ps[:, 5, 64 + t * 32:96 + t * 32], ones, dta[:, t, :], start=True, stop=True)
                    mm.then_inc(pe_step.sem, 1)
                    for t in range(ST):
                        for g in range(SSD_GROUPS):
                            o = (t * SSD_GROUPS + g) * P
                            mm = pe.matmul(ps[:, 6, o:o + P], xbc[:, 8 + g, t * P:(t + 1) * P], xbc[:, 10 + g, t * P:(t + 1) * P],
                                           start=True, stop=True)
                    mm.then_inc(pe_step.sem, 1)
                    pe.wait_ge(dve_step.sem, dve_step.at(10))
                    for d in range(2):
                        for g in range(SSD_GROUPS):
                            pe.matmul(ps[:, 2 * d + g, :], b_tok[:, FIRST[d], g * P:(g + 1) * P],
                                      x_end[:, d, g * 512:(g + 1) * 512], start=True, stop=True).then_inc(pe_step.sem, 1)

                @block.scalar
                def _(act):
                    act.preload_act_table_set(LN_EXP)
                    for n in range(4):
                        act.wait_ge(pe_step.sem, pe_step.at(n + 1))
                        act.activation(xs_tok[:, n // 2, (n % 2) * 512:(n % 2 + 1) * 512], ps[:, n, :], ACT.Copy).then_inc(act_step.sem, 1)
                    act.wait_ge(pe_step.sem, pe_step.at(5))
                    act.activation(b_tok.rearrange("p a b -> p (a b)"), ps[:, 4, :], ACT.Copy).then_inc(act_step.sem, 1)
                    act.wait_ge(dve_step.sem, dve_step.at(3))
                    act.activation(w_end[:, :, :], w_end[:, :, :], ACT.Exp).then_inc(act_step.sem, 1)
                    for n in range(4):
                        act.wait_ge(pe_step.sem, pe_step.at(8 + n))
                        act.activation(state[:, n // 2, (n % 2) * 512:(n % 2 + 1) * 512], ps[:, n, :], ACT.Copy).then_inc(act_step.sem, 1)

                @block.vector
                def _(dve):
                    dve.wait_ge(pe_step.sem, pe_step.at(6))
                    dve.tensor_scalar(ncs.rearrange("p d t h -> p (d t h)"), ps[:, 5, 0:64], -1.0, None, ALU.mult).then_inc(dve_step.sem, 1)
                    dve.wait_ge(dve_step.sem, dve_step.at(1))
                    for d in range(2):
                        t = FIRST[d]
                        o = 64 + t * 32 + d * SSD_HEADS
                        dve.tensor_tensor(w_end[:, d, :], ps[:, 5, o:o + SSD_HEADS], ncs[:, d, t, :], ALU.add).then_inc(dve_step.sem, 1)
                    dve.wait_ge(act_step.sem, act_step.at(4))
                    for d in range(2):
                        for t in range(ST):
                            dve.tensor_tensor(xdt[:, d, t, :].rearrange("p (h e) -> p h e", e=HD),
                                              xs_tok[:, t, :].rearrange("p (h e) -> p h e", e=HD),
                                              dt[:, t, d * SSD_HEADS:(d + 1) * SSD_HEADS].unsqueeze(2).broadcast_to([P, SSD_HEADS, HD]),
                                              ALU.mult).then_inc(dve_step.sem, 1)
                    dve.wait_ge(act_step.sem, act_step.at(6))
                    dve.wait_ge(dve_step.sem, dve_step.at(7))
                    for d in range(2):
                        dve.tensor_tensor(x_end[:, d, :].rearrange("p (h e) -> p h e", e=HD),
                                          xdt[:, d, FIRST[d], :].rearrange("p (h e) -> p h e", e=HD),
                                          w_end[:, d, :].unsqueeze(2).broadcast_to([P, SSD_HEADS, HD]), ALU.mult).then_inc(dve_step.sem, 1)
                    dve.wait_ge(pe_step.sem, pe_step.at(7))
                    dve.tensor_copy(cbt, ps[:, 6, :]).then_inc(dve_step.sem, 1)
            pe_step.passed(11)
            act_step.passed(10)
            dve_step.passed(10)

        def ssd_scan():
            units = [(t, q) for t in range(ST) for q in range(4)]
            n = len(units)
            with stage() as block:
                @block.tensor
                def _(pe):
                    for i in range(n + 1):
                        if i < n:
                            t, q = units[i]
                            into = 1 - t
                            if i >= 2:
                                pe.wait_ge(act_step.sem, act_step.at(i - 1))
                            b0 = 3 * (i % 2)
                            for d in range(2):
                                for m in range(4):
                                    hh = d * SSD_HEADS + 4 * q + m
                                    o = m * P
                                    pe.matmul(ps[:, b0 + d, o:o + P], dta[:, t, hh:hh + 1].broadcast_to([P, P]), tri[d], start=True, stop=False)
                                    pe.matmul(ps[:, b0 + d, o:o + P], ident, tri_mask[d], start=False, stop=True)
                            d = 0 if t == 1 else 1
                            for m in range(4):
                                hh = d * SSD_HEADS + 4 * q + m
                                mm = pe.matmul(ps[:, b0 + 2, m * P:(m + 1) * P], dta[:, t, hh:hh + 1].broadcast_to([P, P]), tri[d],
                                               start=True, stop=True)
                            mm.then_inc(pe_step.sem, 1)
                        if i >= 1:
                            j = i - 1
                            t, q = units[j]
                            d_in = 0 if t == 1 else 1
                            pe.wait_ge(dve_step.sem, dve_step.at(j + 1))
                            if j >= 2:
                                pe.wait_ge(dve_free.sem, dve_free.at(j - 1))
                            for m in range(4):
                                c0 = (4 * q + m) * HD
                                b = HD * (m % 2)
                                to = ps[b:b + HD, 6 + j % 2, (m // 2) * P:(m // 2 + 1) * P]
                                for d in range(2):
                                    pe.matmul(to, xdt[:, d, t, c0:c0 + HD], decays[:, j % 2, 4 * d + m, :], start=(d == 0), stop=False)
                                mm = pe.matmul(to, state[:, d_in, c0:c0 + HD], carry[:, j % 2, m * P:(m + 1) * P], start=False, stop=True)
                            mm.then_inc(gate_done.sem, 1)

                @block.scalar
                def _(act):
                    for i in range(n):
                        t, q = units[i]
                        b0 = 3 * (i % 2)
                        act.wait_ge(pe_step.sem, pe_step.at(i + 1))
                        if i >= 2:
                            act.wait_ge(gate_done.sem, gate_done.at(i - 1))
                        for d in range(2):
                            for m in range(4):
                                hh = 4 * q + m
                                act.activation(decays[:, i % 2, 4 * d + m, :], ps[:, b0 + d, m * P:(m + 1) * P], ACT.Exp,
                                               bias=ncs[:, d, t, hh:hh + 1])
                        act.activation(carry[:, i % 2, :], ps[:, b0 + 2, :], ACT.Exp).then_inc(act_step.sem, 1)

                @block.vector
                def _(dve):
                    for i in range(n + 1):
                        if i < n:
                            t, q = units[i]
                            g = q // 2
                            dve.wait_ge(act_step.sem, act_step.at(i + 1))
                            o = (t * SSD_GROUPS + g) * P
                            dve.tensor_tensor(decays[:, i % 2, :, :], decays[:, i % 2, :, :],
                                              cbt[:, o:o + P].unsqueeze(1).broadcast_to([P, 8, P]), ALU.mult).then_inc(aux.sem, 1)
                            c4 = carry[:, i % 2, :].rearrange("p (m l) -> p m l", m=4)
                            dve.wait_ge(aux.sem, aux.at(i + 1))
                            dve.tensor_tensor(c4, c4, xbc[:, 10 + g, t * P:(t + 1) * P].unsqueeze(1).broadcast_to([P, 4, P]),
                                              ALU.mult).then_inc(dve_step.sem, 1)
                        if i >= 1:
                            j = i - 1
                            t, q = units[j]
                            dve.wait_ge(gate_done.sem, gate_done.at(j + 1))
                            for m in range(2):
                                c = 2 * q + m
                                ins = dve.scalar_tensor_tensor(out=mixed[:, c, t * P:(t + 1) * P], in0=xbc[:, c, t * P:(t + 1) * P],
                                                               scalar=d_skip[:, c:c + 1], in1=ps[:, 6 + j % 2, m * P:(m + 1) * P],
                                                               op0=ALU.mult, op1=ALU.add)
                            ins.then_inc(dve_free.sem, 1)
            pe_step.passed(n)
            act_step.passed(n)
            dve_step.passed(n)
            gate_done.passed(n)
            dve_free.passed(n)
            aux.passed(n)

        MM = Arena(HN_AT)
        k_tok = ul32[:, 0:ST * D].rearrange("p (a b) -> p a b", a=ST)
        IG, LF, FC, BB, MX, NM, FL, SI = [MM.take(2, S) for _ in range(8)]
        kwr = MM.take(2, P)
        wts = MM.take(2, 2, S)
        floors = MM.take(2, 2 * S)
        dens = LF
        nums = IG
        kws = MM.take(2, 2, P)
        cst = MM.take(2, 2 * P)
        qst = MM.take(2, 2, P)
        ml = sb("ml", [P, 8])
        nst = sb("nst", [P, 2, 2])

        def mlstm_prepare():
            H8 = ML_HEADS
            with stage() as block:
                @block.tensor
                def _(pe):
                    for kind, at in ((0, 32), (1, 48)):
                        for d in range(2):
                            for t in range(ST):
                                tr = pe.transpose(ps[0:H8, kind, (d * ST + t) * P:(d * ST + t + 1) * P],
                                                  gate_x[:, t, at + d * H8:at + (d + 1) * H8], ident)
                        tr.then_inc(pe_step.sem, 1)
                    for t in range(ST):
                        for q in range(2):
                            for m in range(4):
                                tr = pe.transpose(ps[:, 2 + 2 * t + q, m * P:(m + 1) * P], mk[:, 4 * q + m, t * P:(t + 1) * P], ident)
                            tr.then_inc(pe_step.sem, 1)
                    pe.wait_ge(dve_step.sem, dve_step.at(1))
                    for d in range(2):
                        for t in range(ST):
                            o = (d * ST + t) * H8
                            pe.transpose(ps[:, 6, o:o + H8], BB[0:H8, d, t * P:(t + 1) * P], ident[0:H8, 0:H8])
                    pe.wait_ge(act_step.sem, act_step.at(7))
                    for d in range(2):
                        tr = pe.transpose(ps[:, 6, (4 + d) * H8:(5 + d) * H8], kwr[0:H8, d, :], ident[0:H8, 0:H8])
                    tr.then_inc(pe_step.sem, 1)

                @block.scalar
                def _(act):
                    act.preload_act_table_set(LN_EXP)
                    act.wait_ge(pe_step.sem, pe_step.at(1))
                    act.activation(IG[0:H8].rearrange("p a b -> p (a b)"), ps[0:H8, 0, :], ACT.Copy).then_inc(act_step.sem, 1)
                    for n in range(4):
                        act.wait_ge(pe_step.sem, pe_step.at(3 + n))
                        act.activation(k_tok[:, n // 2, (n % 2) * 512:(n % 2 + 1) * 512], ps[:, 2 + n, :], ACT.Copy).then_inc(act_step.sem, 1)
                    act.wait_ge(dve_step.sem, dve_step.at(2))
                    for d in range(2):
                        t = FIRST[d]
                        act.activation(kwr[0:H8, d, :], BB[0:H8, d, t * P:(t + 1) * P], ACT.Exp, bias=ml[0:H8, 2 + d:3 + d]).then_inc(act_step.sem, 1)
                    for d in range(2):
                        t = 1 - FIRST[d]
                        act.activation(SI[0:H8, d, t * P:(t + 1) * P], MX[0:H8, d, t * P:(t + 1) * P], ACT.Exp, scale=-1.0,
                                       bias=ml[0:H8, d:d + 1])
                    act.activation(FL[0:H8], FL[0:H8], ACT.Exp, scale=-1.0)

                @block.vector
                def _(dve):
                    link = lambda ins: dve_chain.link(dve, ins)
                    dve.wait_ge(pe_step.sem, pe_step.at(2))
                    link(dve.tensor_copy(LF[0:H8].rearrange("p a b -> p (a b)"), ps[0:H8, 1, :]))

                    def part(v, d, t):
                        s = v[0:H8, d, t * P:(t + 1) * P]
                        return s if d == 0 else s[:, ::-1]
                    one = ones[0:H8, :]
                    for d in range(2):
                        for t in range(ST):
                            link(dve.tensor_tensor_scan(part(FC, d, t), one, part(LF, d, t), 0.0, ALU.mult, ALU.add))
                    dve.wait_ge(act_step.sem, act_step.at(1))
                    link(dve.tensor_tensor(BB[0:H8], IG[0:H8], FC[0:H8], ALU.subtract))
                    for d in range(2):
                        t = FIRST[d]
                        b = part(BB, d, t)
                        link(dve.tensor_tensor_scan(part(MX, d, t), b, b, 0.0, ALU.max, ALU.max))
                        end = t * P + (P - 1 if d == 0 else 0)
                        link(dve.tensor_tensor(ml[0:H8, d:d + 1], FC[0:H8, d, end:end + 1], MX[0:H8, d, end:end + 1], ALU.add))
                        link(dve.tensor_scalar(ml[0:H8, 2 + d:3 + d], MX[0:H8, d, end:end + 1], -1.0, None, ALU.mult))
                        b = part(BB, d, 1 - t)
                        link(dve.tensor_tensor_scan(part(MX, d, 1 - t), b, b, ml[0:H8, d:d + 1], ALU.max, ALU.max))
                    dve.tensor_scalar(NM[0:H8], MX[0:H8], -1.0, None, ALU.mult).then_inc(dve_step.sem, 1)
                    dve.tensor_tensor(FL[0:H8], FC[0:H8], MX[0:H8], ALU.add).then_inc(dve_step.sem, 1)
                    dve.wait_ge(pe_step.sem, pe_step.at(7))
                    dve.tensor_copy(bcol.rearrange("p a b -> p (a b)"), ps[:, 6, 0:6 * H8])
            pe_step.passed(7)
            act_step.passed(7)
            dve_step.passed(2)

        def mlstm():
            H8 = ML_HEADS
            output, dens_ready = gate_done, act_free
            with stage() as block:
                @block.tensor
                def _(pe):
                    for i in range(H8 + 1):
                        if i < H8:
                            hh = i
                            sel = ident[0:H8, hh:hh + 1].broadcast_to([H8, P])
                            b0, b1 = (0, 1) if hh % 2 == 0 else (6, 7)
                            for t in range(ST):
                                pe.matmul(ps[:, b0, t * P:(t + 1) * P], mk[:, hh, t * P:(t + 1) * P], mq[:, hh, t * P:(t + 1) * P], start=True, stop=True)
                            for d in range(2):
                                t = 1 - FIRST[d]
                                pe.matmul(ps[:, b0, (2 + d) * P:(3 + d) * P], sel, SI[0:H8, d, t * P:(t + 1) * P], start=True, stop=True)
                            for d in range(2):
                                pe.matmul(ps[:, b1, d * S:(d + 1) * S], sel, NM[0:H8, d, :], start=True, stop=False)
                                mm = pe.matmul(ps[:, b1, d * S:(d + 1) * S], ident, tri_mask[d].unsqueeze(1).broadcast_to([P, ST, P]), start=False, stop=True)
                            mm.then_inc(pe_step.sem, 1)
                            if hh >= 1:
                                pe.wait_ge(act_step.sem, act_step.at(3 * hh))
                            mm = pe.matmul(ps[:, 2, :], sel, FL[0:H8, :, :], start=True, stop=True)
                            mm.then_inc(pe_step.sem, 1)
                            pe.wait_ge(dve_step.sem, dve_step.at(2 * hh + 1))
                            for d in range(2):
                                pe.matmul(ps[:, 3, d * P:(d + 1) * P], kws[:, hh % 2, d, :], mv[:, FIRST[d], hh * P:(hh + 1) * P], start=True, stop=True)
                                mm = pe.matmul(ps[:, 3, S + d:S + d + 1], kws[:, hh % 2, d, :], ones[:, 0:1], start=True, stop=True)
                            mm.then_inc(pe_step.sem, 1)
                        if i >= 1:
                            hh = i - 1
                            pe.wait_ge(dve_step.sem, dve_step.at(2 * hh + 2))
                            pe.wait_ge(act_step.sem, act_step.at(3 * hh + 3))
                            if hh >= 1:
                                pe.wait_ge(dve_free.sem, dve_free.at(hh))
                            for d in range(2):
                                for t in range(ST):
                                    o = (d * ST + t) * P
                                    wt = wts[:, hh % 2, d, t * P:(t + 1) * P]
                                    second = t != FIRST[d]
                                    pe.matmul(ps[:, 4, o:o + P], mv[:, t, hh * P:(hh + 1) * P], wt, start=True, stop=not second)
                                    if second:
                                        pe.matmul(ps[:, 4, o:o + P], cst[:, hh % 2, d * P:(d + 1) * P], qst[:, hh % 2, d, :], start=False, stop=True)
                                    mm = pe.matmul(ps[:, 5, o:o + P], ones, wt, start=True, stop=not second)
                                    if second:
                                        mm = pe.matmul(ps[:, 5, o:o + P], nst[:, hh % 2, d:d + 1].broadcast_to([P, P]), qst[:, hh % 2, d, :],
                                                       start=False, stop=True)
                            mm.then_inc(output.sem, 1)

                @block.scalar
                def _(act):
                    for i in range(H8 + 1):
                        if i < H8:
                            hh = i
                            b1 = 1 if hh % 2 == 0 else 7
                            act.wait_ge(pe_step.sem, pe_step.at(3 * hh + 1))
                            if hh >= 2:
                                act.wait_ge(output.sem, output.at(hh - 1))
                            for d in range(2):
                                for t in range(ST):
                                    ins = act.activation(wts[:, hh % 2, d, t * P:(t + 1) * P], ps[:, b1, (d * ST + t) * P:(d * ST + t + 1) * P],
                                                         ACT.Exp, bias=bcol[:, d * ST + t, hh:hh + 1])
                            ins.then_inc(act_step.sem, 1)
                            act.wait_ge(pe_step.sem, pe_step.at(3 * hh + 2))
                            if hh >= 2:
                                act.wait_ge(dve_free.sem, dve_free.at(hh - 1))
                            act.activation(floors[:, hh % 2, :], ps[:, 2, :], ACT.Copy).then_inc(act_step.sem, 1)
                            act.wait_ge(pe_step.sem, pe_step.at(3 * hh + 3))
                            act.activation(cst[:, hh % 2, :], ps[:, 3, 0:S], ACT.Copy)
                            act.activation(nst[:, hh % 2, :], ps[:, 3, S:S + 2], ACT.Copy).then_inc(act_step.sem, 1)
                        if i >= 1:
                            act.wait_ge(output.sem, output.at(i))
                            act.activation(dens.rearrange("p a b -> p (a b)"), ps[:, 5, :], ACT.Abs).then_inc(dens_ready.sem, 1)

                @block.vector
                def _(dve):
                    link = lambda ins: dve_chain.link(dve, ins)
                    flat = lambda v: v.rearrange("p a b -> p (a b)")

                    def scaled_keys(hh):
                        if hh >= 2:
                            dve.wait_ge(pe_step.sem, pe_step.at(3 * hh - 3))
                        for d in range(2):
                            ins = dve.tensor_scalar(kws[:, hh % 2, d, :], k_tok[:, FIRST[d], hh * P:(hh + 1) * P], bcol[:, 4 + d, hh:hh + 1], None, ALU.mult)
                        ins.then_inc(dve_step.sem, 1)

                    scaled_keys(0)
                    for i in range(H8 + 1):
                        if i < H8:
                            hh = i
                            b0 = 0 if hh % 2 == 0 else 6
                            dve.wait_ge(act_step.sem, act_step.at(3 * hh + 1))
                            dve.tensor_tensor(wts[:, hh % 2, :, :], wts[:, hh % 2, :, :],
                                              ps[:, b0, 0:S].unsqueeze(1).broadcast_to([P, 2, S]), ALU.mult)
                            for d in range(2):
                                t = 1 - FIRST[d]
                                ins = dve.tensor_tensor(qst[:, hh % 2, d, :], mq[:, hh, t * P:(t + 1) * P], ps[:, b0, (2 + d) * P:(3 + d) * P], ALU.mult)
                            ins.then_inc(dve_step.sem, 1)
                            if hh + 1 < H8:
                                scaled_keys(hh + 1)
                        if i >= 1:
                            hh = i - 1
                            dve.wait_ge(output.sem, output.at(hh + 1))
                            dve.wait_ge(dens_ready.sem, dens_ready.at(hh + 1))
                            link(dve.tensor_tensor(flat(dens), flat(dens), floors[:, hh % 2, :], ALU.max))
                            link(dve.reciprocal(flat(dens), flat(dens)))
                            link(dve.tensor_tensor(flat(nums), ps[:, 4, :], flat(dens), ALU.mult))
                            dve.tensor_tensor(mixed[:, KD + hh, :], nums[:, 0, :], nums[:, 1, :], ALU.add).then_inc(dve_free.sem, 1)
                            dve.wait_ge(dve_free.sem, dve_free.at(hh + 1))
            pe_step.passed(3 * H8)
            act_step.passed(3 * H8)
            dve_step.passed(2 * H8)
            output.passed(H8)
            dens_ready.passed(H8)
            dve_free.passed(H8)

        GM = Arena()
        gq = GM.take(GLA_HEADS, S)
        gk = GM.take(GLA_HEADS, S)
        gv = GM.take(ST, D)
        gr = h[:, :, S:T2]
        low = GM.take(ST, 32)
        low_t = GM.take(2, S)
        w2 = GM.take(2, 512)
        GLA_SQ = GM.at
        la = GM.take(2, GLA_HEADS, S)
        eb = GM.take(2, GLA_HEADS, S)
        qin = GM.take(2, GLA_HEADS, S)
        kout = GM.take(2, GLA_HEADS, S)
        kend_t = ul32[:, 0:2 * GLA_HEADS * ST * P].rearrange("p (a b) -> p a b", b=P)
        gst_two = [GM.take(2, 3, 2 * P) for _ in range(2)]
        restart = GM.take(2, S)
        N_CH = S // GLA_CHUNK
        dec = GM.take(2, GLA_HEADS, N_CH)

        def c_project(norm):
            items = []
            for m in range(4):
                items.append(chunk_item(0, m, 0, S, gq[:, m, :], scale=P ** -0.5))
            for m in range(4):
                items.append(chunk_item(1, m, 0, S, gk[:, m, :]))
            for q in range(4):
                items.append(token_item(2 + q // 2, (q % 2) * 256, 256, range(ST), gv[:, :, q * 256:(q + 1) * 256]))
            for m in range(8):
                items.append(chunk_item(4 + m // 4, m % 4, 0, S, gr[:, m, :]))
            items.append(token_item(6, 0, 32, range(ST), low))
            listed("c_in", C_SPANS, items, norm)

        def gla_prepare():
            with stage() as block:
                @block.sync
                def _(sp):
                    sp.dma_start(w2[0:GLA_RANK], a["c_gate_w2_2"][0].rearrange("i r c -> r i c")).then_inc(loaded.sem, 16)

                @block.gpsimd
                def _(pool):
                    pool_chain.link(pool, pool.memset(restart, 1.0))
                    pool.memset(restart[:, 0, 0::GLA_CHUNK], 0.0).then_inc(pool_step.sem, 1)
                    pool.memset(restart[:, 1, GLA_CHUNK - 1::GLA_CHUNK], 0.0).then_inc(pool_step.sem, 1)
                    pool.wait_ge(pool_step.sem, pool_step.at(2))

                @block.tensor
                def _(pe):
                    for d in range(2):
                        for t in range(ST):
                            tr = pe.transpose(ps[0:GLA_RANK, 0, (d * ST + t) * P:(d * ST + t + 1) * P],
                                              low[:, t, d * GLA_RANK:(d + 1) * GLA_RANK], ident)
                    tr.then_inc(pe_step.sem, 1)
                    pe.wait_ge(loaded.sem, loaded.at(16))
                    pe.wait_ge(act_step.sem, act_step.at(1))
                    for d in range(2):
                        for hh in range(GLA_HEADS):
                            mm = pe.matmul(ps[:, 1 + 2 * d + hh // 2, (hh % 2) * S:(hh % 2 + 1) * S],
                                           w2[0:GLA_RANK, d, hh * P:(hh + 1) * P], low_t[0:GLA_RANK, d, :], start=True, stop=True)
                            if hh % 2:
                                mm.then_inc(pe_step.sem, 1)
                    for n in range(4):
                        pe.wait_ge(dve_step.sem, dve_step.at(5 + n))
                        for m in range(4):
                            b = 4 * n + m
                            d, hh, t = b // 8, (b // 2) % 4, b % 2
                            tr = pe.transpose(ps[:, 4 + n if n < 4 else 0, m * P:(m + 1) * P], eb[:, d, hh, t * P:(t + 1) * P], ident)
                        tr.then_inc(pe_step.sem, 1)

                @block.scalar
                def _(act):
                    act.preload_act_table_set(LN_EXP)
                    link = lambda ins: act_chain.link(act, ins)
                    act.wait_ge(pe_step.sem, pe_step.at(1))
                    act.activation(low_t[0:GLA_RANK].rearrange("p a b -> p (a b)"), ps[0:GLA_RANK, 0, :], ACT.Copy).then_inc(act_step.sem, 1)
                    for d in range(2):
                        act.wait_ge(dve_step.sem, dve_step.at(1 + d))
                        link(act.activation(eb[:, d], la[:, d], ACT.Abs))
                        link(act.activation(eb[:, d], eb[:, d], ACT.Exp, scale=-1.0))
                        act.activation(eb[:, d], eb[:, d], ACT.Ln, bias=ones[:, 0:1]).then_inc(act_step.sem, 1)
                    for d in range(2):
                        act.wait_ge(dve_step.sem, dve_step.at(3 + d))
                        end = la[:, d, :, (GLA_CHUNK - 1 if d == 0 else 0)::GLA_CHUNK]
                        act.activation(dec[:, d, :, :], end, ACT.Exp, scale=1.0 / GLA_TAU)
                        act.activation(kout[:, d], la[:, d], ACT.Exp, scale=-1.0 / GLA_TAU)
                        act.activation(qin[:, d], la[:, d], ACT.Exp, scale=1.0 / GLA_TAU).then_inc(act_step.sem, 1)
                    for n in range(4):
                        act.wait_ge(pe_step.sem, pe_step.at(6 + n))
                        act.activation(kend_t[:, 4 * n:4 * n + 4, :].rearrange("p a b -> p (a b)"), ps[:, 4 + n, :], ACT.Copy)

                @block.vector
                def _(dve):
                    link = lambda ins: dve_chain.link(dve, ins)
                    for d in range(2):
                        for hh in range(GLA_HEADS):
                            dve.wait_ge(pe_step.sem, pe_step.at(2 + 2 * d + hh // 2))
                            ins = dve.tensor_scalar(la[:, d, hh, :], ps[:, 1 + 2 * d + hh // 2, (hh % 2) * S:(hh % 2 + 1) * S],
                                                    col("gate_b", d * GLA_HEADS + hh), None, ALU.add)
                        ins.then_inc(dve_step.sem, 1)
                    dve.wait_ge(pool_step.sem, pool_step.at(2))
                    for d in range(2):
                        dve.wait_ge(act_step.sem, act_step.at(2 + d))
                        dve.wait_ge(dve_step.sem, dve_step.at(1 + d))
                        link(dve.scalar_tensor_tensor(out=la[:, d], in0=la[:, d], scalar=0.0, in1=eb[:, d], op0=ALU.min, op1=ALU.subtract))
                        for hh in range(GLA_HEADS):
                            x_, r_ = la[:, d, hh, :], restart[:, d, :]
                            if d == 1:
                                x_, r_ = x_[:, ::-1], r_[:, ::-1]
                            ins = dve.tensor_tensor_scan(x_, r_, x_, 0.0, ALU.mult, ALU.add)
                        ins.then_inc(dve_step.sem, 1)
                    for d in range(2):
                        dve.wait_ge(act_step.sem, act_step.at(4 + d))
                        link(dve.tensor_tensor(kout[:, d], kout[:, d], gk, ALU.mult))
                        for half in range(2):
                            v = kout[:, d, 2 * half:2 * half + 2, :].rearrange("p h (c l) -> p (h c) l", c=N_CH)
                            to = eb[:, d, 2 * half:2 * half + 2, :].rearrange("p h (c l) -> p (h c) l", c=N_CH)
                            by = dec[:, d, 2 * half:2 * half + 2, :].rearrange("p h c -> p (h c)")
                            dve.tensor_tensor(to, v, by.unsqueeze(2).broadcast_to([P, 2 * N_CH, GLA_CHUNK]), ALU.mult).then_inc(dve_step.sem, 1)
                    for d in range(2):
                        dve.tensor_tensor(qin[:, d], qin[:, d], gq, ALU.mult)
            loaded.passed(16)
            pool_step.passed(2)
            pe_step.passed(9)
            act_step.passed(5)
            dve_step.passed(8)

        def gla():
            output = gate_done
            att = eb
            masks = (mat("gla_upto"), mat("gla_from"))
            C = GLA_CHUNK

            def chunk_sum(d, c):
                return ps[:, 1 + 2 * d + c % 2, (c // 2) * 2 * P:(c // 2 + 1) * 2 * P]

            with stage() as block:
                @block.tensor
                def _(pe):
                    def scores(hh):
                        for d in range(2):
                            for t in range(ST):
                                o = (d * ST + t) * P
                                mm = pe.matmul(ps[:, 0, o:o + P], kout[:, d, hh, t * P:(t + 1) * P], qin[:, d, hh, t * P:(t + 1) * P], start=True, stop=True)
                        mm.then_inc(pe_step.sem, 1)
                        for d in range(2):
                            for n in range(N_CH - 1):
                                c = n if d == 0 else N_CH - 1 - n
                                p0 = C * (c % 2)
                                mm = pe.matmul(chunk_sum(d, c),
                                               kend_t[p0:p0 + C, (d * GLA_HEADS + hh) * ST + c // 2, :],
                                               gv[p0:p0 + C, c // 2, hh * 2 * P:(hh + 1) * 2 * P], start=True, stop=True)
                        mm.then_inc(pe_step.sem, 1)

                    def outputs(hh):
                        gst = gst_two[hh % 2]
                        if hh >= 1:
                            pe.wait_ge(act_step.sem, act_step.at(hh))
                        for m in range(2):
                            for t in range(ST):
                                o = (m * ST + t) * P
                                run = []
                                for d in range(2):
                                    run.append((ps[:, 5, o:o + P], gv[:, t, hh * 2 * P + m * P:hh * 2 * P + (m + 1) * P],
                                                att[:, d, hh, t * P:(t + 1) * P]))
                                for d in range(2):
                                    for c in (2 * t, 2 * t + 1):
                                        n = c if d == 0 else N_CH - 1 - c
                                        if n:
                                            run.append((ps[:, 5, o + (c % 2) * C:o + (c % 2 + 1) * C], gst[:, d, n - 1, m * P:(m + 1) * P],
                                                        qin[:, d, hh, c * C:(c + 1) * C]))
                                for i, (to, stat, mov) in enumerate(run):
                                    mm = pe.matmul(to, stat, mov, start=(i == 0), stop=(i == len(run) - 1), skip_group_check=True)
                        mm.then_inc(output.sem, 1)

                    scores(0)
                    for hh in range(GLA_HEADS):
                        pe.wait_ge(dve_step.sem, dve_step.at(8 * hh + 8))
                        if hh + 1 < GLA_HEADS:
                            scores(hh + 1)
                        outputs(hh)

                @block.scalar
                def _(act):
                    for hh in range(GLA_HEADS):
                        act.wait_ge(output.sem, output.at(hh + 1))
                        act.activation(u32[:, 2 * hh:2 * hh + 2, :], ps[:, 5, :].rearrange("p (a b) -> p a b", a=2), ACT.Copy).then_inc(act_step.sem, 1)

                @block.vector
                def _(dve):
                    for hh in range(GLA_HEADS):
                        gst = gst_two[hh % 2]
                        dve.wait_ge(pe_step.sem, pe_step.at(2 * hh + 1))
                        for d in range(2):
                            v = ps[:, 0, d * S:(d + 1) * S].rearrange("p (t l) -> p t l", t=ST)
                            dve.tensor_tensor(att[:, d, hh, :].rearrange("p (t l) -> p t l", t=ST), v,
                                              masks[d].unsqueeze(1).broadcast_to([P, ST, P]), ALU.mult).then_inc(dve_step.sem, 1)
                        dve.wait_ge(pe_step.sem, pe_step.at(2 * hh + 2))
                        if hh >= 2:
                            dve.wait_ge(output.sem, output.at(hh - 1))
                        for n in range(N_CH - 1):
                            for d in range(2):
                                c = n if d == 0 else N_CH - 1 - n
                                new = chunk_sum(d, c)
                                if n == 0:
                                    dve.tensor_copy(gst[:, d, 0, :], new).then_inc(dve_step.sem, 1)
                                else:
                                    dve.wait_ge(dve_step.sem, dve_step.at(8 * hh + 2 + 2 * (n - 1) + d + 1))
                                    dve.scalar_tensor_tensor(out=gst[:, d, n, :], in0=gst[:, d, n - 1, :], scalar=dec[:, d, hh, c:c + 1],
                                                             in1=new, op0=ALU.mult, op1=ALU.add).then_inc(dve_step.sem, 1)
            pe_step.passed(2 * GLA_HEADS)
            output.passed(GLA_HEADS)
            act_step.passed(GLA_HEADS)
            dve_step.passed(8 * GLA_HEADS)

        program = [setup, modulation]
        tiles = [(l, t) for l in range(DEPTH) for t in range(N_MOD * D // ADA_COLS)][ADA_FIRST:]
        adas = {(0, 0): Ada(tiles[:KF]), (0, 1): Ada(tiles[KF:])}
        for l in range(DEPTH):
            T = S if l == DEPTH - 1 else T2
            before = residual1(l - 1, 6, 5, 0.5) if l else None
            program += [lambda l=l, r=before: ffn1(l, 0, norm1(l, 0, 0, post=r), l, adas.get((l, 0))),
                        lambda l=l: project(l, norm1(l, 3, 2, post=residual1(l, 0, 1, 0.5))), rel_bias,
                        lambda l=l: qk_norm(l), lambda l=l: attention(l),
                        lambda l=l, T=T: wide(Wide(("o", l), uh, ul, KD, T)),
                        lambda l=l, T=T: ffn1(l, 1, norm1(l, 6, 4, T, residual1(l, 3, 3, 1.0, T)),
                                               ada=adas.get((l, 1)))]
        program += [lambda: ab_project(norm2(0, 0, residual1(DEPTH - 1, 6, 5, 0.5, S))),
                    ssd_gates, ssd_prepare, ssd_scan, mlstm_prepare, mlstm,
                    lambda: head_norm("ab_out", HN_AT, (0, KD, 4, "ssd_norm", (ACT.Silu, z), None),
                                      (KD, KD, 1, "mlstm_norm", (ACT.Sigmoid, o_pre), None)),
                    lambda: ffn2(0, norm2(0, 2, residual2(0, 1))),
                    lambda: c_project(norm2(1, 0, residual2(0, 3))), gla_prepare, gla,
                    lambda: head_norm("c_out", GLA_SQ, (0, KD, 2, "gla_norm", None, (ACT.Silu, gr))),
                    lambda: ffn2(1, norm2(1, 2, residual2(1, 1))),
                    lambda: residual(residual2(1, 3))]
        for step in program[:stop]:
            step()
        finish()


_INS = ['x', 'c', 'ctx', 'c_ctx', 'w_ada', 'b_ada', 'norm_g', 'w_in', 'qk_g', 'rpb', 'conv_w', 'w_o', 'ffn_wi', 'ffn_wo',
        'norm_g_2', 'ab_w_in_2', 'ab_conv_w_2', 'ab_conv_b_2', 'ab_dt_bias_2', 'ab_a_log_2', 'ab_d_skip_2',
        'ab_ssd_norm_2', 'ab_ig_bias_2', 'ab_fg_bias_2', 'ab_mlstm_norm_2', 'ab_w_out_2', 'c_w_in_2',
        'c_gate_w2_2', 'c_gate_b_2', 'c_norm_2', 'c_w_out_2', 'ffn_w_up_2', 'ffn_conv_w_2', 'ffn_conv_b_2',
        'ffn_w_down_2']


def kernel(**inputs):
    import numpy as _np
    import concourse.bacc as _bacc
    from concourse import mybir as _mybir
    from concourse.bass_utils import run_bass_kernel_spmd as _run

    nc = _bacc.Bacc("TRN2", target_bir_lowering=False, num_devices=1)
    arrays, aps = {}, {}
    for name in _INS + ["const"]:
        arr = constants() if name == "const" else _np.ascontiguousarray(inputs[name])
        arrays[f"in_{name}_dram"] = arr
        aps[name] = nc.dram_tensor(f"in_{name}_dram", arr.shape, _mybir.dt.from_np(arr.dtype), kind="ExternalInput").ap()
    n = (B_HEADS * RPB_H * RPB_PAD // P + 1) * P
    aps["padded"] = nc.dram_tensor("rpb_padded", (n,), F32, kind="Internal").ap().rearrange("(p n) -> p n", p=P)
    out = nc.dram_tensor("out_0_dram", (1, S, D), F32, kind="ExternalOutput").ap()
    two_blocks(nc, aps, out)
    r = _run(nc, [arrays], core_ids=[0])
    return r.results[0]["out_0_dram"]
```
